# Optimizing a Trainium2 kernel written in Bass

```python
import math
import jax, jax.numpy as jnp
from jax import lax
import numpy as np

D_MODEL = 1024
BATCH = 1
SEQ = 256
DEPTH = 2

MIX_WIDTH = D_MODEL
M_HEADS = 4
M_HEAD_DIM = (MIX_WIDTH // 2) // M_HEADS
M_WIDTH = M_HEADS * M_HEAD_DIM
A_HEADS = 8
A_HEAD_DIM = (MIX_WIDTH - M_WIDTH) // A_HEADS
A_WIDTH = A_HEADS * A_HEAD_DIM
D_FF = 4 * D_MODEL
CONV_WIDTH = 5
M_CHUNK = 64
DILATED_PATTERNS = ((128, 1), (512, 4), (2048, 16))
BAND_BLOCK = 64
ROPE_THETA = 10000.0
NORM_EPS = 1e-6
NEG_INF = -1e30
IN_SPLITS = (M_WIDTH, M_WIDTH, M_WIDTH, M_WIDTH, 2 * M_HEADS, 2 * M_HEADS, A_WIDTH, A_WIDTH, A_WIDTH)
IN_WIDTH = 4 * M_WIDTH + 4 * M_HEADS + 3 * A_WIDTH


def rms_norm(x, g):
    xf = x.astype(jnp.float32)
    y = xf * lax.rsqrt(jnp.mean(xf * xf, axis=-1, keepdims=True) + NORM_EPS)
    return (y * g.astype(jnp.float32)).astype(x.dtype)

def rope(t):
    S, D = t.shape[1], t.shape[-1]
    half = D // 2
    inv_freq = ROPE_THETA ** (-jnp.arange(half, dtype=jnp.float32) / half)
    ang = jnp.arange(S, dtype=jnp.float32)[:, None] * inv_freq[None, :]
    cos = jnp.cos(ang)[None, :, None, :]
    sin = jnp.sin(ang)[None, :, None, :]
    tf = t.astype(jnp.float32)
    t1, t2 = tf[..., :half], tf[..., half:]
    return jnp.concatenate([t1 * cos - t2 * sin, t1 * sin + t2 * cos], axis=-1)

def centred_depthwise_conv(x, w):
    K, C = w.shape
    return lax.conv_general_dilated(
        x, w[:, None, :], window_strides=(1,), padding=[(K // 2, K // 2)],
        dimension_numbers=("NWC", "WIO", "NWC"), feature_group_count=C)

def mlstm_chunkwise(q, k, v, li, lf):
    B, H, S, D = q.shape
    L = M_CHUNK
    NC = S // L
    q = q.reshape(B, H, NC, L, D)
    k = k.reshape(B, H, NC, L, D)
    v = v.reshape(B, H, NC, L, D)
    li = li.reshape(B, H, NC, L)
    lf = lf.reshape(B, H, NC, L)
    b = jnp.cumsum(lf, axis=-1)
    b_last = b[..., -1]
    g = b_last[..., None] - b + li
    g_max = jnp.max(g, axis=-1)

    def step(carry, inp):
        C, n, m = carry
        k_c, v_c, g_c, gmax_c, bl_c = inp
        m_new = jnp.maximum(bl_c + m, gmax_c)
        decay = jnp.exp(bl_c + m - m_new)
        w = jnp.exp(g_c - m_new[..., None])
        C_new = decay[..., None, None] * C + jnp.einsum("bhs,bhsk,bhsv->bhkv", w, k_c, v_c)
        n_new = decay[..., None] * n + jnp.einsum("bhs,bhsk->bhk", w, k_c)
        return (C_new, n_new, m_new), (C, n, m)

    init = (jnp.zeros((B, H, D, D), jnp.float32), jnp.zeros((B, H, D), jnp.float32),
            jnp.full((B, H), NEG_INF, jnp.float32))
    xs = (jnp.moveaxis(k, 2, 0), jnp.moveaxis(v, 2, 0), jnp.moveaxis(g, 2, 0),
          jnp.moveaxis(g_max, 2, 0), jnp.moveaxis(b_last, 2, 0))
    _, (C_prev, n_prev, m_prev) = lax.scan(step, init, xs)
    C_prev = jnp.moveaxis(C_prev, 0, 2)
    n_prev = jnp.moveaxis(n_prev, 0, 2)
    m_prev = jnp.moveaxis(m_prev, 0, 2)

    a = b + m_prev[..., None]
    lower = jnp.tril(jnp.ones((L, L), dtype=bool))
    dmat = jnp.where(lower, b[..., :, None] - b[..., None, :] + li[..., None, :], NEG_INF)
    m_t = jnp.maximum(a, jnp.max(dmat, axis=-1))
    s = jnp.einsum("bhnqd,bhnkd->bhnqk", q, k) * jnp.exp(dmat - m_t[..., None])
    inter = jnp.exp(a - m_t)
    num = (jnp.einsum("bhnqk,bhnkd->bhnqd", s, v)
           + inter[..., None] * jnp.einsum("bhnqk,bhnkv->bhnqv", q, C_prev))
    den = jnp.sum(s, axis=-1) + inter * jnp.einsum("bhnqk,bhnk->bhnq", q, n_prev)
    h = num / jnp.maximum(jnp.abs(den), jnp.exp(-m_t))[..., None]
    return h.reshape(B, H, S, D)

def strided_band_attention(q, k, v, dilation, half):
    B, H, S, D = q.shape
    L = S // dilation
    qb_len = math.gcd(L, BAND_BLOCK)
    nb = L // qb_len
    span = qb_len + 2 * half

    def to_strided(t):
        return t.reshape(B, H, L, dilation, D).transpose(0, 1, 3, 2, 4)

    qs = to_strided(q).reshape(B, H, dilation, nb, qb_len, D)
    pad = ((0, 0), (0, 0), (0, 0), (half, half), (0, 0))
    kp = jnp.pad(to_strided(k), pad)
    vp = jnp.pad(to_strided(v), pad)
    idx = (jnp.arange(nb) * qb_len)[:, None] + jnp.arange(span)[None, :]
    kb = kp[:, :, :, idx, :]
    vb = vp[:, :, :, idx, :]
    qpos = (jnp.arange(nb) * qb_len)[:, None, None] + jnp.arange(qb_len)[None, :, None]
    kpos = idx[:, None, :] - half
    valid = (jnp.abs(kpos - qpos) <= half) & (kpos >= 0) & (kpos < L)
    s = jnp.einsum("bhrnqd,bhrnkd->bhrnqk", qs, kb) * (1.0 / math.sqrt(D))
    s = jnp.where(valid, s, NEG_INF)
    m = jnp.max(s, axis=-1)
    p = jnp.exp(s - m[..., None])
    l = jnp.sum(p, axis=-1)
    o = jnp.einsum("bhrnqk,bhrnkd->bhrnqd", p, vb) / l[..., None]

    def from_strided(t):
        tail = t.shape[5:]
        t = jnp.moveaxis(t.reshape((B, H, dilation, L) + tail), 2, 3)
        return t.reshape((B, H, S) + tail)

    return from_strided(o), from_strided(m), from_strided(l)

def dilated_attention(q, k, v):
    outs = [strided_band_attention(q, k, v, d, w // (2 * d)) for (w, d) in DILATED_PATTERNS]
    m_all = jnp.max(jnp.stack([m for (_, m, _) in outs]), axis=0)
    weights = [l * jnp.exp(m - m_all) for (_, m, l) in outs]
    num = sum(w[..., None] * o for w, (o, _, _) in zip(weights, outs))
    return num / sum(weights)[..., None]

def hybrid_layer(x, norm1_g, w_in, conv_w, gate_i_b, gate_f_b, head_norm_g, w_out,
                 norm2_g, w_up, w_down):
    B, S, _ = x.shape
    h = rms_norm(x, norm1_g)
    proj = h @ w_in
    mq, mk, mv, mo, mi, mf, aq, ak, av = jnp.split(
        proj, list(np.cumsum(IN_SPLITS)[:-1]), axis=-1)

    qk = jax.nn.silu(centred_depthwise_conv(jnp.concatenate([mq, mk], axis=-1), conv_w))
    mq, mk = qk[..., :M_WIDTH], qk[..., M_WIDTH:]

    def m_heads(t):
        return t.reshape(B, S, M_HEADS, M_HEAD_DIM).transpose(0, 2, 1, 3).astype(jnp.float32)

    q_m = m_heads(mq)
    k_m = m_heads(mk) * (1.0 / math.sqrt(M_HEAD_DIM))
    v_m = m_heads(mv)
    gi = (mi + gate_i_b).astype(jnp.float32).reshape(B, S, 2, M_HEADS).transpose(2, 0, 3, 1)
    gf = jax.nn.log_sigmoid((mf + gate_f_b).astype(jnp.float32)).reshape(
        B, S, 2, M_HEADS).transpose(2, 0, 3, 1)
    h_fwd = mlstm_chunkwise(q_m, k_m, v_m, gi[0], gf[0])
    flip = lambda t: jnp.flip(t, axis=2)
    h_bwd = flip(mlstm_chunkwise(flip(q_m), flip(k_m), flip(v_m), flip(gi[1]), flip(gf[1])))
    hm = h_fwd + h_bwd
    hm = hm * lax.rsqrt(jnp.mean(hm * hm, axis=-1, keepdims=True) + NORM_EPS)
    hm = hm.transpose(0, 2, 1, 3).reshape(B, S, M_WIDTH) * head_norm_g.astype(jnp.float32)
    y_m = (hm * jax.nn.sigmoid(mo.astype(jnp.float32))).astype(x.dtype)

    def a_heads(t, rotate):
        t = t.reshape(B, S, A_HEADS, A_HEAD_DIM)
        t = rope(t) if rotate else t.astype(jnp.float32)
        return t.transpose(0, 2, 1, 3)

    o_a = dilated_attention(a_heads(aq, True), a_heads(ak, True), a_heads(av, False))
    y_a = o_a.transpose(0, 2, 1, 3).reshape(B, S, A_WIDTH).astype(x.dtype)

    x = x + jnp.concatenate([y_m, y_a], axis=-1) @ w_out

    u = jax.nn.relu(rms_norm(x, norm2_g) @ w_up)
    return x + (u * u) @ w_down

def first_inputs(seed: int = 0) -> dict:
    key = jax.random.key(seed)
    ks = jax.random.split(key, 13)
    f32 = jnp.float32
    nrm = lambda k, shape: jax.random.normal(k, shape, f32)
    x = nrm(ks[0], (BATCH, SEQ, D_MODEL))
    norm1_g = 1.0 + 0.02 * nrm(ks[1], (DEPTH, D_MODEL))
    w_in = nrm(ks[2], (DEPTH, D_MODEL, IN_WIDTH)) * D_MODEL ** -0.5
    conv_w = nrm(ks[3], (DEPTH, CONV_WIDTH, 2 * M_WIDTH)) * CONV_WIDTH ** -0.5
    gate_i_b = 0.1 * nrm(ks[4], (DEPTH, 2 * M_HEADS))
    gate_f_b = (jnp.tile(jnp.linspace(3.0, 6.0, M_HEADS, dtype=f32), 2)[None, :]
                + 0.1 * nrm(ks[5], (DEPTH, 2 * M_HEADS)))
    head_norm_g = 1.0 + 0.02 * nrm(ks[6], (DEPTH, M_WIDTH))
    w_out = nrm(ks[7], (DEPTH, MIX_WIDTH, D_MODEL)) * MIX_WIDTH ** -0.5
    norm2_g = 1.0 + 0.02 * nrm(ks[8], (DEPTH, D_MODEL))
    w_up = nrm(ks[9], (DEPTH, D_MODEL, D_FF)) * D_MODEL ** -0.5
    w_down = nrm(ks[10], (DEPTH, D_FF, D_MODEL)) * D_FF ** -0.5
    final_g = 1.0 + 0.02 * nrm(ks[11], (D_MODEL,))
    return {"x": x, "norm1_g": norm1_g, "w_in": w_in, "conv_w": conv_w,
            "gate_i_b": gate_i_b, "gate_f_b": gate_f_b, "head_norm_g": head_norm_g,
            "w_out": w_out, "norm2_g": norm2_g, "w_up": w_up, "w_down": w_down,
            "final_g": final_g}

def first_block(x, norm1_g, w_in, conv_w, gate_i_b, gate_f_b, head_norm_g, w_out,
              norm2_g, w_up, w_down, final_g):
    for layer in range(DEPTH):
        x = hybrid_layer(x, norm1_g[layer], w_in[layer], conv_w[layer], gate_i_b[layer],
                         gate_f_b[layer], head_norm_g[layer], w_out[layer], norm2_g[layer],
                         w_up[layer], w_down[layer])
    return rms_norm(x, final_g)


MIX_WIDTH_2 = D_MODEL
GM_HEADS = 4
GM_WIDTH = MIX_WIDTH_2 // 2
GM_HEAD_DIM = GM_WIDTH // GM_HEADS
GM_CHUNK = 128
GLA_HEADS = 4
GLA_WIDTH = MIX_WIDTH_2 - GM_WIDTH
GLA_DV = GLA_WIDTH // GLA_HEADS
GLA_KEY_WIDTH = GLA_WIDTH // 2
GLA_DK = GLA_KEY_WIDTH // GLA_HEADS
GLA_GATE_RANK = 16
GLA_TAU = 16.0
GLA_CHUNK = 64
IN_COLS = 2 * GM_WIDTH + 2 * GLA_KEY_WIDTH + 2 * GLA_WIDTH + GLA_GATE_RANK
D_FF_2 = 2816
N_EXPERTS = 8
TOP_K = 2
D_FF_EXPERT = 3584
N_DENSE = (DEPTH + 1) // 2
N_MOE = DEPTH // 2
LN_EPS = 1e-5
RMS_EPS = 1e-6
DEEPNORM_ALPHA = (2 * DEPTH) ** 0.25
DEEPNORM_BETA = (8 * DEPTH) ** -0.25


def layer_norm(x, g, b):
    xf = x.astype(jnp.float32)
    mu = jnp.mean(xf, axis=-1, keepdims=True)
    var = jnp.mean(jnp.square(xf - mu), axis=-1, keepdims=True)
    y = (xf - mu) * lax.rsqrt(var + LN_EPS) * g.astype(jnp.float32) + b.astype(jnp.float32)
    return y.astype(x.dtype)

def chunked_spatial_gating(u, v, w_s, b_s, ln_g, ln_b):
    B, S, _ = u.shape
    n = S // GM_CHUNK
    v = layer_norm(v.reshape(B, S, GM_HEADS, GM_HEAD_DIM),
                   ln_g.reshape(GM_HEADS, GM_HEAD_DIM), ln_b.reshape(GM_HEADS, GM_HEAD_DIM))
    v = v.reshape(B, n, GM_CHUNK, GM_HEADS, GM_HEAD_DIM)
    causal = jnp.tril(jnp.ones((GM_CHUNK, GM_CHUNK), dtype=bool))
    w = jnp.where(causal[None], w_s, 0)
    s = jnp.einsum('hts,bnshc->bnthc', w, v) + b_s.T[None, None, :, :, None]
    return u * s.reshape(B, S, GM_WIDTH)

def gla_chunked(q, k, v, log_a):
    B, S, H, dk = q.shape
    dv = v.shape[-1]
    n = S // GLA_CHUNK

    def to_chunks(t):
        return t.astype(jnp.float32).reshape(B, n, GLA_CHUNK, H, t.shape[-1]).transpose(1, 0, 3, 2, 4)

    q, k, v, log_a = to_chunks(q), to_chunks(k), to_chunks(v), to_chunks(log_a)
    q = q * (dk ** -0.5)
    b = jnp.cumsum(log_a, axis=3)
    b_last = b[:, :, :, -1:, :]
    q_dec = q * jnp.exp(b)
    k_inv = k * jnp.exp(-b)
    k_dec = k * jnp.exp(b_last - b)
    causal = jnp.tril(jnp.ones((GLA_CHUNK, GLA_CHUNK), dtype=bool))
    scores = jnp.where(causal, jnp.einsum('nbhid,nbhjd->nbhij', q_dec, k_inv), 0.0)
    o_intra = jnp.einsum('nbhij,nbhje->nbhie', scores, v)

    def step(state, inp):
        q_c, k_c, v_c, decay_c = inp
        o = jnp.einsum('bhid,bhde->bhie', q_c, state)
        state = state * decay_c[..., 0, :, None] + jnp.einsum('bhjd,bhje->bhde', k_c, v_c)
        return state, o

    state0 = jnp.zeros((B, H, dk, dv), jnp.float32)
    _, o_inter = lax.scan(step, state0, (q_dec, k_dec, v, jnp.exp(b_last)))
    o = o_intra + o_inter
    return o.transpose(1, 0, 3, 2, 4).reshape(B, S, H, dv)

def hybrid_mixer(x, w_in, gm_ws, gm_bs, gm_ln_g, gm_ln_b, gla_wa2, gla_ba, gla_norm_g, w_out):
    B, S, _ = x.shape
    proj = x @ w_in
    o1 = GM_WIDTH
    o2 = o1 + GM_WIDTH
    o3 = o2 + GLA_KEY_WIDTH
    o4 = o3 + GLA_KEY_WIDTH
    o5 = o4 + GLA_WIDTH
    o6 = o5 + GLA_WIDTH
    gm_u, gm_v, q, k, v, g, a_lr = jnp.split(proj, [o1, o2, o3, o4, o5, o6], axis=-1)
    gm_u = jax.nn.gelu(gm_u, approximate=False)
    gm_v = jax.nn.gelu(gm_v, approximate=False)
    out_a = chunked_spatial_gating(gm_u, gm_v, gm_ws, gm_bs, gm_ln_g, gm_ln_b)
    log_a = jax.nn.log_sigmoid((a_lr @ gla_wa2 + gla_ba).astype(jnp.float32)) / GLA_TAU
    o = gla_chunked(q.reshape(B, S, GLA_HEADS, GLA_DK), k.reshape(B, S, GLA_HEADS, GLA_DK),
                    v.reshape(B, S, GLA_HEADS, GLA_DV), log_a.reshape(B, S, GLA_HEADS, GLA_DK))
    o = o * lax.rsqrt(jnp.mean(jnp.square(o), axis=-1, keepdims=True) + RMS_EPS)
    o = o * gla_norm_g.reshape(GLA_HEADS, GLA_DV).astype(jnp.float32)
    out_b = o.reshape(B, S, GLA_WIDTH).astype(x.dtype) * jax.nn.silu(g)
    return jnp.concatenate([out_a, out_b], axis=-1) @ w_out

def swiglu(x, w_gate, w_up, w_down):
    return (jax.nn.silu(x @ w_gate) * (x @ w_up)) @ w_down

def moe_swiglu(x, w_router, e_gate, e_up, e_down):
    B, S, D = x.shape
    t = x.reshape(B * S, D)
    logits = (t @ w_router).astype(jnp.float32)
    top_val, top_idx = lax.top_k(logits, TOP_K)
    top_w = jax.nn.softmax(top_val, axis=-1)
    gates = jnp.sum(jax.nn.one_hot(top_idx, N_EXPERTS, dtype=jnp.float32) * top_w[..., None], axis=1)
    gates = gates.astype(t.dtype)
    out = jnp.zeros_like(t)
    for e in range(N_EXPERTS):
        out = out + gates[:, e:e + 1] * swiglu(t, e_gate[e], e_up[e], e_down[e])
    return out.reshape(B, S, D)

def second_inputs(seed: int = 0) -> dict:
    key = jax.random.key(seed)
    ks = jax.random.split(key, 22)
    nrm = jax.random.normal
    f32 = jnp.float32
    D = D_MODEL
    return {
        'x': nrm(ks[0], (BATCH, SEQ, D), f32),
        'w_in': nrm(ks[1], (DEPTH, D, IN_COLS), f32) * D ** -0.5,
        'gm_ws': nrm(ks[2], (DEPTH, GM_HEADS, GM_CHUNK, GM_CHUNK), f32) * GM_CHUNK ** -0.5,
        'gm_bs': 1.0 + 0.1 * nrm(ks[3], (DEPTH, GM_HEADS, GM_CHUNK), f32),
        'gm_ln_g': 1.0 + 0.1 * nrm(ks[4], (DEPTH, GM_WIDTH), f32),
        'gm_ln_b': 0.02 * nrm(ks[5], (DEPTH, GM_WIDTH), f32),
        'gla_wa2': nrm(ks[6], (DEPTH, GLA_GATE_RANK, GLA_KEY_WIDTH), f32) * GLA_GATE_RANK ** -0.5,
        'gla_ba': 0.1 * nrm(ks[7], (DEPTH, GLA_KEY_WIDTH), f32),
        'gla_norm_g': 1.0 + 0.1 * nrm(ks[8], (DEPTH, GLA_WIDTH), f32),
        'w_out': nrm(ks[9], (DEPTH, MIX_WIDTH_2, D), f32) * MIX_WIDTH_2 ** -0.5 * DEEPNORM_BETA,
        'ln_mix_g': 1.0 + 0.1 * nrm(ks[10], (DEPTH, D), f32),
        'ln_mix_b': 0.02 * nrm(ks[11], (DEPTH, D), f32),
        'ffn_w_gate': nrm(ks[12], (N_DENSE, D, D_FF_2), f32) * D ** -0.5,
        'ffn_w_up': nrm(ks[13], (N_DENSE, D, D_FF_2), f32) * D ** -0.5,
        'ffn_w_down': nrm(ks[14], (N_DENSE, D_FF_2, D), f32) * D_FF_2 ** -0.5 * DEEPNORM_BETA,
        'router_w': nrm(ks[15], (N_MOE, D, N_EXPERTS), f32) * D ** -0.5,
        'exp_w_gate': nrm(ks[16], (N_MOE, N_EXPERTS, D, D_FF_EXPERT), f32) * D ** -0.5,
        'exp_w_up': nrm(ks[17], (N_MOE, N_EXPERTS, D, D_FF_EXPERT), f32) * D ** -0.5,
        'exp_w_down': nrm(ks[18], (N_MOE, N_EXPERTS, D_FF_EXPERT, D), f32) * D_FF_EXPERT ** -0.5 * DEEPNORM_BETA,
        'ln_ffn_g': 1.0 + 0.1 * nrm(ks[19], (DEPTH, D), f32),
        'ln_ffn_b': 0.02 * nrm(ks[20], (DEPTH, D), f32),
    }

def second_block(x, w_in, gm_ws, gm_bs, gm_ln_g, gm_ln_b, gla_wa2, gla_ba, gla_norm_g, w_out,
              ln_mix_g, ln_mix_b, ffn_w_gate, ffn_w_up, ffn_w_down, router_w,
              exp_w_gate, exp_w_up, exp_w_down, ln_ffn_g, ln_ffn_b):
    for layer in range(DEPTH):
        h = hybrid_mixer(x, w_in[layer], gm_ws[layer], gm_bs[layer], gm_ln_g[layer], gm_ln_b[layer],
                         gla_wa2[layer], gla_ba[layer], gla_norm_g[layer], w_out[layer])
        x = layer_norm(DEEPNORM_ALPHA * x + h, ln_mix_g[layer], ln_mix_b[layer])
        i = layer // 2
        if layer % 2 == 0:
            f = swiglu(x, ffn_w_gate[i], ffn_w_up[i], ffn_w_down[i])
        else:
            f = moe_swiglu(x, router_w[i], exp_w_gate[i], exp_w_up[i], exp_w_down[i])
        x = layer_norm(DEEPNORM_ALPHA * x + f, ln_ffn_g[layer], ln_ffn_b[layer])
    return x


def setup_inputs(seed=0):
    out = dict(first_inputs(seed))
    for name, value in second_inputs(seed + 1).items():
        if name != "x":
            out[name + "_2"] = value
    return out


def reference(
    x, norm1_g, w_in, conv_w, gate_i_b, gate_f_b, head_norm_g, w_out, norm2_g, w_up, w_down,
    final_g, w_in_2, gm_ws_2, gm_bs_2, gm_ln_g_2, gm_ln_b_2, gla_wa2_2, gla_ba_2, gla_norm_g_2,
    w_out_2, ln_mix_g_2, ln_mix_b_2, ffn_w_gate_2, ffn_w_up_2, ffn_w_down_2, router_w_2,
    exp_w_gate_2, exp_w_up_2, exp_w_down_2, ln_ffn_g_2, ln_ffn_b_2,
):
    x = first_block(
        x, norm1_g, w_in, conv_w, gate_i_b, gate_f_b, head_norm_g, w_out, norm2_g, w_up, w_down,
        final_g,
    )
    return second_block(
        x, w_in_2, gm_ws_2, gm_bs_2, gm_ln_g_2, gm_ln_b_2, gla_wa2_2, gla_ba_2, gla_norm_g_2,
        w_out_2, ln_mix_g_2, ln_mix_b_2, ffn_w_gate_2, ffn_w_up_2, ffn_w_down_2, router_w_2,
        exp_w_gate_2, exp_w_up_2, exp_w_down_2, ln_ffn_g_2, ln_ffn_b_2,
    )


_drawn_inputs = setup_inputs


def setup_inputs(seed=0):
    import zlib

    import numpy as np

    out = dict(_drawn_inputs(seed))
    spreads = {}
    factors = {'gate_i_b': 8.0,
     'head_norm_g': 3.349,
     'gm_ln_g_2': 2.943,
     'gm_ln_b_2': 8.0,
     'gla_ba_2': 3.503}
    for name, (base, spread) in spreads.items():
        noise = np.random.default_rng([zlib.crc32(name.encode()), seed]).standard_normal(out[name].shape)
        drawn = base * np.exp(spread * noise) if base else spread * noise
        out[name] = __import__('jax').numpy.asarray(drawn.astype(out[name].dtype))
    for name, factor in factors.items():
        out[name] = (out[name] * factor).astype(out[name].dtype)
    return out
```

```python
from contextlib import ExitStack

import numpy as np
import concourse.bass as bass
from concourse import mybir

F32 = mybir.dt.float32
F32R = mybir.dt.float32r
U32 = mybir.dt.uint32
I32 = mybir.dt.int32
ALU = mybir.AluOpType
ACT = mybir.ActivationFunctionType
AX = mybir.AxisListType

P = 128
S = 256
TT = S // P
D = 1024
KT = D // P
NW = 512
SLABS = 4
UNIT = SLABS * NW
DEPTH = 2
FF1 = 4096
FF2 = 2816
FFE = 3584
NE = 8
MH, MD = 4, 128
AH, AD = 8, 64
GH = 4
CW = 5
EPS = 1e-6
LN_EPS = 1e-5
ALPHA = (2 * DEPTH) ** 0.25
BIG = 1e30

RAW_SLOTS, SPLIT_SLOTS, PAIRS, TBANKS = 3, 3, 2, 2
REPEATS = (DEPTH, 1, NE, NE, 1)
EXPERT_UNITS = 14 + 14 + 14
LAYER1_UNITS = 14 + 4 + 16 + 16
UNITS = (LAYER1_UNITS, 10 + 4 + 22 + 11 + 10 + 4, EXPERT_UNITS, EXPERT_UNITS, 0)
CHUNKS = (7 + 2 + 8 + 2, 5 + 2 + 11 + 2 + 5 + 2, 7 + 1, 7 + 1, 0)
GROUPS = (4 + 4 + 4 + 4 + 4 + 16, 4 + 2 + 4 + 4 + 11 + 4 + 2 + 4 + 4 + 2, 1 + 7 + 2, 1 + 7 + 2, 0)

class Ring:

    def __init__(self, size, uses, offsets):
        self.size, self.uses, self.offsets = size, uses, offsets
        self.base, self.lag, self.slot_base = [], [], []
        last, n, per_slot = {}, 0, [0] * size
        for body, (count, repeats) in enumerate(zip(uses, REPEATS)):
            self.base.append(n)
            self.slot_base.append(list(per_slot))
            lags = [size] * count
            for _ in range(repeats):
                for k in range(count):
                    slot = self.slot(body, k)
                    if slot in last:
                        lags[k] = min(lags[k], n - last[slot])
                    last[slot] = n
                    per_slot[slot] += 1
                    n += 1
            self.lag.append(lags)

    def slot(self, body, k):
        return (self.offsets[body] + k) % self.size

    def done(self, body, step, k):
        return step * self.uses[body] + (self.base[body] + k + 1 + self.size)

    def free(self, body, step, k):
        return step * self.uses[body] + (self.base[body] + k + 1 + self.size - self.lag[body][k])

    def turns(self, body, step, k):
        slot = self.slot(body, k)
        same = [i for i in range(self.uses[body]) if self.slot(body, i) == slot]
        return step * len(same) + (self.slot_base[body][slot] + same.index(k) + 1)


class Signal:

    def __init__(self, sem, raises):
        self.sem, self.raises = sem, raises
        self.base, n = [], 0
        for k, repeats in zip(raises, REPEATS):
            self.base.append(n)
            n += k * repeats


class Place:

    def __init__(self, raised):
        self.raised = raised
        self.enter(0, 0)

    def enter(self, body, step):
        self.body, self.step = body, step
        self.unit = self.slab = self.chunk = self.group = 0
        self.waited = {}

    def up(self, signal, n=1):
        if not isinstance(self.step, int) or self.step == 0:
            key = (signal, self.body)
            self.raised[key] = self.raised.get(key, 0) + n
        return signal.sem, n

    def at(self, signal, k):
        return signal.sem, self.step * signal.raises[self.body] + (signal.base[self.body] + k)

    def next(self, signal, n=1):
        self.waited[signal] = self.waited.get(signal, 0) + n
        return self.at(signal, self.waited[signal])


CONST = {}
_at = 0
for _n, _w in (("ident", P), ("lnc", TT * S), ("dmask", 2 * P), ("cos", TT * 32), ("sin", TT * 32),
               ("sel", MH * P), ("causal", P), ("reset", 2 * S), ("iota", NE)):
    CONST[_n] = (_at, _w)
    _at += _w
N_CONST = _at
PC1 = {"norm1": 0, "norm2": 8, "gout": 16, "conv": 24, "gate": 24 + 8 * CW}
N_PC1 = 24 + 8 * CW + 4
PC2 = {"gout": 0, "ba": 8, "bs": 10}
N_PC2 = 14
PLAN = 53200


def constants():
    c = np.zeros((P, N_CONST), np.float32)

    def put(name, a):
        o, w = CONST[name]
        a = np.asarray(a, np.float32)
        c[: a.shape[0], o:o + w] = a.reshape(a.shape[0], w)

    i = np.arange(P)
    put("ident", np.eye(P))
    t = (np.arange(TT)[None, :] * P + i[:, None])[:, :, None]
    s = np.arange(S)[None, None, :]
    count = (abs(t - s) <= 64).astype(int) + ((t - s) % 4 == 0) + ((t - s) % 16 == 0)
    put("lnc", np.where(count > 0, np.log(np.maximum(count, 1)) * AD ** 0.5, -BIG))
    after = i[:, None] > i[None, :]
    put("dmask", np.stack([np.where(after, BIG, 0), np.where(after.T, BIG, 0)], 1))
    half = AD // 2
    freq = (np.float32(10000.0) ** (-np.arange(half, dtype=np.float32) / np.float32(half))).astype(np.float32)
    ang = np.arange(S, dtype=np.float32)[:, None] * freq[None, :]
    for name, f in (("cos", np.cos), ("sin", np.sin)):
        put(name, f(ang).reshape(TT, P, half).transpose(1, 0, 2))
    put("sel", np.repeat(np.eye(MH)[:, :, None], P, 2))
    put("causal", (i[:, None] <= i[None, :]) & (i[:, None] // 64 == i[None, :] // 64))
    put("reset", np.tile((np.arange(2 * S) % 64 != 0)[None], (P, 1)))
    put("iota", np.tile(np.arange(NE)[None], (P, 1)))
    return c


RAISES = {
    "params": (32, 192, 0, 0, 0),
    "pads": (1, 0, 0, 0, 0),
    "pool_step": (3, 0, 0, 0, 0),
    "rotated": (1, 0, 0, 0, 0),
    "kz_zero": (1, 0, 0, 0, 0),
    "gb_landed": (0, 144, 0, 0, 0),
    "ws_causal": (0, 2, 0, 0, 0),
    "zeros2": (0, 2, 0, 0, 0),
    "act_step": (4, 10, 0, 0, 1),
    "rs_out": (3, 8, 0, 0, 1),
    "gw_high": (1, 2, 0, 0, 0),
    "hi_made": (50, 61, 42, 42, 0),
    "t_hi": (28, 37, 9, 9, 0),
    "softplus_made": (1, 2, 0, 0, 0),
    "em_made": (1, 0, 0, 0, 0),
    "silu_made": (1, 0, 0, 0, 0),
    "w_exp": (8, 0, 0, 0, 0),
    "gate_exp": (1, 0, 0, 0, 0),
    "att_exp": (8, 0, 0, 0, 0),
    "relu_made": (16, 0, 0, 0, 0),
    "decay_exp": (0, 2, 0, 0, 0),
    "silu_gate": (0, 2, 0, 0, 0),
    "top_exp": (0, 1, 0, 0, 0),
    "dve_step": (50, 85, 0, 0, 8),
    "rs_in": (3, 8, 0, 0, 1),
    "rows_ready": (3, 6, 0, 0, 0),
    "gw_low": (1, 2, 0, 0, 0),
    "small_copied": (1, 2, 0, 0, 0),
    "abs_made": (1, 2, 0, 0, 0),
    "ag_made": (1, 0, 0, 0, 0),
    "am_made": (1, 0, 0, 0, 0),
    "conv_made": (1, 0, 0, 0, 0),
    "pt_made": (8, 0, 0, 0, 0),
    "num_read": (1, 0, 0, 0, 0),
    "gate_wanted": (1, 0, 0, 0, 0),
    "amax_made": (8, 0, 0, 0, 0),
    "pts_made": (8, 0, 0, 0, 0),
    "al_made": (0, 2, 0, 0, 0),
    "decays": (0, 2, 0, 0, 0),
    "operands_made": (0, 2, 0, 0, 0),
    "kdt_made": (0, 2, 0, 0, 0),
    "sc_made": (0, 2, 0, 0, 0),
    "states_made": (0, 2, 0, 0, 0),
    "vn_made": (0, 2, 0, 0, 0),
    "top_made": (0, 1, 0, 0, 0),
    "mask_made": (0, 1, 0, 0, 0),
    "acc_added": (0, 2, 4, 4, 0),
    "sel_made": (0, 1, 1, 1, 0),
    "small_full": (1, 2, 0, 0, 0),
    "small_turned": (1, 2, 0, 0, 0),
    "am_full": (1, 0, 0, 0, 0),
    "st_full": (4, 0, 0, 0, 0),
    "w_full": (8, 0, 0, 0, 0),
    "pv_done": (8, 0, 0, 0, 0),
    "as_full": (8, 0, 0, 0, 0),
    "p_turned": (8, 0, 0, 0, 0),
    "apv_done": (8, 0, 0, 0, 0),
    "decay_full": (0, 2, 0, 0, 0),
    "kd_turned": (0, 2, 0, 0, 0),
    "sc_full": (0, 2, 0, 0, 0),
    "updates_full": (0, 2, 0, 0, 0),
    "spatial_full": (0, 2, 0, 0, 0),
    "lin_full": (0, 2, 0, 0, 0),
    "logits_full": (0, 1, 0, 0, 0),
    "counted": (0, 1, 0, 0, 0),
    "scattered": (0, 0, 4, 4, 0),
}


def program(nc, t, debug=()):
    with ExitStack() as ctx:
        plan = ctx.enter_context(nc.sbuf_tensor("plan", [P, PLAN], F32))
        start = nc.sbuf_base - 4 * PLAN
        top = [0]

        def at(name, offset, shape, dt=F32):
            return nc.alloc_sbuf_tensor_at(name, list(shape), dt, offset=start + 4 * offset)

        def take(name, shape, dt=F32):
            n = -(-int(np.prod(shape[1:])) // 8) * 8
            top[0] += n
            assert top[0] <= PLAN, name
            return at(name, top[0] - n, shape, dt)

        def lay(offset, *buffers):
            out = {}
            for name, shape in buffers:
                out[name] = at(name, offset, shape)
                offset += int(np.prod(shape[1:]))
            return out, offset

        raw = [take(f"raw{i}", [P, UNIT]) for i in range(RAW_SLOTS)]
        w_hi = [take(f"w_hi{i}", [P, UNIT], F32R) for i in range(SPLIT_SLOTS)]
        w_lo = [take(f"w_lo{i}", [P, UNIT], F32R) for i in range(SPLIT_SLOTS)]
        x = take("x", [P, TT, D])
        x_hi = take("x_hi", [P, KT, S], F32R)
        x_lo = take("x_lo", [P, KT, S], F32R)
        y_at = top[0]
        y = take("y", [P, TT, D])
        const = take("const", [P, N_CONST])
        pc1 = take("pc1", [P, N_PC1])
        pc2 = take("pc2", [P, N_PC2])
        ws_t = take("ws_t", [P, GH, P])
        wa2 = take("wa2", [16, 256])
        gw = take("gw", [P, KT * 16])
        gw_hi = take("gw_hi", [P, KT * 16], F32R)
        gw_lo = take("gw_lo", [P, KT * 16], F32R)
        rw = take("rw", [P, KT * NE])
        rw_hi = take("rw_hi", [P, KT * NE], F32R)
        rw_lo = take("rw_lo", [P, KT * NE], F32R)
        gates = take("gates", [P, TT, NE])
        ones = take("ones", [P, S])
        small = take("small", [P, 160])
        shared = top[0]
        h_hi = take("h_hi", [P, 32, S], F32R)
        h_lo = take("h_lo", [P, 32, S], F32R)
        rows = top[0]
        xn = take("xn", [P, TT, D])
        hid = [take(f"hid{i}", [P, TT, NW]) for i in range(2)]
        sg = at("sg", rows, [P, TT, NW])
        gb = at("gb", y_at, [P, 2, D])
        ln_gb = take("ln_gb", [P, 2, 512])

        a, o = lay(shared, ("qk", [P, TT, D]), ("v", [P, TT, 512]), ("mo", [P, TT, 512]), ("g16", [P, TT, 16]))
        b1, o = lay(o, ("aqk", [P, TT, D]), ("art", [P, TT, D]), ("av", [P, TT, AH, AD + 1]))
        ct_at = o
        b2, o = lay(o, ("ct", [P, 8, S + 4]), ("aq_t", [P, 4, S]), ("kz", [P, AH, S]),
                    ("wexp", [P, 2, 384]), ("pt", [P, 2, 384]))
        assert o <= rows, (o, rows)
        qk, v, mo, g16, aqk, art, av = *a.values(), *b1.values()
        ct, aq_t, kz, wexp, pt = b2.values()
        conv = at("conv", shared, [P, 8, S])
        pa = at("pa", shared + 4128, [P, 2, TT, S])
        pts = at("pts", shared + 4128 + 1024, [P, 2, TT, S])
        hm = at("hm", ct_at, [P, TT, 512])
        sq = at("sq", ct_at + 1024, [P, TT, 512])
        g, _ = lay(rows, *((n, [4, 2, S]) for n in ("gi", "gz", "gabs", "gcum", "ga", "gmax", "gm")))
        gi, gz, gabs, gcum, ga, gmax, gm = g.values()

        c, o = lay(shared, ("qk2", [P, TT, 512]), ("v2", [P, TT, 512]), ("gv", [P, TT, 512]),
                   ("gu", [P, TT, 512]), ("sg2", [P, TT, 512]), ("alr", [P, TT, 16]), ("al", [16, S]))
        qk2, v2, gv, gu, sg2, alr, al = c.values()
        z_at = o
        c, o = lay(o, *((n, [P, 2, S]) for n in ("z", "az", "bcum", "bd", "eb", "ei", "ed", "qd")))
        z, az, bcum, bd, eb, ei, ed, qd = c.values()
        c, o = lay(o, ("qz", [P, 2, 2, S]), ("kiz", [P, GH, S]), ("kd", [P, 2, S]), ("kdt", [P, TT, S]),
                   ("vz", [P, 2, TT, 512]), ("sc", [P, TT, GH, P]), ("sz", [P, 3, GH, P]), ("vn", [P, TT, 512]))
        qz, kiz, kd, kdt, vz, sc, sz, vn = c.values()
        assert o <= top[0], (o, top[0])
        os_ = at("os", shared, [P, TT, 512])
        sq2 = at("sq2", z_at, [P, TT, 512])

        c, o = lay(shared, ("acc", [P, TT, D]), ("y_e", [P, 2, NW]), ("sel", [P, TT, P]), ("sel_t", [P, TT, P]),
                   ("iota1", [P, P]), ("upto", [P, P]), ("place", [P, TT, 20]), ("mask", [P, TT, NE]),
                   ("load", [P, 8]))
        acc, y_e, sel, sel_t, iota1, upto, place, mask, load_max = c.values()
        o += 8
        xe_hi, xe_lo = (at(f"xe_{n}", o + 1024 * i, [P, KT // 4, 4 * P], F32R) for i, n in enumerate(("hi", "lo")))
        he_hi, he_lo = (at(f"he_{n}", o + 2048 + FFE * i, [P, FFE // NW, 4 * P], F32R) for i, n in enumerate(("hi", "lo")))
        assert o + 2048 + 2 * FFE <= rows
        busiest = at("busiest", o - 8, [1, 1], I32)

        bank = [ctx.enter_context(nc.psum_tensor(f"bank{i}", [P, 512], F32)) for i in range(8)]

        def cst(name, p=P):
            o, w = CONST[name]
            return const[0:p, o:o + w]

        ident = cst("ident")

        def sem(name):
            return ctx.enter_context(nc.semaphore(name))

        units = Ring(RAW_SLOTS, UNITS, (0, 2, 0, 0, 0))
        splits = Ring(SPLIT_SLOTS, UNITS, (0, 2, 0, 0, 0))
        pairs = Ring(PAIRS, CHUNKS, (0, 1, 0, 0, 0))
        tbanks = Ring(TBANKS, GROUPS, (0, 1, 0, 0, 0))
        raw_landed = [sem(f"raw_landed{i}") for i in range(RAW_SLOTS)]
        lo_made = sem("lo_made")
        w_used = sem("w_used")
        out_read = [sem("out_read0"), sem("out_read1")]
        t_full = sem("t_full")
        t_read = sem("t_read")
        const_landed = sem("const_landed")
        out_written = sem("out_written")
        raised = {}
        signals = {}

        class Signals:
            def __getattr__(self, name):
                if name not in signals:
                    signals[name] = Signal(sem(name), RAISES.get(name, (0, 0, 0, 0, 0)))
                return signals[name]

        s = Signals()
        block = ctx.enter_context(nc.Block())

        @block.sync
        def _(sp):
            me = Place(raised)

            def load(first, step, k):
                slot = units.slot(me.body, k)
                sp.wait_ge(lo_made, units.free(me.body, step, k))
                unit = step * UNITS[me.body] + (first + k)
                sp.dma_start(raw[slot][:, :], t["weights"][unit]).then_inc(raw_landed[slot], 16)

            with sp.Fori(0, DEPTH) as layer:
                me.enter(0, layer)
                for k in range(UNITS[0]):
                    load(0, layer, k)
            me.enter(1, 0)
            first = DEPTH * UNITS[0]
            for k in range(UNITS[1]):
                load(first, 0, k)
            with sp.Fori(0, NE) as expert:
                me.enter(2, expert)
                for k in range(UNITS[2]):
                    load(first + UNITS[1], expert, k)
            sp.wait_ge(s.busiest_known.sem, 1)
            with sp.If(sp.value_load(busiest[0:1, 0:1], min_val=0, max_val=S) > P):
                with sp.Fori(0, NE) as expert:
                    me.enter(3, expert)
                    for k in range(UNITS[3]):
                        load(first + UNITS[1], expert, k)
            sp.wait_ge(s.x_final.sem, 1)
            sp.dma_start(t["out"], x[:, :, :]).then_inc(out_written, 16)
            sp.wait_ge(out_written, 16)

        @block.gpsimd
        def _(pool):
            me = Place(raised)

            def link(op):
                op.then_inc(*me.up(s.pool_step))
                pool.wait_ge(*me.next(s.pool_step))

            def load_gb(name, layer):
                for i, part in enumerate("gb"):
                    pool.dma_start(gb[:, i, :], t[f"{name}_{part}"][layer].partition_broadcast(P))\
                        .then_inc(*me.up(s.gb_landed, 16))

            pool.dma_start(const[:, :], t["const"]).then_inc(const_landed, 16)
            pool.dma_start(x[:, :, :], t["x"]).then_inc(const_landed, 16)
            pool.dma_start(rw[:, :], t["router"]).then_inc(const_landed, 16)
            pool.memset(ones[:, :], 1.0).then_inc(s.ones_set.sem, 1)

            def rotary():
                for tt in range(TT):
                    src = aqk[:, tt, :].rearrange("p (h two c) -> p h two c", two=2, c=32)
                    dst = art[:, tt, :].rearrange("p (h two c) -> p h two c", two=2, c=32)
                    cos = cst("cos")[:, tt * 32:tt * 32 + 32].unsqueeze(1).to_broadcast([P, 16, 32])
                    sin = cst("sin")[:, tt * 32:tt * 32 + 32].unsqueeze(1).to_broadcast([P, 16, 32])
                    tmp = rot_tmp
                    pool.tensor_tensor(dst[:, :, 0], src[:, :, 0], cos, ALU.mult)
                    pool.tensor_tensor(dst[:, :, 1], src[:, :, 0], sin, ALU.mult)
                    pool.tensor_tensor(tmp[:, 0], src[:, :, 1], sin, ALU.mult)
                    link(pool.tensor_tensor(tmp[:, 1], src[:, :, 1], cos, ALU.mult))
                    pool.tensor_tensor(dst[:, :, 0], dst[:, :, 0], tmp[:, 0], ALU.subtract)
                    last = pool.tensor_tensor(dst[:, :, 1], dst[:, :, 1], tmp[:, 1], ALU.add)
                    if tt < TT - 1:
                        link(last)
                    else:
                        last.then_inc(*me.up(s.rotated))

            rot_tmp = kz[:, 0:4, :].rearrange("p a (b c) -> p (a b) c", c=32).rearrange(
                "p (two h) c -> p two h c", two=2)
            for layer in range(DEPTH):
                me.enter(0, layer)
                for r in out_read:
                    pool.wait_ge(r, pairs.done(0, layer, -1))
                pool.dma_start(pc1[:, :], t["pc1"][layer]).then_inc(*me.up(s.params, 16))
                pool.dma_start(gw[:, :], t["gw"][layer]).then_inc(*me.up(s.params, 16))
                pool.wait_ge(*me.at(s.rows_ready, 1))
                pool.memset(ct[:, :, 0:2], 0.0)
                pool.memset(ct[:, :, S + 2:S + 4], 0.0)
                pool.memset(av[:, :, :, AD:AD + 1], 1.0).then_inc(*me.up(s.pads))
                for r in out_read:
                    pool.wait_ge(r, pairs.done(0, layer, 4))
                rotary()
                pool.wait_ge(*me.at(s.rotated, 1))
                pool.memset(kz[:, :, :], 0.0).then_inc(*me.up(s.kz_zero))

            me.enter(1, 0)
            for layer in range(DEPTH):
                if layer == 0:
                    for r in out_read:
                        pool.wait_ge(r, pairs.done(1, 0, -1))
                else:
                    pool.wait_ge(*me.at(s.rows_ready, 3))
                pool.dma_start(pc2[:, :], t["pc2"][layer]).then_inc(*me.up(s.params, 16))
                pool.dma_start(gw[:, :], t["gw"][DEPTH + layer]).then_inc(*me.up(s.params, 16))
                pool.dma_start(ws_t[:, :, :], t["ws_t"][layer]).then_inc(*me.up(s.params, 16))
                pool.dma_start(wa2[:, :], t["wa2"][layer]).then_inc(*me.up(s.params, 16))
                for i, name in enumerate(("gm_ln_g", "gm_ln_b")):
                    pool.dma_start(ln_gb[:, i, :], t[name][layer].partition_broadcast(P)).then_inc(*me.up(s.params, 16))
                if layer == 0:
                    pool.dma_start(gb[:, 0, :], t["final_g"].partition_broadcast(P)).then_inc(*me.up(s.gb_landed, 16))
                pool.wait_ge(*me.next(s.params, 16 * 6))
                pool.affine_select(out=ws_t[:, :, :], in_=ws_t[:, :, :], compare_op=ALU.is_ge, fill=0.0, base=0,
                                   pattern=[[0, GH], [1, P]], channel_multiplier=-1).then_inc(*me.up(s.ws_causal))
                pool.wait_ge(*me.at(s.rows_ready, 3 * layer + 1))
                for buf in (qz[:, :, :, :], kiz[:, :, :], vz[:, :, :, :], sc[:, :, :, :]):
                    pool.memset(buf, 0.0)
                pool.memset(sz[:, :, :, :], 0.0).then_inc(*me.up(s.zeros2))
                pool.wait_ge(t_full, tbanks.done(1, 0, (0, 25)[layer] + 9))
                load_gb("ln_mix", layer)
                pool.wait_ge(*me.at(s.rows_ready, 3 * layer + 3))
                load_gb("ln_ffn", layer)

        @block.scalar
        def _(act):
            me = Place(raised)

            def link(op):
                op.then_inc(*me.up(s.act_step))
                act.wait_ge(*me.next(s.act_step))

            def high(until):
                while me.unit < min(until, UNITS[me.body]):
                    k, slot = me.unit, units.slot(me.body, me.unit)
                    act.wait_ge(raw_landed[slot], 16 * units.turns(me.body, me.step, k))
                    act.wait_ge(w_used, splits.free(me.body, me.step, k))
                    act.activation(w_hi[splits.slot(me.body, k)][:, :], raw[slot][:, :], ACT.Copy)\
                        .then_inc(*me.up(s.hi_made))
                    me.unit += 1

            def high_t(dest, kt, n, scale=None, cols=2):
                for i in range(n):
                    b = bank[4 + tbanks.slot(me.body, me.group)]
                    act.wait_ge(t_full, tbanks.done(me.body, me.step, me.group))
                    if scale is None:
                        op = act.activation(dest[:, kt + 2 * i:kt + 2 * i + 2, :].rearrange("p a b -> p (a b)"),
                                            b[:, :], ACT.Copy)
                    else:
                        for j in range(2):
                            o = scale + 2 * i + j
                            src = pc1 if me.body == 0 else pc2
                            op = act.activation(dest[:, kt + 2 * i + j, :], b[:, j * S:(j + 1) * S], ACT.Copy,
                                                scale=src[:, o:o + 1])
                    op.then_inc(*me.up(s.t_hi))
                    me.group += 1

            def chunk(kts):
                me.slab += kts
                act.wait_ge(w_used, splits.done(me.body, me.step, (me.slab - 1) // SLABS))
                pair = pairs.slot(me.body, me.chunk)
                me.chunk += 1
                return bank[2 * pair], bank[2 * pair + 1]

            def rsqrt(n):
                act.wait_ge(*me.next(s.rs_in))
                link(act.activation(small[:, 16:16 + n], small[:, 0:n], ACT.Ln))
                act.activation(small[:, 16:16 + n], small[:, 16:16 + n], ACT.Exp, scale=-0.5)\
                    .then_inc(*me.up(s.rs_out))

            def softplus(e_in):
                act.wait_ge(*me.next(s.abs_made))
                link(act.activation(e_in, e_in, ACT.Exp, scale=-1.0))
                act.activation(e_in, e_in, ACT.Ln, bias=1.0).then_inc(*me.up(s.softplus_made))

            def sg_used():
                for r in out_read:
                    act.wait_ge(r, pairs.done(me.body, me.step, me.chunk - 2))

            def silu_gate(b):
                for tt in range(TT):
                    act.activation(sg[:, tt, :], b[tt][:, :], ACT.Silu).then_inc(out_read[tt], 1)

            def high_four(dest):
                act.wait_ge(t_full, tbanks.done(me.body, me.step, me.group))
                act.activation(dest, bank[4 + tbanks.slot(me.body, me.group)][:, :], ACT.Copy).then_inc(*me.up(s.t_hi))
                me.group += 1

            def small_gates():
                act.wait_ge(*me.next(s.params, 16 * (2 if me.body == 0 else 6)))
                act.activation(gw_hi[:, :], gw[:, :], ACT.Copy).then_inc(*me.up(s.gw_high))

            act.wait_ge(const_landed, 48)
            act.activation(rw_hi[:, :], rw[:, :], ACT.Copy).then_inc(s.rw_high.sem, 1)

            with act.Fori(0, DEPTH) as layer:
                me.enter(0, layer)
                rsqrt(TT)
                small_gates()
                high(2)
                high_t(x_hi, 0, 4, PC1["norm1"])
                for c, dst in enumerate((qk[:, 0, 0:512], qk[:, 0, 512:1024], v[:, 0, :], aqk[:, 0, 0:512],
                                         aqk[:, 0, 512:1024], av[:, 0, :, 0:AD], mo[:, 0, :])):
                    high(2 * c + 4)
                    b, _ = chunk(KT)
                    src = b[:, :] if c != 5 else b[:, :].rearrange("p (h d) -> p h d", d=AD)
                    if c == 0:
                        softplus(gabs[:, :, :])
                    if c == 5:
                        act.wait_ge(*me.at(s.pads, 1))
                    act.activation(dst, src, ACT.Copy).then_inc(out_read[0], 1)
                    if c == 2:
                        act.wait_ge(*me.next(s.am_made))
                        act.activation(small[:, 96:112], small[:, 80:96], ACT.Exp, scale=-1.0).then_inc(*me.up(s.em_made))
                        me.group += 4
                    if c == 4:
                        act.wait_ge(*me.next(s.conv_made))
                        act.activation(conv[:, :, :], conv[:, :, :], ACT.Silu).then_inc(*me.up(s.silu_made))
                high(14 + 3)
                for n in range(2 * MH):
                    h, d = divmod(n, 2)
                    w = bank[4 + n % 2]
                    act.wait_ge(*me.next(s.w_full))
                    if n >= 2:
                        act.wait_ge(*me.at(s.pt_made, n - 1))
                    for region, (lo, hi) in enumerate(((0, 256), (256, 384))):
                        st = region if d == 0 else 1 - region
                        o = 64 + d * 8 + st * 4 + h
                        op = act.activation(wexp[:, n % 2, lo:hi], w[:, lo:hi], ACT.Exp, scale=-1.0,
                                            bias=small[:, o:o + 1])
                    op.then_inc(*me.up(s.w_exp))
                rsqrt(8)
                act.wait_ge(*me.next(s.gate_wanted))
                act.activation(mo[:, :, :], mo[:, :, :], ACT.Exp, scale=-1.0).then_inc(*me.up(s.gate_exp))
                me.group += 4
                for h in range(AH):
                    act.wait_ge(*me.next(s.amax_made))
                    if h >= 2:
                        act.wait_ge(*me.at(s.p_turned, h - 1))
                    for tt in range(TT):
                        o = 112 + (h % 2) * 2 + tt
                        op = act.activation(pa[:, h % 2, tt, :], bank[4 + h % 2][:, tt * S:(tt + 1) * S], ACT.Exp,
                                            scale=AD ** -0.5, bias=small[:, o:o + 1])
                    op.then_inc(*me.up(s.att_exp))
                high_t(x_hi, 0, 4, PC1["gout"])
                for c in range(2):
                    high(14 + 2 * c + 4)
                    chunk(KT)
                rsqrt(TT)
                high_t(x_hi, 0, 4, PC1["norm2"])
                for c in range(FF1 // NW):
                    high(18 + 2 * c + 4)
                    b = chunk(KT)
                    if c:
                        sg_used()
                    for tt in range(TT):
                        act.activation(sg[:, tt, :], b[tt][:, :], ACT.Relu).then_inc(*me.up(s.relu_made))
                    if c:
                        high_t(h_hi, 4 * (c - 1), 2)
                high_t(h_hi, FF1 // P - 4, 2)
                high(UNITS[0])

            me.enter(1, 0)
            rsqrt(TT)
            for layer in range(DEPTH):
                u0 = (0, 47)[layer]
                small_gates()
                high(u0 + 2)
                high_t(x_hi, 0, 4)
                me.group += 2
                for c in range(5):
                    high(u0 + 2 * c + 4)
                    b0, b1 = chunk(KT)
                    if c < 2:
                        dst = (qk2, v2)[c]
                        act.activation(dst[:, 0, :], b0[:, :], ACT.Copy).then_inc(out_read[0], 1)
                    else:
                        dst, f = ((gv, ACT.Gelu), (gu, ACT.Gelu), (sg2, ACT.Silu))[c - 2]
                        if c == 2:
                            act.wait_ge(out_read[1], pairs.done(1, 0, me.chunk - 2))
                        act.activation(dst[:, 0, :], b0[:, :], f).then_inc(out_read[0], 1)
                        act.activation(dst[:, 1, :], b1[:, :], f).then_inc(out_read[1], 1)
                    if c == 1:
                        softplus(az[:, :, :])
                        act.wait_ge(*me.next(s.decays))
                        for dst, src, f in ((eb, bcum, 1 / 16), (ei, bcum, -1 / 16), (ed, bd, 1 / 16)):
                            op = act.activation(dst[:, :, :], src[:, :, :], ACT.Exp, scale=f)
                        op.then_inc(*me.up(s.decay_exp))
                rsqrt(8)
                rsqrt(8)
                high_t(x_hi, 0, 4, PC2["gout"])
                for c in range(2):
                    high(u0 + 10 + 2 * c + 4)
                    chunk(KT)
                rsqrt(TT)
                high_t(x_hi, 0, 4)
                if layer == 0:
                    u0 += 14
                    for c in range(6):
                        if c < 5:
                            high(u0 + 4 * c + 4)
                            b = chunk(KT)
                            if c:
                                sg_used()
                            silu_gate(b)
                            high(u0 + 4 * c + 6)
                            chunk(KT)
                        else:
                            b = chunk(KT)
                            sg_used()
                            for tt in range(TT):
                                act.activation(sg[:, tt, 0:256], b[tt][:, 0:256], ACT.Silu).then_inc(*me.up(s.silu_gate))
                            high(u0 + 24)
                        if c:
                            high_t(h_hi, 4 * (c - 1), 2)
                    high_t(h_hi, 20, 1)
                    high(u0 + 33)
                    me.slab += 44
                    me.chunk += 2
                    rsqrt(TT)
                else:
                    act.wait_ge(*me.next(s.top_made))
                    act.activation(small[:, 48:50], small[:, 48:50], ACT.Exp).then_inc(*me.up(s.top_exp))
                    for i in range(KT // 4):
                        high_four(xe_hi[:, i, :])
                    act.wait_ge(s.busiest_known.sem, 1)

            def experts(body, first):
                with act.Fori(0, NE) as step:
                    me.enter(body, step)
                    me.group = 1
                    for c in range(FFE // NW):
                        high(4 * c + 4)
                        b, _ = chunk(KT)
                        if c:
                            act.wait_ge(out_read[1], pairs.done(body, step, c - 1))
                        act.activation(sg[:, 0, :], b[:, :], ACT.Silu).then_inc(out_read[0], 1)
                        me.slab += KT
                        high(4 * c + 6)
                        if c:
                            high_four(he_hi[:, c - 1, :])
                    high(28 + 7)
                    high_four(he_hi[:, FFE // NW - 1, :])
                    high(28 + 9)
                    b, _ = chunk(FFE // P)
                    act.activation(y_e[:, 0, :], b[:, :], ACT.Copy).then_inc(out_read[0], 1)
                    high(28 + 12)
                    for i in range(KT // 4):
                        high_four(xe_hi[:, i, :])
                    high(EXPERT_UNITS)

            experts(2, 0)
            with act.If(act.value_load(busiest[0:1, 0:1], min_val=0, max_val=S) > P):
                experts(3, NE)
            me.enter(4, 0)
            rsqrt(TT)

        @block.vector
        def _(dve):
            me = Place(raised)

            def link(op):
                op.then_inc(*me.up(s.dve_step))
                dve.wait_ge(*me.next(s.dve_step))

            def low(until):
                while me.unit < min(until, UNITS[me.body]):
                    i = splits.slot(me.body, me.unit)
                    dve.wait_ge(*me.at(s.hi_made, me.unit + 1))
                    dve.tensor_tensor(w_lo[i][:, :], raw[units.slot(me.body, me.unit)][:, :],
                                      w_hi[i][:, :].bitcast(F32), ALU.subtract).then_inc(lo_made, 1)
                    me.unit += 1

            def tbank():
                b = bank[4 + tbanks.slot(me.body, me.group)]
                dve.wait_ge(t_full, tbanks.done(me.body, me.step, me.group))
                me.group += 1
                return b

            def low_t(hi, lo, kt, n, scale=None):
                for i in range(n):
                    b = tbank()
                    dve.wait_ge(*me.next(s.t_hi))
                    if scale is None:
                        op = dve.tensor_tensor(lo[:, kt + 2 * i:kt + 2 * i + 2, :].rearrange("p a b -> p (a b)"), b[:, :],
                                               hi[:, kt + 2 * i:kt + 2 * i + 2, :].rearrange("p a b -> p (a b)").bitcast(F32),
                                               ALU.subtract)
                    else:
                        for j in range(2):
                            o, k = scale + 2 * i + j, kt + 2 * i + j
                            src = pc1 if me.body == 0 else pc2
                            op = dve.scalar_tensor_tensor(out=lo[:, k, :], in0=b[:, j * S:(j + 1) * S],
                                                          scalar=src[:, o:o + 1], in1=hi[:, k, :].bitcast(F32),
                                                          op0=ALU.mult, op1=ALU.subtract)
                    op.then_inc(t_read, 1)

            def chunk(kts):
                me.slab += kts
                dve.wait_ge(w_used, splits.done(me.body, me.step, (me.slab - 1) // SLABS))
                pair = pairs.slot(me.body, me.chunk)
                me.chunk += 1
                return bank[2 * pair], bank[2 * pair + 1]

            def rsqrt(n):
                v, r, q = small[:, 0:n], small[:, 16:16 + n], small[:, 32:32 + n]
                dve.wait_ge(*me.next(s.rs_out))
                link(dve.tensor_tensor(q, r, r, ALU.mult))
                link(dve.tensor_tensor(q, q, v, ALU.mult))
                link(dve.tensor_scalar(q, q, -0.5, 1.5, ALU.mult, ALU.add))
                link(dve.tensor_tensor(r, r, q, ALU.mult))
                return r

            def rms(buf, out):
                for tt in range(TT):
                    op = dve.scalar_tensor_tensor(out=out[:, tt, :], in0=buf[:, tt, :], scalar=1.0, in1=buf[:, tt, :],
                                                  op0=ALU.mult, op1=ALU.mult, accum_out=small[:, 32 + tt:33 + tt])
                link(op)
                dve.tensor_scalar(small[:, 0:TT], small[:, 32:32 + TT], 1.0 / D, EPS, ALU.mult, ALU.add)\
                    .then_inc(*me.up(s.rs_in))
                return rsqrt(TT)

            def head_rms(buf, scratch, heads):
                for tt in range(TT):
                    op = dve.tensor_tensor(scratch[:, tt, :], buf[:, tt, :], buf[:, tt, :], ALU.mult)
                link(op)
                link(dve.tensor_reduce(small[:, 32:32 + TT * heads], scratch[:, :, :].rearrange("p t (h d) -> p (t h) d", h=heads),
                                       AX.X, ALU.add))
                dve.tensor_scalar(small[:, 0:TT * heads], small[:, 32:32 + TT * heads], 1.0 / P, EPS, ALU.mult, ALU.add)\
                    .then_inc(*me.up(s.rs_in))
                return rsqrt(TT * heads)

            def layer_norm(src=x):
                for tt in range(TT):
                    for j in range(2):
                        o = 120 + (tt * 2 + j) * 6
                        op = dve.bn_stats(small[:, o:o + 6], src[:, tt, j * 512:(j + 1) * 512])
                link(op)
                for tt in range(TT):
                    op = dve.bn_aggr(small[:, 144 + 2 * tt:146 + 2 * tt], small[:, 120 + tt * 12:132 + tt * 12])
                link(op)
                mv = small[:, 144:148].rearrange("p (t two) -> p t two", two=2)
                op = dve.tensor_scalar(small[:, 0:TT], mv[:, :, 1], 1.0, LN_EPS, ALU.mult, ALU.add)
                op.then_inc(*me.up(s.rs_in))
                r = rsqrt(TT)
                for tt in range(TT):
                    op = dve.tensor_scalar(x[:, tt, :], src[:, tt, :], mv[:, tt, 0:1], r[:, tt:tt + 1], ALU.subtract, ALU.mult)
                link(op)
                if me.body == 1:
                    dve.wait_ge(*me.next(s.gb_landed, 32))
                else:
                    dve.wait_ge(*me.at(s.gb_landed, 0))
                for tt in range(TT):
                    op = dve.tensor_tensor(x[:, tt, :], x[:, tt, :], gb[:, 0, :], ALU.mult)
                link(op)
                for tt in range(TT):
                    op = dve.tensor_tensor(x[:, tt, :], x[:, tt, :], gb[:, 1, :], ALU.add)
                return op

            def scale_rows(out, r):
                for tt in range(TT):
                    op = dve.tensor_scalar(out[:, tt, :], x[:, tt, :], r[:, tt:tt + 1], None, ALU.mult)
                return op

            def add_chunk(c, kts, factor=1.0):
                b = chunk(kts)
                cols = slice(c * NW, (c + 1) * NW)
                for tt in range(TT):
                    dve.scalar_tensor_tensor(out=x[:, tt, cols], in0=x[:, tt, cols], scalar=factor, in1=b[tt][:, :],
                                             op0=ALU.mult, op1=ALU.add).then_inc(out_read[tt], 1)

            def own_adds():
                for r in out_read:
                    dve.wait_ge(r, pairs.done(me.body, me.step, me.chunk - 1))

            def low_small():
                dve.wait_ge(*me.next(s.gw_high))
                dve.tensor_tensor(gw_lo[:, :], gw[:, :], gw_hi[:, :].bitcast(F32), ALU.subtract).then_inc(*me.up(s.gw_low))

            def mlstm_gates():
                dve.wait_ge(*me.next(s.small_turned))
                for d in range(2):
                    o = PC1["gate"] + d
                    dve.tensor_scalar(gi[:, d, :], bank[6][0:4, d * S:(d + 1) * S], pc1[0:4, o:o + 1], None, ALU.add)
                    op = dve.tensor_scalar(gz[:, d, :], bank[7][0:4, d * S:(d + 1) * S], pc1[0:4, o + 2:o + 3], None, ALU.add)
                link(op)
                dve.scalar_tensor_tensor(out=gabs[:, :, :], in0=gz[:, :, :], scalar=-1.0, in1=gz[:, :, :],
                                         op0=ALU.mult, op1=ALU.max).then_inc(*me.up(s.abs_made))
                dve.wait_ge(*me.next(s.softplus_made))
                link(dve.scalar_tensor_tensor(out=gz[:, :, :], in0=gz[:, :, :], scalar=0.0, in1=gabs[:, :, :],
                                              op0=ALU.min, op1=ALU.subtract))

                def both(out, a, b, first, op0, op1):
                    dve.tensor_tensor_scan(out[:, 0, :], a[:, 0, :], b[:, 0, :], first, op0, op1)
                    return dve.tensor_tensor_scan(out[:, 1, ::-1], a[:, 1, ::-1], b[:, 1, ::-1], first, op0, op1)

                one = ones[0:4, :].unsqueeze(1).to_broadcast([4, 2, S])
                link(both(gcum, one, gz, 0.0, ALU.mult, ALU.add))
                link(dve.tensor_tensor(ga[:, :, :], gi[:, :, :], gcum[:, :, :], ALU.subtract))
                link(both(gmax, ga, ga, -BIG, ALU.max, ALU.max))
                dve.tensor_tensor(gm[:, :, :], gcum[:, :, :], gmax[:, :, :], ALU.add).then_inc(*me.up(s.ag_made))

            def linear_gates():
                dve.wait_ge(*me.next(s.decay_full))
                for j in range(2):
                    o = PC2["ba"] + j
                    op = dve.tensor_scalar(z[:, j, :], bank[7][:, j * S:(j + 1) * S], pc2[:, o:o + 1], None, ALU.add)
                link(op)
                dve.scalar_tensor_tensor(out=az[:, :, :], in0=z[:, :, :], scalar=-1.0, in1=z[:, :, :],
                                         op0=ALU.mult, op1=ALU.max).then_inc(*me.up(s.abs_made))
                dve.wait_ge(*me.next(s.softplus_made))
                link(dve.scalar_tensor_tensor(out=z[:, :, :], in0=z[:, :, :], scalar=0.0, in1=az[:, :, :],
                                              op0=ALU.min, op1=ALU.subtract))
                flat = lambda buf: buf[:, :, :].rearrange("p a b -> p (a b)")
                link(dve.tensor_tensor_scan(flat(bcum), cst("reset"), flat(z), 0.0, ALU.mult, ALU.add))
                chunks = flat(bcum).rearrange("p (n c) -> p n c", c=64)
                dve.tensor_tensor(flat(bd).rearrange("p (n c) -> p n c", c=64), chunks[:, :, 63:64].to_broadcast([P, 8, 64]),
                                  chunks, ALU.subtract).then_inc(*me.up(s.decays))

            def linear_operands():
                dve.wait_ge(*me.next(s.decay_exp))
                dve.wait_ge(*me.next(s.zeros2))
                b = tbank()
                dve.scalar_tensor_tensor(out=qd[:, :, :].rearrange("p a b -> p (a b)"), in0=b[:, :], scalar=64 ** -0.5,
                                         in1=eb[:, :, :].rearrange("p a b -> p (a b)"), op0=ALU.mult, op1=ALU.mult)\
                    .then_inc(t_read, 1)
                b = tbank()
                for j in range(2):
                    for e in range(2):
                        half = slice(64 * e, 64 * e + 64)
                        dve.tensor_tensor(kiz[half, 2 * j + e, :], b[half, j * S:(j + 1) * S], ei[half, j, :], ALU.mult)
                dve.tensor_tensor(kd[:, :, :].rearrange("p a b -> p (a b)"), b[:, :],
                                  ed[:, :, :].rearrange("p a b -> p (a b)"), ALU.mult).then_inc(t_read, 1)
                dve.wait_ge(t_read, tbanks.done(1, 0, me.group - 1))
                for par in range(2):
                    split = lambda buf: buf.rearrange("p b (t q c) -> p (b t) q c", t=TT, q=2)[:, :, par, :]
                    dve.tensor_copy(split(qz[:, par, :, :]), split(qd[:, :, :]))
                for r in out_read:
                    dve.wait_ge(r, pairs.done(1, 0, me.chunk - 2))
                for par in range(2):
                    half = slice(64 * par, 64 * par + 64)
                    op = dve.tensor_copy(vz[half, par, :, :], v2[half, :, :])
                op.then_inc(*me.up(s.operands_made))

            def causal_scores():
                dve.wait_ge(*me.next(s.kd_turned))
                dve.tensor_copy(kdt[:, :, :].rearrange("p a b -> p (a b)"), bank[6][:, :]).then_inc(*me.up(s.kdt_made))
                dve.wait_ge(*me.next(s.sc_full))
                mask = cst("causal").bitcast(U32).unsqueeze(1).to_broadcast([P, GH, P])
                for tt in range(TT):
                    op = dve.copy_predicated(sc[:, tt, :, :], mask, bank[4 + tt][:, :].rearrange("p (h i) -> p h i", h=GH))
                op.then_inc(*me.up(s.sc_made))

            def states():
                dve.wait_ge(*me.next(s.updates_full))
                for c, b in enumerate((bank[6], bank[7], bank[4])):
                    for h in range(GH):
                        half = slice(64 * (h % 2), 64 * (h % 2) + 64)
                        update = b[half, (h // 2) * 256 + (h % 2) * P:(h // 2) * 256 + (h % 2) * P + P]
                        if c == 0:
                            op = dve.tensor_copy(sz[half, 0, h, :], update)
                        else:
                            last = c * 64 + 63
                            op = dve.scalar_tensor_tensor(out=sz[half, c, h, :], in0=sz[half, c - 1, h, :],
                                                          scalar=eb[half, h // 2, last:last + 1], in1=update,
                                                          op0=ALU.mult, op1=ALU.add)
                    if c < 2:
                        link(op)
                    else:
                        op.then_inc(*me.up(s.states_made))

            def spatial_norm():
                for r in out_read:
                    dve.wait_ge(r, pairs.done(1, 0, me.chunk - 1))
                for i in range(TT * GH):
                    tt, h = divmod(i, GH)
                    op = dve.bn_stats(small[:, 112 + 6 * i:118 + 6 * i], gv[:, tt, h * P:(h + 1) * P])
                link(op)
                for i in range(TT * GH):
                    op = dve.bn_aggr(small[:, 96 + 2 * i:98 + 2 * i], small[:, 112 + 6 * i:118 + 6 * i])
                link(op)
                mv = small[:, 96:112].rearrange("p (n two) -> p n two", two=2)
                dve.tensor_scalar(small[:, 0:8], mv[:, :, 1], 1.0, LN_EPS, ALU.mult, ALU.add).then_inc(*me.up(s.rs_in))
                r = rsqrt(8)
                for i in range(TT * GH):
                    tt, h = divmod(i, GH)
                    cols = slice(h * P, (h + 1) * P)
                    op = dve.tensor_scalar(vn[:, tt, cols], gv[:, tt, cols], mv[:, i, 0:1], r[:, i:i + 1],
                                           ALU.subtract, ALU.mult)
                link(op)
                for i, f in ((0, ALU.mult), (1, ALU.add)):
                    for tt in range(TT):
                        op = dve.tensor_tensor(vn[:, tt, :], vn[:, tt, :], ln_gb[:, i, :], f)
                    if i == 0:
                        link(op)
                op.then_inc(*me.up(s.vn_made))

            def low_four(hi, lo):
                b = tbank()
                dve.wait_ge(*me.next(s.t_hi))
                dve.tensor_tensor(lo, b[:, :], hi.bitcast(F32), ALU.subtract).then_inc(t_read, 1)

            def select(n):
                for tt in range(TT):
                    op = dve.tensor_scalar(sel[:, tt, :], iota1[:, :], place[:, tt, bass.ds(n, 1)], None, ALU.is_equal)
                op.then_inc(*me.up(s.sel_made))

            def route():
                dve.wait_ge(*me.next(s.logits_full))
                logits, top = small[:, 64:80], small[:, 80:96]
                index = small[:, 96:112].bitcast(U32)
                link(dve.tensor_copy(logits, bank[6][:, 0:TT * NE]))
                for tt in range(TT):
                    part = slice(tt * NE, (tt + 1) * NE)
                    link(dve.max(top[:, part], logits[:, part]))
                    link(dve.max_index(index[:, part], top[:, part], logits[:, part]))
                tops = top.rearrange("p (t n) -> p t n", n=NE)
                link(dve.tensor_copy(small[:, 112:128], index))
                dve.tensor_tensor(small[:, 48:50], tops[:, :, 1], tops[:, :, 0], ALU.subtract).then_inc(*me.up(s.top_made))
                for tt in range(TT):
                    op = dve.tensor_scalar(mask[:, tt, :], cst("iota"), small[:, 112 + tt * NE:113 + tt * NE], None, ALU.is_equal)
                link(op)
                for tt in range(TT):
                    op = dve.scalar_tensor_tensor(out=mask[:, tt, :], in0=cst("iota"), scalar=small[:, 113 + tt * NE:114 + tt * NE],
                                                  in1=mask[:, tt, :], op0=ALU.is_equal, op1=ALU.add)
                dve.tensor_tensor_scan(iota1[:, :], ones[:, 0:P], ones[:, 0:P], 0.0, ALU.mult, ALU.add)
                dve.scalar_tensor_tensor(out=upto[:, :], in0=cst("dmask")[:, P:2 * P], scalar=1.0, in1=ident,
                                         op0=ALU.min, op1=ALU.add).then_inc(*me.up(s.mask_made))
                dve.wait_ge(*me.next(s.top_exp))
                link(dve.tensor_scalar(small[:, 50:52], small[:, 48:50], 1.0, None, ALU.add))
                link(dve.reciprocal(small[:, 52:54], small[:, 50:52]))
                link(dve.tensor_tensor(small[:, 54:56], small[:, 52:54], small[:, 48:50], ALU.mult))
                for tt in range(TT):
                    o = 112 + tt * NE
                    dve.tensor_scalar(gates[:, tt, :], cst("iota"), small[:, o:o + 1], small[:, 52 + tt:53 + tt],
                                      ALU.is_equal, ALU.mult)
                    op = dve.tensor_scalar(small[:, 128 + tt * NE:136 + tt * NE], cst("iota"), small[:, o + 1:o + 2],
                                           small[:, 54 + tt:55 + tt], ALU.is_equal, ALU.mult)
                link(op)
                dve.tensor_tensor(gates[:, :, :].rearrange("p t n -> p (t n)"), gates[:, :, :].rearrange("p t n -> p (t n)"),
                                  small[:, 128:144], ALU.add)
                for tt in range(TT):
                    dve.tensor_scalar(acc[:, tt, :], x[:, tt, :], ALPHA, None, ALU.mult).then_inc(*me.up(s.acc_added))
                dve.wait_ge(*me.next(s.counted))
                for tt in range(TT):
                    dve.tensor_tensor(place[:, tt, 0:NE], bank[7][:, tt * NE:(tt + 1) * NE], mask[:, tt, :], ALU.mult)
                link(dve.tensor_reduce(load_max[:, 0:1], bank[7][:, TT * NE:(TT + 1) * NE], AX.X, ALU.max))
                dve.tensor_copy(busiest[0:1, 0:1], load_max[0:1, 0:1]).then_inc(s.busiest_known.sem, 1)
                for tt in range(TT):
                    op = dve.tensor_scalar(place[:, tt, NE:2 * NE], place[:, tt, 0:NE], -float(P), None, ALU.add)
                    op = dve.memset(place[:, tt, 2 * NE:2 * NE + 1], 0.0)
                link(op)
                select(0)
                for i in range(KT // 4):
                    low_four(xe_hi[:, i, :], xe_lo[:, i, :])

            dve.sem_inc(lo_made, RAW_SLOTS)
            for r in out_read:
                dve.sem_inc(r, PAIRS)
            dve.sem_inc(t_read, TBANKS)
            dve.wait_ge(const_landed, 48)
            dve.wait_ge(s.ones_set.sem, 1)
            dve.wait_ge(s.rw_high.sem, 1)
            dve.tensor_tensor(rw_lo[:, :], rw[:, :], rw_hi[:, :].bitcast(F32), ALU.subtract).then_inc(s.rw_low.sem, 1)

            with dve.Fori(0, DEPTH) as layer:
                me.enter(0, layer)
                r = rms(x, xn)
                scale_rows(xn, r).then_inc(*me.up(s.rows_ready))
                low_small()
                low(2)
                low_t(x_hi, x_lo, 0, 4, PC1["norm1"])
                for c, dst in enumerate((qk[:, 1, 0:512], qk[:, 1, 512:1024], v[:, 1, :], aqk[:, 1, 0:512],
                                         aqk[:, 1, 512:1024], av[:, 1, :, 0:AD], mo[:, 1, :])):
                    low(2 * c + 4)
                    if c == 0:
                        dve.wait_ge(*me.next(s.small_full))
                        dve.tensor_copy(g16[:, :, :].rearrange("p a b -> p (a b)"), bank[6][:, 0:TT * 16])\
                            .then_inc(*me.up(s.small_copied))
                    _, b = chunk(KT)
                    src = b[:, :] if c != 5 else b[:, :].rearrange("p (h d) -> p h d", d=AD)
                    if c == 5:
                        dve.wait_ge(*me.at(s.pads, 1))
                    dve.tensor_copy(dst, src).then_inc(out_read[1], 1)
                    if c == 0:
                        mlstm_gates()
                    if c == 2:
                        dve.wait_ge(*me.next(s.am_full))
                        dve.tensor_copy(small[:, 64:96], bank[7][:, 0:32]).then_inc(*me.up(s.am_made))
                        dve.wait_ge(*me.at(s.pads, 1))
                        for i in range(4):
                            b = tbank()
                            dve.tensor_copy(ct[:, 2 * i:2 * i + 2, 2:S + 2], b[:, :].rearrange("p (a b) -> p a b", a=2))\
                                .then_inc(t_read, 1)
                    if c in (3, 4):
                        dve.wait_ge(t_read, tbanks.done(0, layer, 7))
                        for j in range(CW):
                            for blk in range(4 * (c - 3), 4 * (c - 3) + 4):
                                w = pc1[:, PC1["conv"] + blk * CW + j:PC1["conv"] + blk * CW + j + 1]
                                if j == 0:
                                    op = dve.tensor_scalar(conv[:, blk, :], ct[:, blk, 0:S], w, None, ALU.mult)
                                else:
                                    op = dve.scalar_tensor_tensor(out=conv[:, blk, :], in0=ct[:, blk, j:j + S], scalar=w,
                                                                  in1=conv[:, blk, :], op0=ALU.mult, op1=ALU.add)
                            if j < CW - 1 or c == 3:
                                link(op)
                            else:
                                op.then_inc(*me.up(s.conv_made))
                low(14 + 3)
                for n in range(2 * MH):
                    h, d = divmod(n, 2)
                    if d == 0:
                        dve.wait_ge(*me.next(s.st_full))
                    dve.wait_ge(*me.next(s.w_exp))
                    if n >= 2:
                        dve.wait_ge(*me.at(s.pv_done, n - 1))
                    for region, (lo, hi) in enumerate(((0, 256), (256, 384))):
                        st = region if d == 0 else 1 - region
                        t0 = 0 if region == 0 else P * (1 - d)
                        op = dve.scalar_tensor_tensor(out=pt[:, n % 2, lo:hi],
                                                      in0=bank[6][:, st * S + t0:st * S + t0 + hi - lo],
                                                      scalar=MD ** -0.5, in1=wexp[:, n % 2, lo:hi],
                                                      op0=ALU.mult, op1=ALU.mult)
                    op.then_inc(*me.up(s.pt_made))
                dve.wait_ge(*me.at(s.pv_done, 2 * MH))
                dve.wait_ge(*me.next(s.em_made))
                den = small[:, 0:16]
                link(dve.tensor_copy(den, bank[7][:, 0:16]))
                link(dve.scalar_tensor_tensor(out=den, in0=den, scalar=-1.0, in1=den, op0=ALU.mult, op1=ALU.max))
                em = small[:, 96:112].rearrange("p (d t h) -> p t d h", d=2, t=TT)
                link(dve.tensor_tensor(den.rearrange("p (t d h) -> p t d h", t=TT, d=2), den.rearrange("p (t d h) -> p t d h", t=TT, d=2),
                                       em, ALU.max))
                link(dve.reciprocal(small[:, 16:32], den))
                for d in range(2):
                    for tt in range(TT):
                        rd = small[:, 16 + tt * 8 + d * 4:20 + tt * 8 + d * 4].unsqueeze(2).to_broadcast([P, MH, MD])
                        op = dve.tensor_tensor((hm, sq)[d][:, tt, :].rearrange("p (h c) -> p h c", h=MH),
                                               bank[2 * d + tt][:, :].rearrange("p (h c) -> p h c", h=MH), rd, ALU.mult)
                op.then_inc(*me.up(s.num_read))
                dve.wait_ge(*me.at(s.num_read, 1))
                for tt in range(TT):
                    op = dve.tensor_tensor(hm[:, tt, :], hm[:, tt, :], sq[:, tt, :], ALU.add)
                link(op)
                r = head_rms(hm, sq, MH)
                op = None
                for tt in range(TT):
                    rd = r[:, tt * MH:(tt + 1) * MH].unsqueeze(2).to_broadcast([P, MH, MD])
                    op = dve.tensor_tensor(hm[:, tt, :].rearrange("p (h c) -> p h c", h=MH),
                                           hm[:, tt, :].rearrange("p (h c) -> p h c", h=MH), rd, ALU.mult)
                op.then_inc(*me.up(s.gate_wanted))
                dve.wait_ge(*me.next(s.kz_zero))
                for i in range(4):
                    b = tbank()
                    if i < 2:
                        op = dve.tensor_copy(aq_t[:, 2 * i:2 * i + 2, :].rearrange("p a b -> p (a b)"), b[:, :])
                    else:
                        for j in range(2):
                            for e in range(2):
                                rows_ = slice(64 * e, 64 * e + 64)
                                op = dve.tensor_copy(kz[rows_, 2 * (2 * (i - 2) + j) + e, :], b[rows_, j * S:(j + 1) * S])
                    op.then_inc(t_read, 1)
                dve.wait_ge(*me.next(s.gate_exp))
                dve.wait_ge(*me.at(s.gate_wanted, 1))
                for tt in range(TT):
                    op = dve.tensor_scalar(mo[:, tt, :], mo[:, tt, :], 1.0, None, ALU.add)
                link(op)
                for tt in range(TT):
                    op = dve.reciprocal(mo[:, tt, :], mo[:, tt, :])
                link(op)
                for tt in range(TT):
                    dve.tensor_tensor(y[:, tt, 0:512], hm[:, tt, :], mo[:, tt, :], ALU.mult)

                def turned(h):
                    dve.wait_ge(*me.at(s.p_turned, h + 1))
                    if h >= 2:
                        dve.wait_ge(*me.at(s.apv_done, h - 1))
                    dve.tensor_copy(pts[:, h % 2, :, :].rearrange("p a b -> p (a b)"), bank[6 + h % 2][:, :])\
                        .then_inc(*me.up(s.pts_made))

                def normalise(half):
                    dve.wait_ge(*me.at(s.apv_done, 4 * half + 4))
                    for tt in range(TT):
                        o = bank[2 * half + tt][:, 0:4 * (AD + 1)].rearrange("p (h c) -> p h c", h=4)
                        rr = small[:, 16 + 4 * tt:20 + 4 * tt]
                        link(dve.reciprocal(rr, o[:, :, AD]))
                        op = dve.tensor_tensor(y[:, tt, 512 + half * 256:768 + half * 256].rearrange("p (h c) -> p h c", h=4),
                                               o[:, :, 0:AD], rr.unsqueeze(2).to_broadcast([P, 4, AD]), ALU.mult)
                    return op

                for h in range(AH):
                    dve.wait_ge(*me.next(s.as_full))
                    o = 116 + 2 * (h % 2)
                    if h >= 2:
                        dve.wait_ge(*me.at(s.att_exp, h - 1))
                    link(dve.tensor_reduce(small[:, o:o + 2], bank[4 + h % 2][:, :].rearrange("p (t k) -> p t k", t=TT),
                                           AX.X, ALU.max))
                    dve.tensor_scalar(small[:, o - 4:o - 2], small[:, o:o + 2], -AD ** -0.5, None, ALU.mult)\
                        .then_inc(*me.up(s.amax_made))
                    if h:
                        turned(h - 1)
                    if h == 5:
                        link(normalise(0))
                turned(AH - 1)
                normalise(1).then_inc(*me.up(s.rows_ready))
                low_t(x_hi, x_lo, 0, 4, PC1["gout"])
                for c in range(2):
                    low(14 + 2 * c + 4)
                    add_chunk(c, KT)
                own_adds()
                r = rms(x, xn)
                scale_rows(xn, r).then_inc(*me.up(s.rows_ready))
                low_t(x_hi, x_lo, 0, 4, PC1["norm2"])
                for c in range(FF1 // NW):
                    low(18 + 2 * c + 4)
                    b = chunk(KT)
                    for tt in range(TT):
                        dve.wait_ge(*me.next(s.relu_made))
                        dve.tensor_tensor(hid[c % 2][:, tt, :], b[tt][:, :], sg[:, tt, :], ALU.mult)\
                            .then_inc(out_read[tt], 1)
                    if c:
                        low_t(h_hi, h_lo, 4 * (c - 1), 2)
                low_t(h_hi, h_lo, FF1 // P - 4, 2)
                for c in range(2):
                    low(34 + 8 * c + 8 + 2)
                    add_chunk(c, FF1 // P)
                own_adds()

            me.enter(1, 0)
            r = rms(x, xn)
            link(scale_rows(x, r))
            dve.wait_ge(*me.next(s.gb_landed, 16))
            for tt in range(TT):
                op = dve.tensor_tensor(x[:, tt, :], x[:, tt, :], gb[:, 0, :], ALU.mult)
            op.then_inc(*me.up(s.rows_ready))
            for layer in range(DEPTH):
                u0 = (0, 47)[layer]
                low_small()
                low(u0 + 2)
                low_t(x_hi, x_lo, 0, 4)
                for c in range(5):
                    low(u0 + 2 * c + 4)
                    if c == 0:
                        dve.wait_ge(*me.next(s.small_full))
                        dve.tensor_copy(alr[:, :, :].rearrange("p a b -> p (a b)"), bank[6][:, 0:TT * 16])\
                            .then_inc(*me.up(s.small_copied))
                    _, b = chunk(KT)
                    if c < 2:
                        dve.tensor_copy((qk2, v2)[c][:, 1, :], b[:, :]).then_inc(out_read[1], 1)
                    if c == 0:
                        dve.wait_ge(*me.next(s.small_turned))
                        dve.tensor_copy(al[:, :], bank[6][0:16, 0:S]).then_inc(*me.up(s.al_made))
                    if c == 1:
                        linear_gates()
                    if c == 2:
                        linear_operands()
                    if c == 3:
                        causal_scores()
                states()
                spatial_norm()
                dve.wait_ge(*me.next(s.spatial_full))
                for tt in range(TT):
                    for h in range(GH):
                        cols = slice(h * P, (h + 1) * P)
                        op = dve.scalar_tensor_tensor(out=y[:, tt, cols], in0=bank[tt][:, cols],
                                                      scalar=pc2[:, PC2["bs"] + h:PC2["bs"] + h + 1], in1=gu[:, tt, cols],
                                                      op0=ALU.add, op1=ALU.mult)
                dve.wait_ge(*me.next(s.lin_full))
                for tt in range(TT):
                    op = dve.tensor_copy(os_[:, tt, :], bank[2 + tt][:, :])
                link(op)
                r = head_rms(os_, sq2, GH)
                for tt in range(TT):
                    rd = r[:, tt * GH:(tt + 1) * GH].unsqueeze(2).to_broadcast([P, GH, P])
                    op = dve.tensor_tensor(os_[:, tt, :].rearrange("p (h c) -> p h c", h=GH),
                                           os_[:, tt, :].rearrange("p (h c) -> p h c", h=GH), rd, ALU.mult)
                link(op)
                for tt in range(TT):
                    op = dve.tensor_tensor(y[:, tt, 512:1024], os_[:, tt, :], sg2[:, tt, :], ALU.mult)
                op.then_inc(*me.up(s.rows_ready))
                low_t(x_hi, x_lo, 0, 4, PC2["gout"])
                for c in range(2):
                    low(u0 + 10 + 2 * c + 4)
                    add_chunk(c, KT, ALPHA)
                own_adds()
                layer_norm().then_inc(*me.up(s.rows_ready))
                low_t(x_hi, x_lo, 0, 4)
                if layer == 0:
                    u0 += 14
                    for c in range(6):
                        wide = NW if c < 5 else 256
                        if c < 5:
                            low(u0 + 4 * c + 4)
                            chunk(KT)
                            low(u0 + 4 * c + 6)
                            b = chunk(KT)
                            up0 = 0
                        else:
                            b = chunk(KT)
                            up0 = 256
                        for tt in range(TT):
                            if c < 5:
                                dve.wait_ge(out_read[tt], pairs.done(1, 0, me.chunk - 2))
                            else:
                                dve.wait_ge(*me.next(s.silu_gate))
                            dve.tensor_tensor(hid[c % 2][:, tt, 0:wide], b[tt][:, up0:up0 + wide], sg[:, tt, 0:wide],
                                              ALU.mult).then_inc(out_read[tt], 1)
                        if c == 5:
                            low(u0 + 24)
                        if c:
                            low_t(h_hi, h_lo, 4 * (c - 1), 2)
                    low_t(h_hi, h_lo, 20, 1)
                    for c in range(2):
                        low(u0 + 22 + (8, 11)[c])
                        add_chunk(c, FF2 // P, ALPHA)
                    own_adds()
                    layer_norm().then_inc(*me.up(s.rows_ready))
                else:
                    route()

            def experts(body, first):
                with dve.Fori(0, NE) as step:
                    me.enter(body, step)
                    b = tbank()
                    dve.tensor_copy(sel_t[:, :, :].rearrange("p a b -> p (a b)"), b[:, 0:TT * P]).then_inc(t_read, 1)
                    for c in range(FFE // NW):
                        low(4 * c + 6)
                        _, b = chunk(2 * KT)
                        dve.wait_ge(out_read[0], pairs.done(body, step, c))
                        dve.tensor_tensor(hid[c % 2][:, 0, :], b[:, :], sg[:, 0, :], ALU.mult).then_inc(out_read[1], 1)
                        if c:
                            low_four(he_hi[:, c - 1, :], he_lo[:, c - 1, :])
                    low(28 + 7)
                    low_four(he_hi[:, FFE // NW - 1, :], he_lo[:, FFE // NW - 1, :])
                    select(first + step + 1)
                    low(28 + 9)

                    def add(half):
                        cols = slice(half * NW, (half + 1) * NW)
                        for tt in range(TT):
                            dve.wait_ge(*me.next(s.scattered))
                            dve.scalar_tensor_tensor(out=acc[:, tt, cols], in0=bank[6 + tt][:, :],
                                                     scalar=gates[:, tt, bass.ds(step, 1)], in1=acc[:, tt, cols],
                                                     op0=ALU.mult, op1=ALU.add).then_inc(*me.up(s.acc_added))

                    low(28 + 10)
                    add(0)
                    low(28 + 12)
                    for i in range(KT // 4):
                        low_four(xe_hi[:, i, :], xe_lo[:, i, :])
                    low(EXPERT_UNITS)
                    _, b = chunk(FFE // P * 2)
                    dve.tensor_copy(y_e[:, 1, :], b[:, :]).then_inc(out_read[1], 1)
                    add(1)
                    dve.wait_ge(*me.at(s.acc_added, 2 * TT))

            experts(2, 0)
            with dve.If(dve.value_load(busiest[0:1, 0:1], min_val=0, max_val=S) > P):
                experts(3, NE)
            me.enter(4, 0)
            layer_norm(acc).then_inc(s.x_final.sem, 1)

        @block.tensor
        def _(pe):
            me = Place(raised)

            def product(hi, lo, kts, chunks, group=None, per_chunk=None):
                for c in range(chunks):
                    pair = pairs.slot(me.body, me.chunk)
                    for r in out_read:
                        pe.wait_ge(r, pairs.free(me.body, me.step, me.chunk))
                    me.chunk += 1
                    for kt in range(kts):
                        if group is not None and c == 0 and kt % 2 == 0:
                            pe.wait_ge(t_read, tbanks.done(me.body, me.step, group + kt // 2))
                        k, j = divmod(me.slab, SLABS)
                        slot = splits.slot(me.body, k)
                        if j == 0:
                            pe.wait_ge(lo_made, units.done(me.body, me.step, k))
                        for tt in range(TT):
                            out = bank[2 * pair + tt][:, :]
                            rows = slice(tt * P, (tt + 1) * P)
                            cols = slice(j * NW, (j + 1) * NW)
                            pe.matmul(out, hi[:, kt, rows], w_hi[slot][:, cols], start=kt == 0, stop=False)
                            pe.matmul(out, lo[:, kt, rows], w_hi[slot][:, cols], start=False, stop=False)
                            mm = pe.matmul(out, hi[:, kt, rows], w_lo[slot][:, cols], start=False, stop=kt == kts - 1)
                        if j == SLABS - 1:
                            mm.then_inc(w_used, 1)
                        me.slab += 1
                    if per_chunk is not None:
                        per_chunk(c)

            def turn(src, n):
                for i in range(n):
                    slot = tbanks.slot(me.body, me.group)
                    pe.wait_ge(t_read, tbanks.free(me.body, me.step, me.group))
                    me.group += 1
                    for j in range(2):
                        for tt in range(TT):
                            o = j * S + tt * P
                            op = pe.transpose(bank[4 + slot][:, o:o + P], src(2 * i + j, tt), ident)
                    op.then_inc(t_full, 1)

            def turn_four(src):
                b = bank[4 + tbanks.slot(me.body, me.group)]
                pe.wait_ge(t_read, tbanks.free(me.body, me.step, me.group))
                me.group += 1
                for j in range(4):
                    op = pe.transpose(b[:, j * P:(j + 1) * P], src(j), ident)
                op.then_inc(t_full, 1)

            def gather():
                pe.wait_ge(*me.next(s.sel_made))
                for i in range(KT // 4):
                    b = bank[4 + tbanks.slot(me.body, me.group)]
                    pe.wait_ge(t_read, tbanks.free(me.body, me.step, me.group))
                    me.group += 1
                    for j in range(4):
                        cols = slice((4 * i + j) * P, (4 * i + j + 1) * P)
                        for tt in range(TT):
                            op = pe.matmul(b[:, j * P:(j + 1) * P], x[:, tt, cols], sel[:, tt, :],
                                           start=tt == 0, stop=tt == TT - 1)
                    op.then_inc(t_full, 1)

            def rows_of(buf, start=0):
                return lambda blk, tt: buf[:, tt, start + blk * P:start + (blk + 1) * P]

            def small_product(w_h, w_l, n, b, passes=3):
                for tt in range(TT):
                    rows = slice(tt * P, (tt + 1) * P)
                    for kt in range(KT):
                        cols = slice(kt * n, (kt + 1) * n)
                        out = b[:, tt * n:(tt + 1) * n]
                        pe.matmul(out, x_hi[:, kt, rows], w_h[:, cols], start=kt == 0, stop=False)
                        pe.matmul(out, x_lo[:, kt, rows], w_h[:, cols], start=False, stop=False)
                        op = pe.matmul(out, x_hi[:, kt, rows], w_l[:, cols], start=False, stop=kt == KT - 1)
                return op

            def inputs_made(group):
                pe.wait_ge(t_read, tbanks.done(me.body, me.step, group + 3))

            def small_gates(group):
                inputs_made(group)
                pe.wait_ge(*me.next(s.gw_low))
                small_product(gw_hi, gw_lo, 16, bank[6]).then_inc(*me.up(s.small_full))

            def chunk_read(k):
                for r in out_read:
                    pe.wait_ge(r, pairs.done(me.body, me.step, k))

            pe.sem_inc(w_used, SPLIT_SLOTS)
            pe.sem_inc(t_full, TBANKS)
            pe.wait_ge(const_landed, 48)

            def after_w_in(c):
                if c == 0:
                    pe.wait_ge(*me.next(s.small_copied))
                    for i in range(4):
                        for tt in range(TT):
                            o = (i % 2) * S + tt * P
                            op = pe.transpose(bank[6 + i // 2][0:4, o:o + P], g16[:, tt, 4 * i:4 * i + 4], ident)
                    op.then_inc(*me.up(s.small_turned))
                if c == 2:
                    pe.wait_ge(*me.next(s.ag_made))
                    for i, src in enumerate((ga, gm)):
                        for d in range(2):
                            for tt in range(TT):
                                o = i * 16 + d * 8 + tt * 4
                                op = pe.matmul(bank[7][:, o:o + 4], src[0:4, d, tt * P:(tt + 1) * P], ident[0:4, 0:4],
                                               start=True, stop=True)
                    op.then_inc(*me.up(s.am_full))
                    chunk_read(1)
                    turn(rows_of(qk), 4)

            with pe.Fori(0, DEPTH) as layer:
                me.enter(0, layer)
                pe.wait_ge(*me.next(s.rows_ready))
                turn(rows_of(xn), 4)
                small_gates(0)
                product(x_hi, x_lo, KT, 7, 0, after_w_in)
                def scores(h):
                    if h:
                        pe.wait_ge(*me.at(s.pt_made, 2 * h))
                    for st in range(TT):
                        op = pe.matmul(bank[6][:, st * S:(st + 1) * S], conv[:, 4 + h, st * P:(st + 1) * P], conv[:, h, :],
                                       start=True, stop=True)
                    op.then_inc(*me.up(s.st_full))

                def weights(n):
                    h, d = divmod(n, 2)
                    b = bank[4 + n % 2]
                    if n >= 2:
                        pe.wait_ge(*me.at(s.w_exp, n - 1))
                    sel = cst("sel", 4)[:, h * P:(h + 1) * P]
                    mask = cst("dmask")[:, d * P:(d + 1) * P]
                    pe.matmul(b[:, 0:S], sel, gmax[:, d, :], start=True, stop=False)
                    o = d * P
                    pe.matmul(b[:, o:o + P], ident, mask, start=False, stop=True)
                    q0 = P * (1 - d)
                    pe.matmul(b[:, S:S + P], sel, gmax[:, d, q0:q0 + P], start=True, stop=False)
                    pe.matmul(b[:, S:S + P], ident, mask, start=False, stop=True).then_inc(*me.up(s.w_full))

                def mix(n):
                    h, d = divmod(n, 2)
                    pe.wait_ge(*me.at(s.pt_made, n + 1))
                    for tt in range(TT):
                        first = [(d, tt * P)]
                        if tt == 1 - d:
                            first.append((1 - d, S))
                        for out, rhs in ((bank[2 * d + tt][:, h * MD:(h + 1) * MD], None),
                                         (bank[7][:, tt * 8 + d * 4 + h:tt * 8 + d * 4 + h + 1], ones[:, 0:1])):
                            for i, (st, o) in enumerate(first):
                                r = v[:, st, h * MD:(h + 1) * MD] if rhs is None else rhs
                                op = pe.matmul(out, pt[:, n % 2, o:o + P], r, start=i == 0, stop=i == len(first) - 1)
                    op.then_inc(*me.up(s.pv_done))

                pe.wait_ge(*me.next(s.silu_made))
                chunk_read(6)
                scores(0)
                weights(0)
                weights(1)
                for n in range(2 * MH):
                    mix(n)
                    if n + 2 < 2 * MH:
                        weights(n + 2)
                    if n % 2 and n + 1 < 2 * MH:
                        scores(n // 2 + 1)
                pe.wait_ge(*me.at(s.rotated, 1))
                turn(rows_of(art), 4)
                pe.wait_ge(t_read, tbanks.done(0, layer, 11))
                pe.wait_ge(*me.at(s.num_read, 1))

                def logits(h):
                    if h >= 2:
                        pe.wait_ge(*me.at(s.att_exp, h - 1))
                    b = bank[4 + h % 2]
                    for tt in range(TT):
                        pe.matmul(b[:, tt * S:(tt + 1) * S], aq_t[:, h // 2, tt * P:(tt + 1) * P], kz[:, h, :],
                                  start=True, stop=False)
                        op = pe.matmul(b[:, tt * S:(tt + 1) * S], ident, cst("lnc")[:, tt * S:(tt + 1) * S],
                                       start=False, stop=True)
                    op.then_inc(*me.up(s.as_full))

                def turn_p(h):
                    pe.wait_ge(*me.at(s.att_exp, h + 1))
                    if h >= 2:
                        pe.wait_ge(*me.at(s.pts_made, h - 1))
                    for st in range(TT):
                        for tt in range(TT):
                            o = st * S + tt * P
                            op = pe.transpose(bank[6 + h % 2][:, o:o + P], pa[:, h % 2, tt, st * P:(st + 1) * P], ident)
                    op.then_inc(*me.up(s.p_turned))

                def attend(h):
                    pe.wait_ge(*me.at(s.pts_made, h + 1))
                    for tt in range(TT):
                        for st in range(TT):
                            o = (h % 4) * (AD + 1)
                            op = pe.matmul(bank[2 * (h // 4) + tt][:, o:o + AD + 1], pts[:, h % 2, st, tt * P:(tt + 1) * P],
                                           av[:, st, h, :], start=st == 0, stop=st == TT - 1)
                    op.then_inc(*me.up(s.apv_done))

                logits(0)
                logits(1)
                for h in range(AH):
                    turn_p(h)
                    if h + 2 < AH:
                        logits(h + 2)
                    attend(h)
                pe.wait_ge(*me.next(s.rows_ready))
                turn(rows_of(y), 4)
                product(x_hi, x_lo, KT, 2, 12)
                pe.wait_ge(*me.next(s.rows_ready))
                turn(rows_of(xn), 4)

                def after_up(c, n=FF1 // NW):
                    if c:
                        hidden_turn(c - 1)
                    if c == n - 1:
                        hidden_turn(c)

                def hidden_turn(c, n=2):
                    chunk_read(hidden_chunk(c))
                    turn(rows_of(hid[c % 2]), n)

                hidden_chunk = lambda c: 9 + c
                product(x_hi, x_lo, KT, FF1 // NW, 16, after_up)
                product(h_hi, h_lo, FF1 // P, 2, 20)

            me.enter(1, 0)
            for layer in range(DEPTH):
                g0, c0 = (0, 25)[layer], (0, 20)[layer]
                pe.wait_ge(*me.next(s.rows_ready))
                turn(rows_of(x), 4)
                small_gates(g0)

                def after_w_in2(c):
                    if c == 0:
                        pe.wait_ge(*me.next(s.small_copied))
                        for tt in range(TT):
                            op = pe.transpose(bank[6][0:16, tt * P:(tt + 1) * P], alr[:, tt, :], ident)
                        op.then_inc(*me.up(s.small_turned))
                    if c == 1:
                        pe.wait_ge(*me.next(s.al_made))
                        for j in range(2):
                            op = pe.matmul(bank[7][:, j * S:(j + 1) * S], wa2[:, j * P:(j + 1) * P], al[:, :],
                                           start=True, stop=True)
                        op.then_inc(*me.up(s.decay_full))
                        chunk_read(c0)
                        turn(rows_of(qk2), 2)
                    if c == 3:
                        pe.wait_ge(*me.next(s.operands_made))
                        for tt in range(TT):
                            for j in range(2):
                                o = tt * S + j * P
                                op = pe.transpose(bank[6][:, o:o + P], kd[:, j, tt * P:(tt + 1) * P], ident)
                        op.then_inc(*me.up(s.kd_turned))
                        for tt in range(TT):
                            for h in range(GH):
                                rows = slice(tt * P, (tt + 1) * P)
                                op = pe.matmul(bank[4 + tt][:, h * P:(h + 1) * P], kiz[:, h, rows], qd[:, h // 2, rows],
                                               start=True, stop=True)
                        op.then_inc(*me.up(s.sc_full))
                    if c == 4:
                        pe.wait_ge(*me.next(s.kdt_made))
                        pe.wait_ge(*me.next(s.sc_made))
                        for n, b in enumerate((bank[6], bank[7], bank[4])):
                            tt, par = divmod(n, 2)
                            for j in range(2):
                                op = pe.matmul(b[:, j * 256:(j + 1) * 256], kdt[:, tt, j * P:(j + 1) * P],
                                               vz[:, par, tt, j * 256:(j + 1) * 256], start=True, stop=True)
                        op.then_inc(*me.up(s.updates_full))

                product(x_hi, x_lo, KT, 5, g0, after_w_in2)
                chunk_read(c0 + 4)
                pe.wait_ge(*me.next(s.vn_made))
                pe.wait_ge(*me.next(s.ws_causal))
                for tt in range(TT):
                    for h in range(GH):
                        op = pe.matmul(bank[tt][:, h * P:(h + 1) * P], ws_t[:, h, :], vn[:, tt, h * P:(h + 1) * P],
                                       start=True, stop=True)
                op.then_inc(*me.up(s.spatial_full))
                pe.wait_ge(*me.next(s.states_made))
                for tt in range(TT):
                    for h in range(GH):
                        rows = slice(tt * P, (tt + 1) * P)
                        parts = [(sc[:, tt, h, :], v2[:, tt, h * P:(h + 1) * P])]
                        for par in range(2):
                            n = 2 * tt + par
                            if n:
                                parts.append((qz[:, par, h // 2, rows], sz[:, n - 1, h, :]))
                        for i, (a, b) in enumerate(parts):
                            op = pe.matmul(bank[2 + tt][:, h * P:(h + 1) * P], a, b, start=i == 0, stop=i == len(parts) - 1)
                op.then_inc(*me.up(s.lin_full))
                pe.wait_ge(*me.next(s.rows_ready))
                turn(rows_of(y), 4)
                product(x_hi, x_lo, KT, 2, g0 + 6)
                pe.wait_ge(*me.next(s.rows_ready))
                turn(rows_of(x), 4)
                if layer == 0:
                    def after_pair(c):
                        j = c // 2
                        hidden_chunk = lambda i: 8 + 2 * i if i < 5 else 17
                        if c % 2 and j or c == 10:
                            chunk_read(hidden_chunk(j - 1))
                            turn(rows_of(hid[(j - 1) % 2]), 2)
                        if c == 10:
                            chunk_read(17)
                            turn(rows_of(hid[1]), 1)

                    product(x_hi, x_lo, KT, 11, 10, after_pair)
                    product(h_hi, h_lo, FF2 // P, 2, 14)
                else:
                    inputs_made(35)
                    pe.wait_ge(s.rw_low.sem, 1)
                    small_product(rw_hi, rw_lo, NE, bank[6]).then_inc(*me.up(s.logits_full))
                    pe.wait_ge(*me.next(s.mask_made))
                    pe.matmul(bank[7][:, 0:NE], upto[:, :], mask[:, 0, :], start=True, stop=True)
                    for o, stationary in ((NE, upto[:, :]), (2 * NE, ones[:, 0:P])):
                        pe.matmul(bank[7][:, o:o + NE], ones[:, 0:P], mask[:, 0, :], start=True, stop=False)
                        op = pe.matmul(bank[7][:, o:o + NE], stationary, mask[:, 1, :], start=False, stop=True)
                    op.then_inc(*me.up(s.counted))
                    gather()
                    pe.wait_ge(s.busiest_known.sem, 1)

            def experts(body, first):
                with pe.Fori(0, NE) as step:
                    me.enter(body, step)
                    slot = tbanks.slot(body, 0)
                    pe.wait_ge(t_read, tbanks.free(body, step, 0))
                    me.group = 1
                    for tt in range(TT):
                        op = pe.transpose(bank[4 + slot][:, tt * P:(tt + 1) * P], sel[:, tt, :], ident)
                    op.then_inc(t_full, 1)

                    def slabs(hi, lo, kts, half, before=None):
                        out = bank[2 * pairs.slot(body, me.chunk) + half][:, :]
                        pe.wait_ge(out_read[half], pairs.free(body, step, me.chunk))
                        for kt in range(kts):
                            if before is not None:
                                before(half, kt)
                            k, j = divmod(me.slab, SLABS)
                            slot = splits.slot(body, k)
                            if j == 0:
                                pe.wait_ge(lo_made, units.done(body, step, k))
                            rows = slice(kt % 4 * P, kt % 4 * P + P)
                            cols = slice(j * NW, (j + 1) * NW)
                            pe.matmul(out, hi[:, kt // 4, rows], w_hi[slot][:, cols], start=kt == 0, stop=False)
                            pe.matmul(out, lo[:, kt // 4, rows], w_hi[slot][:, cols], start=False, stop=False)
                            mm = pe.matmul(out, hi[:, kt // 4, rows], w_lo[slot][:, cols], start=False, stop=kt == kts - 1)
                            if j == SLABS - 1:
                                mm.then_inc(w_used, 1)
                            me.slab += 1

                    def hidden_four(c):
                        pe.wait_ge(out_read[1], pairs.done(body, step, c))
                        turn_four(lambda j: hid[c % 2][:, 0, j * P:(j + 1) * P])

                    def before_input(half, kt):
                        if half == 0 and kt % 4 == 0:
                            pe.wait_ge(t_read, tbanks.done(body, step, kt // 4 - 2))

                    def before_down(half, kt):
                        if half == 0 and kt == 20:
                            hidden_four(FFE // NW - 1)
                        if half == 0 and kt % 4 == 0:
                            pe.wait_ge(t_read, tbanks.done(body, step, 1 + kt // 4))
                        if half == 1 and kt == 8:
                            scatter(0)
                        if half == 1 and kt == 16:
                            gather()

                    def scatter(half):
                        pe.wait_ge(out_read[half], pairs.done(body, step, FFE // NW))
                        for tt in range(TT):
                            pe.wait_ge(*me.at(s.acc_added, TT * (half - 1) + tt + 1))
                            pe.matmul(bank[6 + tt][:, :], sel_t[:, tt, :], y_e[:, half, :], start=True, stop=True)\
                                .then_inc(*me.up(s.scattered))

                    for c in range(FFE // NW):
                        slabs(xe_hi, xe_lo, KT, 0, before_input if c == 0 else None)
                        slabs(xe_hi, xe_lo, KT, 1)
                        me.chunk += 1
                        if c:
                            hidden_four(c - 1)
                    for half in range(2):
                        slabs(he_hi, he_lo, FFE // P, half, before_down)
                    me.chunk += 1
                    scatter(1)

            experts(2, 0)
            with pe.If(pe.value_load(busiest[0:1, 0:1], min_val=0, max_val=S) > P):
                experts(3, NE)

        for key, n in raised.items():
            assert key[0].raises[key[1]] == n or debug, (key, n)
        return raised, signals



def unit_stream(parts):
    slabs = []
    for w in parts:
        slabs.append(w.reshape(-1, P, NW))
    slabs = np.concatenate(slabs)
    return slabs.reshape(-1, SLABS, P, NW).transpose(0, 2, 1, 3).reshape(-1, P, UNIT)


def layout(inputs):
    a = {k: np.asarray(v) for k, v in inputs.items()}

    def chunks(w, starts):
        return [w[:, c:c + NW] for c in starts]

    def cols(v):
        return v.reshape(-1, P).T

    parts = []
    w = 512
    for l in range(DEPTH):
        w_in = a["w_in"][l]
        parts += chunks(w_in, (0, w, 2 * w, 4 * w + 16, 5 * w + 16, 6 * w + 16, 3 * w))
        parts += chunks(a["w_out"][l], range(0, D, NW)) + chunks(a["w_up"][l], range(0, FF1, NW))
        parts += chunks(a["w_down"][l], range(0, D, NW))
    for l in range(DEPTH):
        w_in = a["w_in_2"][l]
        parts += chunks(w_in, (1024, 1536, 512, 0, 2048)) + chunks(a["w_out_2"][l], range(0, D, NW))
        if l == 0:
            gate, up = a["ffn_w_gate_2"][0], a["ffn_w_up_2"][0]
            for c in range(0, 5 * NW, NW):
                parts += [gate[:, c:c + NW], up[:, c:c + NW]]
            parts += [np.concatenate([gate[:, 5 * NW:], up[:, 5 * NW:]], 1)]
            parts += chunks(a["ffn_w_down_2"][0], range(0, D, NW))
    for e in range(NE):
        for c in range(0, FFE, NW):
            parts += [a["exp_w_gate_2"][0, e][:, c:c + NW], a["exp_w_up_2"][0, e][:, c:c + NW]]
        parts += chunks(a["exp_w_down_2"][0, e], range(0, D, NW))

    def small_w(m):
        n = m.shape[1]
        return m.reshape(KT, P, n).transpose(1, 0, 2).reshape(P, KT * n)

    def rows4(m, n):
        out = np.zeros((P, n), np.float32)
        out[:4] = m
        return out

    pc1 = np.stack([np.concatenate([
        cols(a["norm1_g"][l]), cols(a["norm2_g"][l]), cols(a["head_norm_g"][l]), np.ones((P, 4), np.float32),
        a["conv_w"][l].reshape(CW, 8, P).transpose(2, 1, 0).reshape(P, 8 * CW),
        rows4(np.concatenate([a["gate_i_b"][l].reshape(2, MH).T, a["gate_f_b"][l].reshape(2, MH).T], 1), 4),
    ], 1) for l in range(DEPTH)])
    pc2 = np.stack([np.concatenate([
        np.ones((P, 4), np.float32), cols(a["gla_norm_g_2"][l]), cols(a["gla_ba_2"][l]), a["gm_bs_2"][l].T,
    ], 1) for l in range(DEPTH)])
    tokens = a["x"].reshape(TT, P, D).transpose(1, 0, 2)
    return {
        "weights": unit_stream(parts),
        "x": tokens,
        "const": constants(),
        "pc1": pc1,
        "pc2": pc2,
        "gw": np.stack([small_w(a["w_in"][l][:, 2048:2064]) for l in range(DEPTH)]
                       + [small_w(a["w_in_2"][l][:, 2560:2576]) for l in range(DEPTH)]),
        "router": small_w(a["router_w_2"][0]),
        "ws_t": a["gm_ws_2"].transpose(0, 3, 1, 2),
        "wa2": a["gla_wa2_2"],
        "gm_ln_g": a["gm_ln_g_2"], "gm_ln_b": a["gm_ln_b_2"],
        "ln_mix_g": a["ln_mix_g_2"], "ln_mix_b": a["ln_mix_b_2"],
        "ln_ffn_g": a["ln_ffn_g_2"], "ln_ffn_b": a["ln_ffn_b_2"],
        "final_g": a["final_g"],
    }


def build(nc, arrays, debug=()):
    t = {n: nc.dram_tensor(f"in_{n}", a.shape, F32, kind="ExternalInput").ap() for n, a in arrays.items()}
    t["out"] = nc.dram_tensor("out_x", (P, TT, D), F32, kind="ExternalOutput").ap()
    return program(nc, t, debug)


def kernel(**inputs):
    import concourse.bacc as bacc
    from concourse.bass_utils import run_bass_kernel_spmd

    arrays = {n: np.ascontiguousarray(v) for n, v in layout(inputs).items()}
    nc = bacc.Bacc("TRN2", target_bir_lowering=False, num_devices=1)
    build(nc, arrays)
    r = run_bass_kernel_spmd(nc, [{f"in_{n}": v for n, v in arrays.items()}], core_ids=[0])
    return r.results[0]["out_x"].transpose(1, 0, 2).reshape(1, S, D)
```

```python
from contextlib import ExitStack

import numpy as np
import concourse.bass as bass
from concourse import mybir

F32 = mybir.dt.float32
F32R = mybir.dt.float32r
U32 = mybir.dt.uint32
I32 = mybir.dt.int32
ALU = mybir.AluOpType
ACT = mybir.ActivationFunctionType
AX = mybir.AxisListType

P = 128
S = 256
TT = S // P
D = 1024
KT = D // P
NW = 512
SLABS = 4
UNIT = SLABS * NW
DEPTH = 2
FF1 = 4096
FF2 = 2816
FFE = 3584
NE = 8
MH, MD = 4, 128
AH, AD = 8, 64
GH = 4
CW = 5
EPS = 1e-6
LN_EPS = 1e-5
ALPHA = (2 * DEPTH) ** 0.25
BIG = 1e30

LO_SLOTS = (5, 5, 7, 7, 7)
HI_SLOTS = (4, 4, 6, 6, 6)
PAIRS, TBANKS = (2,) * 5, (2,) * 5
REPEATS = (DEPTH, 1, NE, NE, 1)
EXPERT_UNITS = 14 + 14 + 14
LEAD = 2
LAYER1_UNITS = 14 + 4 + 16 + 16
UNITS = (LAYER1_UNITS, 10 + 4 + 22 + 11 + 10 + 4, EXPERT_UNITS, EXPERT_UNITS, 0)
CHUNKS = (7 + 2 + 8 + 2, 5 + 2 + 11 + 2 + 5 + 2, 7 + 1, 7 + 1, 0)
GROUPS = (4 + 4 + 4 + 4 + 4 + 16, 4 + 2 + 4 + 4 + 11 + 4 + 2 + 4 + 4 + 2, 1 + 7 + 2, 1 + 7 + 2, 0)

class Ring:

    def __init__(self, sizes, uses, offsets, spare):
        self.sizes, self.uses, self.offsets, self.spare = sizes, uses, offsets, spare
        self.base, self.lag, self.slot_base = [], [], []
        last, n, per_slot = {}, 0, [0] * max(sizes)
        for body, (count, repeats) in enumerate(zip(uses, REPEATS)):
            self.base.append(n)
            self.slot_base.append(list(per_slot))
            lags = [sizes[body]] * count
            for _ in range(repeats):
                for k in range(count):
                    slot = self.slot(body, k)
                    if slot in last:
                        lags[k] = min(lags[k], n - last[slot])
                    last[slot] = n
                    per_slot[slot] += 1
                    n += 1
            self.lag.append(lags)

    def slot(self, body, k):
        return (self.offsets[body] + k) % self.sizes[body]

    def done(self, body, step, k):
        return step * self.uses[body] + (self.base[body] + k + 1 + self.spare)

    def free(self, body, step, k):
        return step * self.uses[body] + (self.base[body] + k + 1 + self.spare - self.lag[body][k])

    def turns(self, body, step, k):
        slot = self.slot(body, k)
        same = [i for i in range(self.uses[body]) if self.slot(body, i) == slot]
        return step * len(same) + (self.slot_base[body][slot] + same.index(k) + 1)


class Signal:

    def __init__(self, sem, raises):
        self.sem, self.raises = sem, raises
        self.base, n = [], 0
        for k, repeats in zip(raises, REPEATS):
            self.base.append(n)
            n += k * repeats


class Place:

    def __init__(self, raised):
        self.raised = raised
        self.enter(0, 0)

    def enter(self, body, step):
        self.body, self.step = body, step
        self.unit = self.slab = self.chunk = self.group = 0
        self.waited = {}

    def up(self, signal, n=1):
        if not isinstance(self.step, int) or self.step == 0:
            key = (signal, self.body)
            self.raised[key] = self.raised.get(key, 0) + n
        return signal.sem, n

    def at(self, signal, k):
        return signal.sem, self.step * signal.raises[self.body] + (signal.base[self.body] + k)

    def body_end(self, signal, body):
        return signal.sem, signal.base[body] + signal.raises[body] * REPEATS[body]

    def next(self, signal, n=1):
        self.waited[signal] = self.waited.get(signal, 0) + n
        return self.at(signal, self.waited[signal])


CONST = {}
_at = 0
for _n, _w in (("ident", P), ("lnc", TT * S), ("dmask", 2 * P), ("cos", TT * 32), ("sin", TT * 32),
               ("sel", MH * P), ("causal", P), ("reset", 2 * S), ("iota", NE)):
    CONST[_n] = (_at, _w)
    _at += _w
N_CONST = _at
PC1 = {"norm1": 0, "norm2": 8, "gout": 16, "conv": 24, "gate": 24 + 8 * CW}
N_PC1 = 24 + 8 * CW + 4
PC2 = {"gout": 0, "ba": 8, "bs": 10}
N_PC2 = 14
PLAN = 53208


def constants():
    c = np.zeros((P, N_CONST), np.float32)

    def put(name, a):
        o, w = CONST[name]
        a = np.asarray(a, np.float32)
        c[: a.shape[0], o:o + w] = a.reshape(a.shape[0], w)

    i = np.arange(P)
    put("ident", np.eye(P))
    t = (np.arange(TT)[None, :] * P + i[:, None])[:, :, None]
    s = np.arange(S)[None, None, :]
    count = (abs(t - s) <= 64).astype(int) + ((t - s) % 4 == 0) + ((t - s) % 16 == 0)
    put("lnc", np.where(count > 0, np.log(np.maximum(count, 1)) * AD ** 0.5, -BIG))
    after = i[:, None] > i[None, :]
    put("dmask", np.stack([np.where(after, BIG, 0), np.where(after.T, BIG, 0)], 1))
    half = AD // 2
    freq = (np.float32(10000.0) ** (-np.arange(half, dtype=np.float32) / np.float32(half))).astype(np.float32)
    ang = np.arange(S, dtype=np.float32)[:, None] * freq[None, :]
    for name, f in (("cos", np.cos), ("sin", np.sin)):
        put(name, f(ang).reshape(TT, P, half).transpose(1, 0, 2))
    put("sel", np.repeat(np.eye(MH)[:, :, None], P, 2))
    put("causal", (i[:, None] <= i[None, :]) & (i[:, None] // 64 == i[None, :] // 64))
    put("reset", np.tile((np.arange(2 * S) % 64 != 0)[None], (P, 1)))
    put("iota", np.tile(np.arange(NE)[None], (P, 1)))
    return c


RAISES = {
    "params": (32, 192, 0, 0, 0),
    "pads": (1, 0, 0, 0, 0),
    "pool_step": (3, 0, 0, 0, 0),
    "rotated": (1, 0, 0, 0, 0),
    "kz_zero": (1, 0, 0, 0, 0),
    "gb_landed": (0, 144, 0, 0, 0),
    "ws_causal": (0, 2, 0, 0, 0),
    "zeros2": (0, 2, 0, 0, 0),
    "hi_made": (50, 63, 42, 42, 0),
    "t_hi": (28, 37, 9, 9, 0),
    "gw_high": (1, 2, 0, 0, 0),
    "act_step": (4, 10, 0, 0, 1),
    "rs_out": (3, 8, 0, 0, 1),
    "softplus_made": (1, 2, 0, 0, 0),
    "em_made": (1, 0, 0, 0, 0),
    "w_exp": (8, 0, 0, 0, 0),
    "silu_made": (1, 0, 0, 0, 0),
    "att_exp": (8, 0, 0, 0, 0),
    "relu_made": (16, 0, 0, 0, 0),
    "decay_exp": (0, 2, 0, 0, 0),
    "silu_gate": (0, 2, 0, 0, 0),
    "top_exp": (0, 1, 0, 0, 0),
    "gw_low": (1, 2, 0, 0, 0),
    "dve_step": (47, 84, 0, 0, 8),
    "rs_in": (3, 8, 0, 0, 1),
    "r_made": (2, 0, 0, 0, 0),
    "small_copied": (1, 0, 0, 0, 0),
    "g16_made": (1, 0, 0, 0, 0),
    "abs_made": (1, 2, 0, 0, 0),
    "ag_made": (1, 0, 0, 0, 0),
    "am_made": (1, 0, 0, 0, 0),
    "conv_made": (1, 0, 0, 0, 0),
    "pt_made": (8, 0, 0, 0, 0),
    "num_read": (1, 0, 0, 0, 0),
    "amax_made": (8, 0, 0, 0, 0),
    "pts_made": (8, 0, 0, 0, 0),
    "rows_ready": (2, 12, 0, 0, 0),
    "al_made": (0, 2, 0, 0, 0),
    "decays": (0, 2, 0, 0, 0),
    "operands_made": (0, 2, 0, 0, 0),
    "kdt_made": (0, 2, 0, 0, 0),
    "sc_made": (0, 2, 0, 0, 0),
    "vn_made": (0, 2, 0, 0, 0),
    "states_made": (0, 2, 0, 0, 0),
    "logits_copied": (0, 1, 0, 0, 0),
    "top_made": (0, 1, 0, 0, 0),
    "mask_made": (0, 1, 0, 0, 0),
    "acc_added": (0, 2, 4, 4, 0),
    "sel_made": (0, 1, 1, 1, 0),
    "small_full": (1, 2, 0, 0, 0),
    "small_by_token": (1, 0, 0, 0, 0),
    "small_turned": (1, 0, 0, 0, 0),
    "am_full": (1, 0, 0, 0, 0),
    "w_full": (8, 0, 0, 0, 0),
    "st_full": (4, 0, 0, 0, 0),
    "pv_done": (8, 0, 0, 0, 0),
    "as_full": (8, 0, 0, 0, 0),
    "p_turned": (8, 0, 0, 0, 0),
    "apv_done": (8, 0, 0, 0, 0),
    "decay_full": (0, 2, 0, 0, 0),
    "kd_turned": (0, 2, 0, 0, 0),
    "sc_full": (0, 2, 0, 0, 0),
    "updates_full": (0, 2, 0, 0, 0),
    "spatial_full": (0, 2, 0, 0, 0),
    "lin_full": (0, 2, 0, 0, 0),
    "logits_full": (0, 1, 0, 0, 0),
    "logits_by_token": (0, 1, 0, 0, 0),
    "counted": (0, 1, 0, 0, 0),
    "scattered": (0, 0, 4, 4, 0),
}


def program(nc, t, debug=()):
    with ExitStack() as ctx:
        plan = ctx.enter_context(nc.sbuf_tensor("plan", [P, PLAN], F32))
        start = nc.sbuf_base - 4 * PLAN
        top = [0]

        def at(name, offset, shape, dt=F32):
            return nc.alloc_sbuf_tensor_at(name, list(shape), dt, offset=start + 4 * offset)

        def take(name, shape, dt=F32):
            n = -(-int(np.prod(shape[1:])) // 8) * 8
            top[0] += n
            assert top[0] <= PLAN, name
            return at(name, top[0] - n, shape, dt)

        def lay(offset, *buffers):
            out = {}
            for name, shape in buffers:
                out[name] = at(name, offset, shape)
                offset += int(np.prod(shape[1:]))
            return out, offset

        raw_at = [top[0] + i * UNIT for i in range(LO_SLOTS[0])]
        for i in range(LO_SLOTS[0]):
            take(f"raw_space{i}", [P, UNIT])
        w_hi = [take(f"w_hi{i}", [P, UNIT], F32R) for i in range(HI_SLOTS[0])]
        x = take("x", [P, TT, D])
        x_t_at = top[0]
        x_hi = take("x_hi", [P, KT, S], F32R)
        x_lo = take("x_lo", [P, KT, S], F32R)
        y_at = top[0]
        y = take("y", [P, TT, D])
        const = take("const", [P, N_CONST])
        pc1 = take("pc1", [P, N_PC1])
        pc2 = take("pc2", [P, N_PC2])
        ws_t = take("ws_t", [P, GH, P])
        wa2 = take("wa2", [16, 256])
        gw = take("gw", [P, KT * 16])
        gw_hi = take("gw_hi", [P, KT * 16], F32R)
        gw_lo = take("gw_lo", [P, KT * 16], F32R)
        rw = take("rw", [P, KT * NE])
        rw_hi = take("rw_hi", [P, KT * NE], F32R)
        rw_lo = take("rw_lo", [P, KT * NE], F32R)
        gates = take("gates", [P, TT, NE])
        ones = take("ones", [P, S])
        small = take("small", [P, 160])
        warm = take("warm", [P, 8])
        r1, r2 = small[:, 152:154], small[:, 154:156]
        shared = top[0]
        h_hi = take("h_hi", [P, 32, S], F32R)
        h_lo = take("h_lo", [P, 32, S], F32R)
        rows = top[0]
        xn = take("xn", [P, TT, D])
        hid = [take(f"hid{i}", [P, TT, NW]) for i in range(2)]
        sg = at("sg", rows, [P, TT, NW])
        gb = at("gb", y_at, [P, 2, D])
        ln_gb = take("ln_gb", [P, 2, 512])

        a, o = lay(shared, ("qk", [P, TT, D]), ("v", [P, TT, MH, MD + 1]), ("mo", [P, TT, 512]), ("g16", [P, TT, 16]))
        aqk_at = o
        b1, o = lay(o, ("aqk", [P, TT, D]), ("art", [P, TT, D]), ("av", [P, TT, AH, AD + 1]))
        ct_at = o
        b2, o = lay(o, ("ct", [P, 8, S + 4]), ("aq_t", [P, 4, S]), ("kz", [P, AH, S]),
                    ("pt", [P, 2, 384]))
        wexp_at = o
        o += 2 * 384
        assert o <= rows, (o, rows)
        qk, v, mo, g16, aqk, art, av = *a.values(), *b1.values()
        ct, aq_t, kz, pt = b2.values()
        conv = at("conv", shared, [P, 8, S])
        pa = at("pa", aqk_at, [P, 2, TT, S])
        pts = at("pts", aqk_at + 1024, [P, 2, TT, S])
        hm = at("hm", ct_at, [P, TT, 512])
        sq = at("sq", ct_at + 1024, [P, TT, 512])
        g, _ = lay(rows, *((n, [4, 2, S]) for n in ("gi", "gz", "gabs", "gcum", "ga", "gmax", "gm")))
        gi, gz, gabs, gcum, ga, gmax, gm = g.values()
        g16t = at("g16t", rows + 7 * 2 * S, [16, S])
        wexp = [at(f"wexp{i}", o, [P, 384]) for i, o in enumerate(
            [rows + 384 * i for i in range(5)] + [rows + 7 * 2 * S] + [wexp_at, wexp_at + 384])]

        c, o = lay(shared, ("qk2", [P, TT, 512]), ("v2", [P, TT, 512]), ("gv", [P, TT, 512]),
                   ("gu", [P, TT, 512]), ("sg2", [P, TT, 512]), ("al", [16, S]))
        qk2, v2, gv, gu, sg2, al = c.values()
        z_at = o
        c, o = lay(o, *((n, [P, 2, S]) for n in ("z", "az", "bcum", "bd", "eb", "ei", "ed", "qd")))
        z, az, bcum, bd, eb, ei, ed, qd = c.values()
        c, o = lay(o, ("qz", [P, 2, 2, S]), ("kiz", [P, GH, S]), ("kd", [P, 2, S]), ("kdt", [P, TT, S]),
                   ("vz", [P, 2, TT, 512]), ("sc", [P, TT, GH, P]), ("sz", [P, 3, GH, P]), ("vn", [P, TT, 512]))
        qz, kiz, kd, kdt, vz, sc, sz, vn = c.values()
        assert o <= top[0], (o, top[0])
        os_ = at("os", shared, [P, TT, 512])
        sq2 = at("sq2", z_at, [P, TT, 512])

        c, o = lay(shared, ("acc", [P, TT, D]), ("y_e", [P, 2, NW]), ("sel", [P, TT, P]), ("sel_t", [P, TT, P]),
                   ("iota1", [P, P]), ("upto", [P, P]), ("place", [P, TT, 20]), ("mask", [P, TT, NE]), ("logits_t", [NE, S]),
                   ("load", [P, 8]))
        acc, y_e, sel, sel_t, iota1, upto, place, mask, logits_t, load_max = c.values()
        busiest = at("busiest", o, [1, 1], I32)
        o += 8
        xe_hi, xe_lo = (at(f"xe_{n}", o + 1024 * i, [P, KT // 4, 4 * P], F32R) for i, n in enumerate(("hi", "lo")))
        he_hi, he_lo = (at(f"he_{n}", o + 2048 + FFE * i, [P, FFE // NW, 4 * P], F32R) for i, n in enumerate(("hi", "lo")))
        o += 2048 + 2 * FFE
        raw_at += [x_t_at, x_t_at + UNIT]
        w_hi += [at(f"w_hi{HI_SLOTS[0] + i}", o + i * UNIT, [P, UNIT], F32R) for i in range(2)]
        sg_e = at("sg_e", rows + 1536, [P, NW])
        assert o + 2 * UNIT <= rows + 1536
        raw = [at(f"raw{i}", o, [P, UNIT]) for i, o in enumerate(raw_at)]
        w_lo = [at(f"w_lo{i}", o, [P, UNIT], F32R) for i, o in enumerate(raw_at)]

        bank = [ctx.enter_context(nc.psum_tensor(f"bank{i}", [P, 512], F32)) for i in range(8)]

        def mixed(d, tt, h):
            if h < 3:
                return bank[2 * d + tt][:, h * (MD + 1):(h + 1) * (MD + 1)]
            i = 2 * d + tt
            return bank[7][:, i * (MD + 1):(i + 1) * (MD + 1)] if i < 3 else bank[5][:, 0:MD + 1]

        def cst(name, p=P):
            o, w = CONST[name]
            return const[0:p, o:o + w]

        ident = cst("ident")

        def sem(name):
            return ctx.enter_context(nc.semaphore(name))

        spare = max(LO_SLOTS)
        units = Ring(LO_SLOTS, UNITS, (0, 0, 1, 1, 1), spare)
        splits = Ring(HI_SLOTS, UNITS, (0, 2, 3, 3, 3), spare)
        pairs = Ring(PAIRS, CHUNKS, (0, 1, 0, 0, 0), 2)
        tbanks = Ring(TBANKS, GROUPS, (0, 1, 0, 0, 0), 2)
        raw_landed = [sem(f"raw_landed{i}") for i in range(spare)]
        lo_made = sem("lo_made")
        w_used = sem("w_used")
        out_read = [sem("out_read0"), sem("out_read1")]
        t_full = sem("t_full")
        t_read = sem("t_read")
        x_landed = sem("x_landed")
        const_landed = sem("const_landed")
        out_written = sem("out_written")
        raised = {}
        signals = {}

        class Signals:
            def __getattr__(self, name):
                if name not in signals:
                    signals[name] = Signal(sem(name), RAISES.get(name, (0, 0, 0, 0, 0)))
                return signals[name]

        s = Signals()
        def unit_of(body, step, k):
            return (step, k) if body < 2 or k < EXPERT_UNITS else (step + 1, k - EXPERT_UNITS)

        block = ctx.enter_context(nc.Block())

        @block.sync
        def _(sp):
            me = Place(raised)

            def load(first, step, k):
                unit = step * UNITS[me.body] + (first + k)
                step, k = unit_of(me.body, step, k)
                slot = units.slot(me.body, k)
                sp.wait_ge(w_used, units.free(me.body, step, k))
                sp.dma_start(raw[slot][:, :], t["weights"][unit]).then_inc(raw_landed[slot], 16)

            sp.dma_start(const[:, 0:P], t["const"][:, 0:P]).then_inc(x_landed, 16)
            sp.dma_start(x[:, :, :], t["x"]).then_inc(x_landed, 16)
            with sp.Fori(0, DEPTH) as layer:
                me.enter(0, layer)
                for k in range(UNITS[0]):
                    load(0, layer, k)
            me.enter(1, 0)
            first = DEPTH * UNITS[0]
            for k in range(UNITS[1]):
                load(first, 0, k)
            with sp.Fori(0, NE) as expert:
                me.enter(2, expert)
                for k in range(UNITS[2]):
                    if k == LO_SLOTS[1] - 1:
                        sp.wait_ge(*me.body_end(s.logits_full, 1))
                    load(first + UNITS[1], expert, k)
            for k in range(LEAD):
                load(first + UNITS[1], NE, k)
            sp.wait_ge(s.busiest_known.sem, 1)
            with sp.If(sp.value_load(busiest[0:1, 0:1], min_val=0, max_val=S) > P):
                with sp.Fori(0, NE) as expert:
                    me.enter(3, expert)
                    for k in range(LEAD, UNITS[3] + LEAD):
                        load(first + UNITS[1], expert, k)
            sp.wait_ge(s.x_final.sem, 1)
            sp.dma_start(t["out"], x[:, :, :]).then_inc(out_written, 16)
            sp.wait_ge(out_written, 16)

        @block.gpsimd
        def _(pool):
            me = Place(raised)

            def link(op):
                op.then_inc(*me.up(s.pool_step))
                pool.wait_ge(*me.next(s.pool_step))

            def load_gb(name, layer):
                for i, part in enumerate("gb"):
                    pool.dma_start(gb[:, i, :], t[f"{name}_{part}"][layer].partition_broadcast(P))\
                        .then_inc(*me.up(s.gb_landed, 16))

            pool.memset(ones[:, :], 1.0).then_inc(s.ones_set.sem, 1)

            def rotary():
                for tt in range(TT):
                    src = aqk[:, tt, :].rearrange("p (h two c) -> p h two c", two=2, c=32)
                    dst = art[:, tt, :].rearrange("p (h two c) -> p h two c", two=2, c=32)
                    cos = cst("cos")[:, tt * 32:tt * 32 + 32].unsqueeze(1).to_broadcast([P, 16, 32])
                    sin = cst("sin")[:, tt * 32:tt * 32 + 32].unsqueeze(1).to_broadcast([P, 16, 32])
                    tmp = rot_tmp
                    pool.tensor_tensor(dst[:, :, 0], src[:, :, 0], cos, ALU.mult)
                    pool.tensor_tensor(dst[:, :, 1], src[:, :, 0], sin, ALU.mult)
                    pool.tensor_tensor(tmp[:, 0], src[:, :, 1], sin, ALU.mult)
                    link(pool.tensor_tensor(tmp[:, 1], src[:, :, 1], cos, ALU.mult))
                    pool.tensor_tensor(dst[:, :, 0], dst[:, :, 0], tmp[:, 0], ALU.subtract)
                    last = pool.tensor_tensor(dst[:, :, 1], dst[:, :, 1], tmp[:, 1], ALU.add)
                    if tt < TT - 1:
                        link(last)
                    else:
                        last.then_inc(*me.up(s.rotated))

            rot_tmp = kz[:, 0:4, :].rearrange("p a (b c) -> p (a b) c", c=32).rearrange(
                "p (two h) c -> p two h c", two=2)
            for layer in range(DEPTH):
                me.enter(0, layer)
                if layer:
                    pool.wait_ge(*me.at(s.r_made, 0))
                pool.dma_start(pc1[:, :], t["pc1"][layer]).then_inc(*me.up(s.params, 16))
                pool.dma_start(gw[:, :], t["gw"][layer]).then_inc(*me.up(s.params, 16))
                if layer == 0:
                    pool.dma_start(const[:, P:N_CONST], t["const"][:, P:N_CONST]).then_inc(const_landed, 16)
                    pool.dma_start(rw[:, :], t["router"]).then_inc(const_landed, 16)
                for r in out_read:
                    pool.wait_ge(r, pairs.done(0, layer, -1))
                pool.memset(ct[:, :, 0:2], 0.0)
                pool.memset(ct[:, :, S + 2:S + 4], 0.0)
                pool.memset(v[:, :, :, MD:MD + 1], 1.0)
                pool.memset(av[:, :, :, AD:AD + 1], 1.0).then_inc(*me.up(s.pads))
                for r in out_read:
                    pool.wait_ge(r, pairs.done(0, layer, 4))
                pool.wait_ge(const_landed, 32)
                rotary()
                pool.wait_ge(*me.at(s.rotated, 1))
                pool.memset(kz[:, :, :], 0.0).then_inc(*me.up(s.kz_zero))

            me.enter(1, 0)
            for layer in range(DEPTH):
                if layer == 0:
                    pool.wait_ge(*me.at(s.r_made, 0))
                else:
                    pool.wait_ge(*me.at(s.rows_ready, 6))
                pool.dma_start(pc2[:, :], t["pc2"][layer]).then_inc(*me.up(s.params, 16))
                pool.dma_start(gw[:, :], t["gw"][DEPTH + layer]).then_inc(*me.up(s.params, 16))
                pool.dma_start(ws_t[:, :, :], t["ws_t"][layer]).then_inc(*me.up(s.params, 16))
                pool.dma_start(wa2[:, :], t["wa2"][layer]).then_inc(*me.up(s.params, 16))
                for i, name in enumerate(("gm_ln_g", "gm_ln_b")):
                    pool.dma_start(ln_gb[:, i, :], t[name][layer].partition_broadcast(P)).then_inc(*me.up(s.params, 16))
                if layer == 0:
                    pool.dma_start(gb[:, 0, :], t["final_g"].partition_broadcast(P)).then_inc(*me.up(s.gb_landed, 16))
                pool.wait_ge(*me.next(s.params, 16 * 6))
                pool.affine_select(out=ws_t[:, :, :], in_=ws_t[:, :, :], compare_op=ALU.is_ge, fill=0.0, base=0,
                                   pattern=[[0, GH], [1, P]], channel_multiplier=-1).then_inc(*me.up(s.ws_causal))
                pool.wait_ge(*me.at(s.rows_ready, (2, 8)[layer]))
                for buf in (qz[:, :, :, :], kiz[:, :, :], vz[:, :, :, :], sc[:, :, :, :]):
                    pool.memset(buf, 0.0)
                pool.memset(sz[:, :, :, :], 0.0).then_inc(*me.up(s.zeros2))
                pool.wait_ge(t_full, tbanks.done(1, 0, (0, 25)[layer] + 9))
                load_gb("ln_mix", layer)
                pool.wait_ge(*me.at(s.rows_ready, (6, 12)[layer]))
                load_gb("ln_ffn", layer)

        @block.scalar
        def _(act):
            me = Place(raised)

            def link(op):
                op.then_inc(*me.up(s.act_step))
                act.wait_ge(*me.next(s.act_step))

            def high_part(body, step, k):
                step, k = unit_of(body, step, k)
                slot = units.slot(body, k)
                act.wait_ge(raw_landed[slot], 16 * units.turns(body, step, k))
                act.wait_ge(w_used, splits.free(body, step, k))
                act.activation(w_hi[splits.slot(body, k)][:, :], raw[slot][:, :], ACT.Copy).then_inc(*me.up(s.hi_made))

            def high(until):
                while me.unit < min(until, UNITS[me.body] + (LEAD if me.body >= 2 else 0)):
                    high_part(me.body, me.step, me.unit)
                    me.unit += 1

            def high_t(dest, kt, n, scale=None, cols=2):
                for i in range(n):
                    b = bank[4 + tbanks.slot(me.body, me.group)]
                    act.wait_ge(t_full, tbanks.done(me.body, me.step, me.group))
                    if scale is None:
                        op = act.activation(dest[:, kt + 2 * i:kt + 2 * i + 2, :].rearrange("p a b -> p (a b)"),
                                            b[:, :], ACT.Copy)
                    else:
                        for j in range(2):
                            o = scale + 2 * i + j
                            src = pc1 if me.body == 0 else pc2
                            op = act.activation(dest[:, kt + 2 * i + j, :], b[:, j * S:(j + 1) * S], ACT.Copy,
                                                scale=src[:, o:o + 1])
                    op.then_inc(*me.up(s.t_hi))
                    me.group += 1

            def chunk(kts):
                me.slab += kts
                act.wait_ge(w_used, splits.done(me.body, me.step, (me.slab - 1) // SLABS))
                pair = pairs.slot(me.body, me.chunk)
                me.chunk += 1
                return bank[2 * pair], bank[2 * pair + 1]

            def root(n):
                link(act.activation(warm[:, 0:1], ones[:, 0:1], ACT.Sqrt))
                act.wait_ge(*me.next(s.rs_in))
                act.activation(small[:, 16:16 + n], small[:, 0:n], ACT.Sqrt).then_inc(*me.up(s.rs_out))

            def softplus(e_in):
                act.wait_ge(*me.next(s.abs_made))
                link(act.activation(e_in, e_in, ACT.Exp, scale=-1.0))
                act.activation(e_in, e_in, ACT.Ln, bias=1.0).then_inc(*me.up(s.softplus_made))

            def sg_used():
                for r in out_read:
                    act.wait_ge(r, pairs.done(me.body, me.step, me.chunk - 2))

            def silu_gate(b):
                for tt in range(TT):
                    act.activation(sg[:, tt, :], b[tt][:, :], ACT.Silu).then_inc(out_read[tt], 1)

            def high_four(dest):
                act.wait_ge(t_full, tbanks.done(me.body, me.step, me.group))
                act.activation(dest, bank[4 + tbanks.slot(me.body, me.group)][:, :], ACT.Copy).then_inc(*me.up(s.t_hi))
                me.group += 1

            def small_gates():
                act.activation(gw_hi[:, :], gw[:, :], ACT.Copy).then_inc(*me.up(s.gw_high))

            def decay_weights(first):
                for n in range(first, first + 2):
                    h, d = divmod(n, 2)
                    act.wait_ge(*me.next(s.w_full))
                    for region, (lo, hi) in enumerate(((0, 256), (256, 384))):
                        st = region if d == 0 else 1 - region
                        o = 64 + d * 8 + st * 4 + h
                        op = act.activation(wexp[n][:, lo:hi], bank[4 + n % 2][:, lo:hi], ACT.Exp, scale=-1.0,
                                            bias=small[:, o:o + 1])
                    op.then_inc(*me.up(s.w_exp))

            act.wait_ge(s.ones_set.sem, 1)

            with act.Fori(0, DEPTH) as layer:
                me.enter(0, layer)
                high(2)
                act.wait_ge(*me.next(s.params, 16 * 2))
                high_t(x_hi, 0, 4, PC1["norm1"])
                small_gates()
                root(TT)
                act.wait_ge(*me.next(s.r_made))
                for c, dst in enumerate((qk[:, 0, 0:512], qk[:, 0, 512:1024], v[:, 0, :, 0:MD], aqk[:, 0, 0:512],
                                         aqk[:, 0, 512:1024], av[:, 0, :, 0:AD], mo[:, 0, :])):
                    if c == 2:
                        softplus(gabs[:, :, :])
                    high(2 * c + 4)
                    if c >= 4:
                        decay_weights(2 * (c - 4))
                    if c == 6:
                        act.wait_ge(*me.next(s.conv_made))
                        act.activation(conv[:, :, :], conv[:, :, :], ACT.Silu).then_inc(*me.up(s.silu_made))
                    b, b1 = chunk(KT)
                    src = b[:, :] if c not in (2, 5) else b[:, :].rearrange("p (h d) -> p h d", d=MD if c == 2 else AD)
                    if c == 6:
                        for tt in range(TT):
                            act.activation(mo[:, tt, :], (b, b1)[tt][:, :], ACT.Sigmoid, scale=r1[:, tt:tt + 1])\
                                .then_inc(out_read[tt], 1)
                        continue
                    if c == 5:
                        act.wait_ge(*me.at(s.pads, 1))
                    act.activation(dst, src, ACT.Copy, scale=r1[:, 0:1]).then_inc(out_read[0], 1)
                    if c == 3:
                        act.wait_ge(*me.next(s.am_made))
                        act.activation(small[:, 96:112], small[:, 80:96], ACT.Exp, scale=-1.0).then_inc(*me.up(s.em_made))
                        me.group += 4
                high(14 + 3)
                decay_weights(6)
                me.group += 4
                for h in range(AH):
                    act.wait_ge(*me.next(s.amax_made))
                    if h >= 2:
                        act.wait_ge(*me.at(s.p_turned, h - 1))
                    for tt in range(TT):
                        o = 112 + (h % 2) * 2 + tt
                        op = act.activation(pa[:, h % 2, tt, :], bank[4 + h % 2][:, tt * S:(tt + 1) * S], ACT.Exp,
                                            scale=AD ** -0.5, bias=small[:, o:o + 1])
                    op.then_inc(*me.up(s.att_exp))
                    if h == 2:
                        root(8)
                high_t(x_hi, 0, 4, PC1["gout"])
                for c in range(2):
                    high(14 + 2 * c + 4)
                    chunk(KT)
                high_t(x_hi, 0, 4, PC1["norm2"])
                root(TT)
                act.wait_ge(*me.next(s.r_made))
                for c in range(FF1 // NW):
                    high(18 + 2 * c + 4)
                    b = chunk(KT)
                    if c:
                        sg_used()
                    for tt in range(TT):
                        act.activation(sg[:, tt, :], b[tt][:, :], ACT.Relu, scale=r2[:, tt:tt + 1]).then_inc(*me.up(s.relu_made))
                    if c:
                        high_t(h_hi, 4 * (c - 1), 2)
                high(34 + 6)
                high_t(h_hi, FF1 // P - 4, 2)
                high(UNITS[0])

            me.enter(1, 0)
            root(TT)
            act.wait_ge(const_landed, 32)
            act.activation(rw_hi[:, :], rw[:, :], ACT.Copy).then_inc(s.rw_high.sem, 1)
            for layer in range(DEPTH):
                u0 = (0, 47)[layer]
                high(u0 + 2)
                high_t(x_hi, 0, 4)
                act.wait_ge(*me.next(s.params, 16 * 6))
                small_gates()
                me.group += 2
                for c in range(5):
                    high(u0 + 2 * c + 4)
                    if c == 4:
                        root(8)
                    b0, b1 = chunk(KT)
                    if c < 2:
                        dst = (qk2, v2)[c]
                        act.activation(dst[:, 0, :], b0[:, :], ACT.Copy).then_inc(out_read[0], 1)
                    else:
                        dst, f = ((gv, ACT.Gelu), (gu, ACT.Gelu), (sg2, ACT.Silu))[c - 2]
                        if c == 2:
                            act.wait_ge(out_read[1], pairs.done(1, 0, me.chunk - 2))
                        act.activation(dst[:, 0, :], b0[:, :], f).then_inc(out_read[0], 1)
                        act.activation(dst[:, 1, :], b1[:, :], f).then_inc(out_read[1], 1)
                    if c == 1:
                        softplus(az[:, :, :])
                        act.wait_ge(*me.next(s.decays))
                        for dst, src, f in ((eb, bcum, 1 / 16), (ei, bcum, -1 / 16), (ed, bd, 1 / 16)):
                            op = act.activation(dst[:, :, :], src[:, :, :], ACT.Exp, scale=f)
                        op.then_inc(*me.up(s.decay_exp))
                high_t(x_hi, 0, 2, PC2["gout"])
                root(8)
                high_t(x_hi, 4, 2, PC2["gout"] + 4)
                for c in range(2):
                    high(u0 + 10 + 2 * c + 4)
                    chunk(KT)
                root(TT)
                high_t(x_hi, 0, 4)
                if layer == 0:
                    u0 += 14
                    for c in range(6):
                        if c < 5:
                            high(u0 + 4 * c + 4)
                            b = chunk(KT)
                            if c:
                                sg_used()
                            silu_gate(b)
                            high(u0 + 4 * c + 6)
                            chunk(KT)
                        else:
                            high(u0 + 24)
                            b = chunk(KT)
                            sg_used()
                            for tt in range(TT):
                                act.activation(sg[:, tt, 0:256], b[tt][:, 0:256], ACT.Silu).then_inc(*me.up(s.silu_gate))
                        if c:
                            high_t(h_hi, 4 * (c - 1), 2)
                    high(u0 + 22 + 4)
                    high_t(h_hi, 20, 1)
                    high(u0 + 33)
                    high(u0 + 33 + 2)
                    me.slab += 44
                    me.chunk += 2
                    root(TT)
                else:
                    act.wait_ge(*me.next(s.top_made))
                    act.activation(small[:, 48:50], small[:, 48:50], ACT.Exp).then_inc(*me.up(s.top_exp))
                    for k in range(LEAD):
                        high_part(2, 0, k)
                    for i in range(KT // 4):
                        high_four(xe_hi[:, i, :])
                    act.wait_ge(s.busiest_known.sem, 1)

            def experts(body):
                with act.Fori(0, NE) as step:
                    me.enter(body, step)
                    me.unit, me.group = LEAD, 1
                    for c in range(FFE // NW):
                        high(4 * c + 4)
                        b, _ = chunk(KT)
                        if c:
                            act.wait_ge(out_read[1], pairs.done(body, step, c - 1))
                        act.activation(sg_e[:, :], b[:, :], ACT.Silu).then_inc(out_read[0], 1)
                        me.slab += KT
                        high(4 * c + 6)
                        if c:
                            high_four(he_hi[:, c - 1, :])
                    high(28 + 7)
                    high_four(he_hi[:, FFE // NW - 1, :])
                    high(28 + 9)
                    b, _ = chunk(FFE // P)
                    act.activation(y_e[:, 0, :], b[:, :], ACT.Copy).then_inc(out_read[0], 1)
                    high(28 + 14)
                    for i in range(KT // 4):
                        high_four(xe_hi[:, i, :])
                    high(EXPERT_UNITS + LEAD)

            experts(2)
            with act.If(act.value_load(busiest[0:1, 0:1], min_val=0, max_val=S) > P):
                experts(3)
            me.enter(4, 0)
            root(TT)

        @block.vector
        def _(dve):
            me = Place(raised)

            def link(op):
                op.then_inc(*me.up(s.dve_step))
                dve.wait_ge(*me.next(s.dve_step))

            def low_part(body, step, k):
                step, k = unit_of(body, step, k)
                slot, high = units.slot(body, k), splits.slot(body, k)
                dve.tensor_tensor(w_lo[slot][:, :], raw[slot][:, :], w_hi[high][:, :].bitcast(F32), ALU.subtract)\
                    .then_inc(lo_made, 1)

            def low(until):
                lead = LEAD if me.body >= 2 else 0
                while me.unit < min(until, UNITS[me.body] + lead):
                    dve.wait_ge(*me.at(s.hi_made, me.unit + 1 - lead))
                    low_part(me.body, me.step, me.unit)
                    me.unit += 1

            def low_lead(k):
                dve.wait_ge(*me.at(s.hi_made, UNITS[1] + k + 1))
                low_part(2, 0, k)

            def tbank():
                b = bank[4 + tbanks.slot(me.body, me.group)]
                dve.wait_ge(t_full, tbanks.done(me.body, me.step, me.group))
                me.group += 1
                return b

            def low_t(hi, lo, kt, n, scale=None):
                for i in range(n):
                    b = tbank()
                    dve.wait_ge(*me.next(s.t_hi))
                    if scale is None:
                        op = dve.tensor_tensor(lo[:, kt + 2 * i:kt + 2 * i + 2, :].rearrange("p a b -> p (a b)"), b[:, :],
                                               hi[:, kt + 2 * i:kt + 2 * i + 2, :].rearrange("p a b -> p (a b)").bitcast(F32),
                                               ALU.subtract)
                    else:
                        for j in range(2):
                            o, k = scale + 2 * i + j, kt + 2 * i + j
                            src = pc1 if me.body == 0 else pc2
                            op = dve.scalar_tensor_tensor(out=lo[:, k, :], in0=b[:, j * S:(j + 1) * S],
                                                          scalar=src[:, o:o + 1], in1=hi[:, k, :].bitcast(F32),
                                                          op0=ALU.mult, op1=ALU.subtract)
                    op.then_inc(t_read, 1)

            def chunk(kts):
                me.slab += kts
                dve.wait_ge(w_used, splits.done(me.body, me.step, (me.slab - 1) // SLABS))
                pair = pairs.slot(me.body, me.chunk)
                me.chunk += 1
                return bank[2 * pair], bank[2 * pair + 1]

            def rsqrt(n, out=None):
                v, q = small[:, 0:n], small[:, 32:32 + n]
                r = small[:, 16:16 + n]
                dve.wait_ge(*me.next(s.rs_out))
                link(dve.reciprocal(r, r))
                link(dve.scalar_tensor_tensor(out=q, in0=r, scalar=-0.5, in1=r, op0=ALU.mult, op1=ALU.mult))
                link(dve.tensor_tensor(q, q, v, ALU.mult))
                last = dve.scalar_tensor_tensor(out=r if out is None else out, in0=q, scalar=1.5, in1=r, op0=ALU.add,
                                                op1=ALU.mult)
                if out is None:
                    link(last)
                    return r
                return last

            def rms(out, scratch):
                for tt in range(TT):
                    op = dve.scalar_tensor_tensor(out=scratch[:, tt, :], in0=x[:, tt, :], scalar=1.0, in1=x[:, tt, :],
                                                  op0=ALU.mult, op1=ALU.mult, accum_out=small[:, 32 + tt:33 + tt])
                link(op)
                dve.tensor_scalar(small[:, 0:TT], small[:, 32:32 + TT], 1.0 / D, EPS, ALU.mult, ALU.add)\
                    .then_inc(*me.up(s.rs_in))
                return rsqrt(TT, out)

            def head_means(squares, heads):
                link(dve.tensor_reduce(small[:, 32:32 + TT * heads], squares[:, :, :].rearrange("p t (h d) -> p (t h) d", h=heads),
                                       AX.X, ALU.add))
                dve.tensor_scalar(small[:, 0:TT * heads], small[:, 32:32 + TT * heads], 1.0 / P, EPS, ALU.mult, ALU.add)\
                    .then_inc(*me.up(s.rs_in))

            def half_stats(src, half):
                for tt in range(TT):
                    o = 120 + (tt * 2 + half) * 6
                    op = dve.bn_stats(small[:, o:o + 6], src[:, tt, half * 512:(half + 1) * 512])
                return op

            def layer_norm(src=x):
                if src is not x:
                    half_stats(src, 0)
                link(half_stats(src, 1))
                for tt in range(TT):
                    op = dve.bn_aggr(small[:, 144 + 2 * tt:146 + 2 * tt], small[:, 120 + tt * 12:132 + tt * 12])
                link(op)
                mv = small[:, 144:148].rearrange("p (t two) -> p t two", two=2)
                if me.body == 1:
                    dve.wait_ge(*me.next(s.gb_landed, 32))
                else:
                    dve.wait_ge(*me.at(s.gb_landed, 0))
                dve.tensor_scalar(small[:, 0:TT], mv[:, :, 1], 1.0, LN_EPS, ALU.mult, ALU.add).then_inc(*me.up(s.rs_in))

                def centre(half):
                    cols = slice(half * 512, half * 512 + 512)
                    for tt in range(TT):
                        op = dve.scalar_tensor_tensor(out=x[:, tt, cols], in0=src[:, tt, cols], scalar=mv[:, tt, 0:1],
                                                      in1=gb[:, 0, cols], op0=ALU.subtract, op1=ALU.mult)
                    link(op)

                centre(0)
                r = rsqrt(TT)
                for half in range(2):
                    cols = slice(half * 512, half * 512 + 512)
                    if half:
                        centre(1)
                    for tt in range(TT):
                        op = dve.scalar_tensor_tensor(out=x[:, tt, cols], in0=x[:, tt, cols], scalar=r[:, tt:tt + 1],
                                                      in1=gb[:, 1, cols], op0=ALU.mult, op1=ALU.add)
                    if me.body == 1:
                        op.then_inc(*me.up(s.rows_ready))
                return op

            def add_chunk(c, kts, factor=1.0):
                b = chunk(kts)
                cols = slice(c * NW, (c + 1) * NW)
                for tt in range(TT):
                    dve.scalar_tensor_tensor(out=x[:, tt, cols], in0=x[:, tt, cols], scalar=factor, in1=b[tt][:, :],
                                             op0=ALU.mult, op1=ALU.add).then_inc(out_read[tt], 1)

            def own_adds():
                for r in out_read:
                    dve.wait_ge(r, pairs.done(me.body, me.step, me.chunk - 1))

            def low_small():
                dve.wait_ge(*me.next(s.gw_high))
                dve.tensor_tensor(gw_lo[:, :], gw[:, :], gw_hi[:, :].bitcast(F32), ALU.subtract).then_inc(*me.up(s.gw_low))

            def mlstm_gates():
                dve.wait_ge(*me.next(s.small_turned))
                for d in range(2):
                    o = PC1["gate"] + d
                    dve.tensor_scalar(gi[:, d, :], bank[6][0:4, d * S:(d + 1) * S], pc1[0:4, o:o + 1], None, ALU.add)
                    op = dve.tensor_scalar(gz[:, d, :], bank[7][0:4, d * S:(d + 1) * S], pc1[0:4, o + 2:o + 3], None, ALU.add)
                link(op)
                dve.scalar_tensor_tensor(out=gabs[:, :, :], in0=gz[:, :, :], scalar=-1.0, in1=gz[:, :, :],
                                         op0=ALU.mult, op1=ALU.max).then_inc(*me.up(s.abs_made))
                dve.wait_ge(*me.next(s.softplus_made))
                link(dve.scalar_tensor_tensor(out=gz[:, :, :], in0=gz[:, :, :], scalar=0.0, in1=gabs[:, :, :],
                                              op0=ALU.min, op1=ALU.subtract))

                def both(out, a, b, first, op0, op1):
                    dve.tensor_tensor_scan(out[:, 0, :], a[:, 0, :], b[:, 0, :], first, op0, op1)
                    return dve.tensor_tensor_scan(out[:, 1, ::-1], a[:, 1, ::-1], b[:, 1, ::-1], first, op0, op1)

                one = ones[0:4, :].unsqueeze(1).to_broadcast([4, 2, S])
                link(both(gcum, one, gz, 0.0, ALU.mult, ALU.add))
                link(dve.tensor_tensor(ga[:, :, :], gi[:, :, :], gcum[:, :, :], ALU.subtract))
                link(both(gmax, ga, ga, -BIG, ALU.max, ALU.max))
                dve.tensor_tensor(gm[:, :, :], gcum[:, :, :], gmax[:, :, :], ALU.add).then_inc(*me.up(s.ag_made))

            def linear_gates():
                dve.wait_ge(*me.next(s.decay_full))
                for j in range(2):
                    o = PC2["ba"] + j
                    op = dve.tensor_scalar(z[:, j, :], bank[7][:, j * S:(j + 1) * S], pc2[:, o:o + 1], None, ALU.add)
                link(op)
                dve.scalar_tensor_tensor(out=az[:, :, :], in0=z[:, :, :], scalar=-1.0, in1=z[:, :, :],
                                         op0=ALU.mult, op1=ALU.max).then_inc(*me.up(s.abs_made))
                dve.wait_ge(*me.next(s.softplus_made))
                link(dve.scalar_tensor_tensor(out=z[:, :, :], in0=z[:, :, :], scalar=0.0, in1=az[:, :, :],
                                              op0=ALU.min, op1=ALU.subtract))
                flat = lambda buf: buf[:, :, :].rearrange("p a b -> p (a b)")
                link(dve.tensor_tensor_scan(flat(bcum), cst("reset"), flat(z), 0.0, ALU.mult, ALU.add))
                chunks = flat(bcum).rearrange("p (n c) -> p n c", c=64)
                dve.tensor_tensor(flat(bd).rearrange("p (n c) -> p n c", c=64), chunks[:, :, 63:64].to_broadcast([P, 8, 64]),
                                  chunks, ALU.subtract).then_inc(*me.up(s.decays))

            def linear_operands():
                dve.wait_ge(*me.next(s.decay_exp))
                dve.wait_ge(*me.next(s.zeros2))
                b = tbank()
                dve.scalar_tensor_tensor(out=qd[:, :, :].rearrange("p a b -> p (a b)"), in0=b[:, :], scalar=64 ** -0.5,
                                         in1=eb[:, :, :].rearrange("p a b -> p (a b)"), op0=ALU.mult, op1=ALU.mult)\
                    .then_inc(t_read, 1)
                b = tbank()
                for j in range(2):
                    for e in range(2):
                        half = slice(64 * e, 64 * e + 64)
                        dve.tensor_tensor(kiz[half, 2 * j + e, :], b[half, j * S:(j + 1) * S], ei[half, j, :], ALU.mult)
                dve.tensor_tensor(kd[:, :, :].rearrange("p a b -> p (a b)"), b[:, :],
                                  ed[:, :, :].rearrange("p a b -> p (a b)"), ALU.mult).then_inc(t_read, 1)
                dve.wait_ge(t_read, tbanks.done(1, 0, me.group - 1))
                for par in range(2):
                    split = lambda buf: buf.rearrange("p b (t q c) -> p (b t) q c", t=TT, q=2)[:, :, par, :]
                    dve.tensor_copy(split(qz[:, par, :, :]), split(qd[:, :, :]))
                for r in out_read:
                    dve.wait_ge(r, pairs.done(1, 0, me.chunk - 2))
                for par in range(2):
                    half = slice(64 * par, 64 * par + 64)
                    op = dve.tensor_copy(vz[half, par, :, :], v2[half, :, :])
                op.then_inc(*me.up(s.operands_made))

            def causal_scores():
                dve.wait_ge(*me.next(s.kd_turned))
                dve.tensor_copy(kdt[:, :, :].rearrange("p a b -> p (a b)"), bank[6][:, :]).then_inc(*me.up(s.kdt_made))
                dve.wait_ge(*me.next(s.sc_full))
                mask = cst("causal").bitcast(U32).unsqueeze(1).to_broadcast([P, GH, P])
                for tt in range(TT):
                    op = dve.copy_predicated(sc[:, tt, :, :], mask, bank[4 + tt][:, :].rearrange("p (h i) -> p h i", h=GH))
                op.then_inc(*me.up(s.sc_made))

            def states():
                dve.wait_ge(*me.next(s.updates_full))
                for c, b in enumerate((bank[6], bank[7], bank[4])):
                    for h in range(GH):
                        half = slice(64 * (h % 2), 64 * (h % 2) + 64)
                        update = b[half, (h // 2) * 256 + (h % 2) * P:(h // 2) * 256 + (h % 2) * P + P]
                        if c == 0:
                            op = dve.tensor_copy(sz[half, 0, h, :], update)
                        else:
                            last = c * 64 + 63
                            op = dve.scalar_tensor_tensor(out=sz[half, c, h, :], in0=sz[half, c - 1, h, :],
                                                          scalar=eb[half, h // 2, last:last + 1], in1=update,
                                                          op0=ALU.mult, op1=ALU.add)
                    if c < 2:
                        link(op)
                    else:
                        op.then_inc(*me.up(s.states_made))

            def spatial_norm():
                for r in out_read:
                    dve.wait_ge(r, pairs.done(1, 0, me.chunk - 2))
                for i in range(TT * GH):
                    tt, h = divmod(i, GH)
                    op = dve.bn_stats(small[:, 112 + 6 * i:118 + 6 * i], gv[:, tt, h * P:(h + 1) * P])
                link(op)
                for i in range(TT * GH):
                    op = dve.bn_aggr(small[:, 96 + 2 * i:98 + 2 * i], small[:, 112 + 6 * i:118 + 6 * i])
                link(op)
                mv = small[:, 96:112].rearrange("p (n two) -> p n two", two=2)
                dve.tensor_scalar(small[:, 0:8], mv[:, :, 1], 1.0, LN_EPS, ALU.mult, ALU.add).then_inc(*me.up(s.rs_in))
                r = rsqrt(8)
                for i in range(TT * GH):
                    tt, h = divmod(i, GH)
                    cols = slice(h * P, (h + 1) * P)
                    op = dve.tensor_scalar(vn[:, tt, cols], gv[:, tt, cols], mv[:, i, 0:1], r[:, i:i + 1],
                                           ALU.subtract, ALU.mult)
                link(op)
                for i, f in ((0, ALU.mult), (1, ALU.add)):
                    for tt in range(TT):
                        op = dve.tensor_tensor(vn[:, tt, :], vn[:, tt, :], ln_gb[:, i, :], f)
                    if i == 0:
                        link(op)
                op.then_inc(*me.up(s.vn_made))

            def low_four(hi, lo):
                b = tbank()
                dve.wait_ge(*me.next(s.t_hi))
                dve.tensor_tensor(lo, b[:, :], hi.bitcast(F32), ALU.subtract).then_inc(t_read, 1)

            def select(n):
                for tt in range(TT):
                    op = dve.tensor_scalar(sel[:, tt, :], iota1[:, :], place[:, tt, bass.ds(n, 1)], None, ALU.is_equal)
                op.then_inc(*me.up(s.sel_made))

            def route():
                dve.wait_ge(s.rw_high.sem, 1)
                dve.tensor_tensor(rw_lo[:, :], rw[:, :], rw_hi[:, :].bitcast(F32), ALU.subtract).then_inc(s.rw_low.sem, 1)
                dve.wait_ge(*me.next(s.logits_full))
                dve.tensor_copy(logits_t[:, :], bank[6][0:NE, 0:S]).then_inc(*me.up(s.logits_copied))
                dve.wait_ge(*me.next(s.logits_by_token))
                logits, top = small[:, 64:80], small[:, 80:96]
                index = small[:, 96:112].bitcast(U32)
                link(dve.tensor_copy(logits, bank[7][:, 0:TT * NE]))
                for tt in range(TT):
                    part = slice(tt * NE, (tt + 1) * NE)
                    link(dve.max(top[:, part], logits[:, part]))
                    link(dve.max_index(index[:, part], top[:, part], logits[:, part]))
                tops = top.rearrange("p (t n) -> p t n", n=NE)
                link(dve.tensor_copy(small[:, 112:128], index))
                dve.tensor_tensor(small[:, 48:50], tops[:, :, 1], tops[:, :, 0], ALU.subtract).then_inc(*me.up(s.top_made))
                for tt in range(TT):
                    op = dve.tensor_scalar(mask[:, tt, :], cst("iota"), small[:, 112 + tt * NE:113 + tt * NE], None, ALU.is_equal)
                link(op)
                for tt in range(TT):
                    op = dve.scalar_tensor_tensor(out=mask[:, tt, :], in0=cst("iota"), scalar=small[:, 113 + tt * NE:114 + tt * NE],
                                                  in1=mask[:, tt, :], op0=ALU.is_equal, op1=ALU.add)
                dve.tensor_tensor_scan(iota1[:, :], ones[:, 0:P], ones[:, 0:P], 0.0, ALU.mult, ALU.add)
                dve.scalar_tensor_tensor(out=upto[:, :], in0=cst("dmask")[:, P:2 * P], scalar=1.0, in1=ident,
                                         op0=ALU.min, op1=ALU.add).then_inc(*me.up(s.mask_made))
                dve.wait_ge(*me.next(s.top_exp))
                link(dve.tensor_scalar(small[:, 50:52], small[:, 48:50], 1.0, None, ALU.add))
                link(dve.reciprocal(small[:, 52:54], small[:, 50:52]))
                link(dve.tensor_tensor(small[:, 54:56], small[:, 52:54], small[:, 48:50], ALU.mult))
                for tt in range(TT):
                    o = 112 + tt * NE
                    dve.tensor_scalar(gates[:, tt, :], cst("iota"), small[:, o:o + 1], small[:, 52 + tt:53 + tt],
                                      ALU.is_equal, ALU.mult)
                    op = dve.tensor_scalar(small[:, 128 + tt * NE:136 + tt * NE], cst("iota"), small[:, o + 1:o + 2],
                                           small[:, 54 + tt:55 + tt], ALU.is_equal, ALU.mult)
                link(op)
                dve.tensor_tensor(gates[:, :, :].rearrange("p t n -> p (t n)"), gates[:, :, :].rearrange("p t n -> p (t n)"),
                                  small[:, 128:144], ALU.add)
                for tt in range(TT):
                    dve.tensor_scalar(acc[:, tt, :], x[:, tt, :], ALPHA, None, ALU.mult).then_inc(*me.up(s.acc_added))
                dve.wait_ge(*me.next(s.counted))
                for tt in range(TT):
                    dve.tensor_tensor(place[:, tt, 0:NE], bank[7][:, tt * NE:(tt + 1) * NE], mask[:, tt, :], ALU.mult)
                link(dve.tensor_reduce(load_max[:, 0:1], bank[7][:, TT * NE:(TT + 1) * NE], AX.X, ALU.max))
                dve.tensor_copy(busiest[0:1, 0:1], load_max[0:1, 0:1]).then_inc(s.busiest_known.sem, 1)
                for tt in range(TT):
                    op = dve.tensor_scalar(place[:, tt, NE:2 * NE], place[:, tt, 0:NE], -float(P), None, ALU.add)
                    op = dve.memset(place[:, tt, 2 * NE:2 * NE + 1], 0.0)
                link(op)
                select(0)
                for i in range(KT // 4):
                    low_lead(i)
                    low_four(xe_hi[:, i, :], xe_lo[:, i, :])

            dve.sem_inc(lo_made, spare)
            for r in out_read:
                dve.sem_inc(r, 2)
            dve.sem_inc(t_read, 2)
            dve.wait_ge(x_landed, 32)
            dve.wait_ge(s.ones_set.sem, 1)

            with dve.Fori(0, DEPTH) as layer:
                me.enter(0, layer)
                low(1)
                low_t(x_hi, x_lo, 0, 4, PC1["norm1"])
                low_small()
                low(2)
                rms(r1, y).then_inc(*me.up(s.r_made))
                dve.wait_ge(*me.at(s.r_made, 1))
                for c, dst in enumerate((qk[:, 1, 0:512], qk[:, 1, 512:1024], v[:, 1, :, 0:MD], aqk[:, 1, 0:512],
                                         aqk[:, 1, 512:1024], av[:, 1, :, 0:AD], mo[:, 1, :])):
                    low(2 * c + 4)
                    if c == 0:
                        dve.wait_ge(*me.next(s.small_full))
                        dve.tensor_copy(g16t[:, :], bank[6][0:16, 0:S]).then_inc(*me.up(s.small_copied))
                    if c == 1:
                        dve.wait_ge(*me.next(s.small_by_token))
                        for tt in range(TT):
                            op = dve.tensor_scalar(g16[:, tt, :], bank[7][:, tt * 16:(tt + 1) * 16], r1[:, tt:tt + 1], None,
                                                   ALU.mult)
                        op.then_inc(*me.up(s.g16_made))
                    if c == 6:
                        dve.wait_ge(*me.next(s.kz_zero))
                        for i in range(4):
                            b = tbank()
                            if i < 2:
                                op = dve.tensor_copy(aq_t[:, 2 * i:2 * i + 2, :].rearrange("p a b -> p (a b)"), b[:, :])
                            else:
                                for j in range(2):
                                    for e in range(2):
                                        rows_ = slice(64 * e, 64 * e + 64)
                                        op = dve.tensor_copy(kz[rows_, 2 * (2 * (i - 2) + j) + e, :], b[rows_, j * S:(j + 1) * S])
                            op.then_inc(t_read, 1)
                    _, b = chunk(KT)
                    if c == 6:
                        continue
                    src = b[:, :] if c not in (2, 5) else b[:, :].rearrange("p (h d) -> p h d", d=MD if c == 2 else AD)
                    if c == 5:
                        dve.wait_ge(*me.at(s.pads, 1))
                    dve.tensor_scalar(dst, src, r1[:, 1:2], None, ALU.mult).then_inc(out_read[1], 1)
                    if c == 1:
                        mlstm_gates()
                    if c == 3:
                        dve.wait_ge(*me.next(s.am_full))
                        dve.tensor_copy(small[:, 64:96], bank[7][:, 0:32]).then_inc(*me.up(s.am_made))
                    if c == 2:
                        dve.wait_ge(*me.at(s.pads, 1))
                        for i in range(4):
                            b = tbank()
                            dve.tensor_copy(ct[:, 2 * i:2 * i + 2, 2:S + 2], b[:, :].rearrange("p (a b) -> p a b", a=2))\
                                .then_inc(t_read, 1)
                    if c in (3, 4):
                        low(2 * c + 6)
                        dve.wait_ge(t_read, tbanks.done(0, layer, 7))
                        for j in range(CW):
                            for blk in range(4 * (c - 3), 4 * (c - 3) + 4):
                                w = pc1[:, PC1["conv"] + blk * CW + j:PC1["conv"] + blk * CW + j + 1]
                                if j == 0:
                                    op = dve.tensor_scalar(conv[:, blk, :], ct[:, blk, 0:S], w, None, ALU.mult)
                                else:
                                    op = dve.scalar_tensor_tensor(out=conv[:, blk, :], in0=ct[:, blk, j:j + S], scalar=w,
                                                                  in1=conv[:, blk, :], op0=ALU.mult, op1=ALU.add)
                            if j < CW - 1 or c == 3:
                                link(op)
                            else:
                                op.then_inc(*me.up(s.conv_made))
                low(14 + 3)
                for n in range(2 * MH):
                    h, d = divmod(n, 2)
                    if d == 0:
                        dve.wait_ge(*me.next(s.st_full))
                    dve.wait_ge(*me.next(s.w_exp))
                    if n >= 2:
                        dve.wait_ge(*me.at(s.pv_done, n - 1))
                    for region, (lo, hi) in enumerate(((0, 256), (256, 384))):
                        st = region if d == 0 else 1 - region
                        t0 = 0 if region == 0 else P * (1 - d)
                        op = dve.scalar_tensor_tensor(out=pt[:, n % 2, lo:hi],
                                                      in0=bank[6 - 2 * (h % 2)][:, st * S + t0:st * S + t0 + hi - lo],
                                                      scalar=MD ** -0.5, in1=wexp[n][:, lo:hi],
                                                      op0=ALU.mult, op1=ALU.mult)
                    op.then_inc(*me.up(s.pt_made))
                dve.wait_ge(*me.at(s.pv_done, 2 * MH))
                dve.wait_ge(*me.next(s.em_made))
                den = small[:, 0:16]
                for d in range(2):
                    for tt in range(TT):
                        o = tt * 8 + d * 4
                        heads = bank[2 * d + tt][:, 0:3 * (MD + 1)].rearrange("p (h c) -> p h c", h=3)
                        dve.tensor_copy(small[:, o:o + 3], heads[:, :, MD])
                        op = dve.tensor_copy(small[:, o + 3:o + 4], mixed(d, tt, 3)[:, MD:MD + 1])
                link(op)
                link(dve.scalar_tensor_tensor(out=den, in0=den, scalar=-1.0, in1=den, op0=ALU.mult, op1=ALU.max))
                em = small[:, 96:112].rearrange("p (d t h) -> p t d h", d=2, t=TT)
                link(dve.tensor_tensor(den.rearrange("p (t d h) -> p t d h", t=TT, d=2), den.rearrange("p (t d h) -> p t d h", t=TT, d=2),
                                       em, ALU.max))
                link(dve.reciprocal(small[:, 16:32], den))
                for d in range(2):
                    for tt in range(TT):
                        rd, out = small[:, 16 + tt * 8 + d * 4:20 + tt * 8 + d * 4], (hm, sq)[d]
                        heads = bank[2 * d + tt][:, 0:3 * (MD + 1)].rearrange("p (h c) -> p h c", h=3)
                        dve.tensor_tensor(out[:, tt, 0:3 * MD].rearrange("p (h c) -> p h c", h=3), heads[:, :, 0:MD],
                                          rd[:, 0:3].unsqueeze(2).to_broadcast([P, 3, MD]), ALU.mult)
                        op = dve.tensor_scalar(out[:, tt, 3 * MD:], mixed(d, tt, 3)[:, 0:MD], rd[:, 3:4], None, ALU.mult)
                op.then_inc(*me.up(s.num_read))
                dve.wait_ge(*me.at(s.num_read, 1))

                def hm_sum():
                    for tt in range(TT):
                        op = dve.tensor_tensor(hm[:, tt, :], hm[:, tt, :], sq[:, tt, :], ALU.add)
                    link(op)

                def hm_squares():
                    for tt in range(TT):
                        op = dve.tensor_tensor(sq[:, tt, :], hm[:, tt, :], hm[:, tt, :], ALU.mult)
                    link(op)

                def hm_means():
                    head_means(sq, MH)

                def hm_norm():
                    r = rsqrt(TT * MH)
                    for tt in range(TT):
                        rd = r[:, tt * MH:(tt + 1) * MH].unsqueeze(2).to_broadcast([P, MH, MD])
                        op = dve.tensor_tensor(hm[:, tt, :].rearrange("p (h c) -> p h c", h=MH),
                                               hm[:, tt, :].rearrange("p (h c) -> p h c", h=MH), rd, ALU.mult)
                    link(op)

                def hm_gate():
                    for r in out_read:
                        dve.wait_ge(r, pairs.done(0, layer, 6))
                    for tt in range(TT):
                        op = dve.tensor_tensor(y[:, tt, 0:512], hm[:, tt, :], mo[:, tt, :], ALU.mult)
                    op.then_inc(*me.up(s.rows_ready))

                def turned(h):
                    dve.wait_ge(*me.at(s.p_turned, h + 1))
                    if h >= 2:
                        dve.wait_ge(*me.at(s.apv_done, h - 1))
                    dve.tensor_copy(pts[:, h % 2, :, :].rearrange("p a b -> p (a b)"), bank[6 + h % 2][:, :])\
                        .then_inc(*me.up(s.pts_made))

                def normalise(half):
                    dve.wait_ge(*me.at(s.apv_done, 4 * half + 4))
                    for tt in range(TT):
                        o = bank[2 * (1 - half) + tt][:, 0:4 * (AD + 1)].rearrange("p (h c) -> p h c", h=4)
                        rr = small[:, 16 + 4 * tt:20 + 4 * tt]
                        link(dve.reciprocal(rr, o[:, :, AD]))
                        op = dve.tensor_tensor(y[:, tt, 512 + half * 256:768 + half * 256].rearrange("p (h c) -> p h c", h=4),
                                               o[:, :, 0:AD], rr.unsqueeze(2).to_broadcast([P, 4, AD]), ALU.mult)
                    return op

                for h in range(AH):
                    dve.wait_ge(*me.next(s.as_full))
                    o = 116 + 2 * (h % 2)
                    if h >= 2:
                        dve.wait_ge(*me.at(s.att_exp, h - 1))
                    link(dve.tensor_reduce(small[:, o:o + 2], bank[4 + h % 2][:, :].rearrange("p (t k) -> p t k", t=TT),
                                           AX.X, ALU.max))
                    dve.tensor_scalar(small[:, o - 4:o - 2], small[:, o:o + 2], -AD ** -0.5, None, ALU.mult)\
                        .then_inc(*me.up(s.amax_made))
                    if h:
                        turned(h - 1)
                    if h < 5:
                        (hm_sum, hm_squares, hm_means, hm_norm, hm_gate)[h]()
                    if h == 5:
                        link(normalise(0))
                turned(AH - 1)
                normalise(1).then_inc(*me.up(s.rows_ready))
                low_t(x_hi, x_lo, 0, 4, PC1["gout"])
                for c in range(2):
                    low(14 + 2 * c + 4)
                    add_chunk(c, KT)
                low_t(x_hi, x_lo, 0, 4, PC1["norm2"])
                own_adds()
                rms(r2, y).then_inc(*me.up(s.r_made))
                dve.wait_ge(*me.at(s.r_made, 2))
                for c in range(FF1 // NW):
                    low(18 + 2 * c + 4)
                    b = chunk(KT)
                    for tt in range(TT):
                        dve.wait_ge(*me.next(s.relu_made))
                        dve.scalar_tensor_tensor(out=hid[c % 2][:, tt, :], in0=b[tt][:, :], scalar=r2[:, tt:tt + 1],
                                                 in1=sg[:, tt, :], op0=ALU.mult, op1=ALU.mult)\
                            .then_inc(out_read[tt], 1)
                    if c:
                        low_t(h_hi, h_lo, 4 * (c - 1), 2)
                low(34 + 6)
                low_t(h_hi, h_lo, FF1 // P - 4, 2)
                for c in range(2):
                    low(34 + 8 * c + 8 + 2)
                    add_chunk(c, FF1 // P)
                own_adds()

            me.enter(1, 0)
            link(rms(r1, xn))
            dve.wait_ge(*me.next(s.gb_landed, 16))
            for half in range(2):
                for tt in range(TT):
                    cols = slice(half * 512, half * 512 + 512)
                    op = dve.scalar_tensor_tensor(out=x[:, tt, cols], in0=x[:, tt, cols], scalar=r1[:, tt:tt + 1],
                                                  in1=gb[:, 0, cols], op0=ALU.mult, op1=ALU.mult)
                op.then_inc(*me.up(s.rows_ready))
            for layer in range(DEPTH):
                u0 = (0, 47)[layer]
                low(u0 + 1)
                low_t(x_hi, x_lo, 0, 4)
                low_small()
                for c in range(5):
                    low(u0 + 2 * c + 4)
                    if c == 0:
                        dve.wait_ge(*me.next(s.small_full))
                        dve.tensor_copy(al[:, :], bank[6][0:16, 0:S]).then_inc(*me.up(s.al_made))
                    _, b = chunk(KT)
                    if c < 2:
                        dve.tensor_copy((qk2, v2)[c][:, 1, :], b[:, :]).then_inc(out_read[1], 1)
                    if c == 1:
                        linear_gates()
                    if c == 2:
                        linear_operands()
                    if c == 3:
                        causal_scores()
                        spatial_norm()
                states()
                dve.wait_ge(*me.next(s.spatial_full))
                for tt in range(TT):
                    for h in range(GH):
                        cols = slice(h * P, (h + 1) * P)
                        op = dve.scalar_tensor_tensor(out=y[:, tt, cols], in0=bank[tt][:, cols],
                                                      scalar=pc2[:, PC2["bs"] + h:PC2["bs"] + h + 1], in1=gu[:, tt, cols],
                                                      op0=ALU.add, op1=ALU.mult)
                op.then_inc(*me.up(s.rows_ready))
                dve.wait_ge(*me.next(s.lin_full))
                for tt in range(TT):
                    op = dve.tensor_copy(os_[:, tt, :], bank[2 + tt][:, :])
                link(op)
                for tt in range(TT):
                    op = dve.tensor_tensor(sq2[:, tt, :], os_[:, tt, :], os_[:, tt, :], ALU.mult)
                link(op)
                head_means(sq2, GH)
                low_t(x_hi, x_lo, 0, 2, PC2["gout"])
                r = rsqrt(TT * GH)
                for tt in range(TT):
                    rd = r[:, tt * GH:(tt + 1) * GH].unsqueeze(2).to_broadcast([P, GH, P])
                    op = dve.tensor_tensor(os_[:, tt, :].rearrange("p (h c) -> p h c", h=GH),
                                           os_[:, tt, :].rearrange("p (h c) -> p h c", h=GH), rd, ALU.mult)
                link(op)
                for tt in range(TT):
                    op = dve.tensor_tensor(y[:, tt, 512:1024], os_[:, tt, :], sg2[:, tt, :], ALU.mult)
                op.then_inc(*me.up(s.rows_ready))
                low_t(x_hi, x_lo, 4, 2, PC2["gout"] + 4)
                for c in range(2):
                    low(u0 + 10 + 2 * c + 4)
                    add_chunk(c, KT, ALPHA)
                    if c == 0:
                        own_adds()
                        half_stats(x, 0)
                own_adds()
                layer_norm()
                low_t(x_hi, x_lo, 0, 4)
                if layer == 0:
                    u0 += 14
                    for c in range(6):
                        wide = NW if c < 5 else 256
                        if c < 5:
                            low(u0 + 4 * c + 4)
                            chunk(KT)
                            low(u0 + 4 * c + 6)
                            b = chunk(KT)
                            up0 = 0
                        else:
                            low(u0 + 24)
                            b = chunk(KT)
                            up0 = 256
                        for tt in range(TT):
                            if c < 5:
                                dve.wait_ge(out_read[tt], pairs.done(1, 0, me.chunk - 2))
                            else:
                                dve.wait_ge(*me.next(s.silu_gate))
                            dve.tensor_tensor(hid[c % 2][:, tt, 0:wide], b[tt][:, up0:up0 + wide], sg[:, tt, 0:wide],
                                              ALU.mult).then_inc(out_read[tt], 1)
                        if c:
                            low_t(h_hi, h_lo, 4 * (c - 1), 2)
                    low(u0 + 22 + 4)
                    low_t(h_hi, h_lo, 20, 1)
                    for c in range(2):
                        low(u0 + 22 + (8, 13)[c])
                        add_chunk(c, FF2 // P, ALPHA)
                        if c == 0:
                            own_adds()
                            half_stats(x, 0)
                    own_adds()
                    layer_norm()
                else:
                    route()

            def experts(body, first):
                with dve.Fori(0, NE) as step:
                    me.enter(body, step)
                    me.unit = LEAD
                    b = tbank()
                    dve.tensor_copy(sel_t[:, :, :].rearrange("p a b -> p (a b)"), b[:, 0:TT * P]).then_inc(t_read, 1)
                    for c in range(FFE // NW):
                        low(4 * c + 6)
                        _, b = chunk(2 * KT)
                        dve.wait_ge(out_read[0], pairs.done(body, step, c))
                        dve.tensor_tensor(hid[c % 2][:, 0, :], b[:, :], sg_e[:, :], ALU.mult).then_inc(out_read[1], 1)
                        if c:
                            low_four(he_hi[:, c - 1, :], he_lo[:, c - 1, :])
                    low(28 + 7)
                    low_four(he_hi[:, FFE // NW - 1, :], he_lo[:, FFE // NW - 1, :])
                    select(first + step + 1)
                    low(28 + 9)

                    def add(half):
                        cols = slice(half * NW, (half + 1) * NW)
                        for tt in range(TT):
                            dve.wait_ge(*me.next(s.scattered))
                            dve.scalar_tensor_tensor(out=acc[:, tt, cols], in0=bank[6 + tt][:, :],
                                                     scalar=gates[:, tt, bass.ds(step, 1)], in1=acc[:, tt, cols],
                                                     op0=ALU.mult, op1=ALU.add).then_inc(*me.up(s.acc_added))

                    low(28 + 12)
                    add(0)
                    low(28 + 14)
                    for i in range(KT // 4):
                        low_four(xe_hi[:, i, :], xe_lo[:, i, :])
                    low(EXPERT_UNITS + 1)
                    _, b = chunk(FFE // P * 2)
                    dve.tensor_copy(y_e[:, 1, :], b[:, :]).then_inc(out_read[1], 1)
                    low(EXPERT_UNITS + 2)
                    add(1)
                    dve.wait_ge(*me.at(s.acc_added, 2 * TT))

            experts(2, 0)
            with dve.If(dve.value_load(busiest[0:1, 0:1], min_val=0, max_val=S) > P):
                experts(3, NE)
            me.enter(4, 0)
            layer_norm(acc).then_inc(s.x_final.sem, 1)

        @block.tensor
        def _(pe):
            me = Place(raised)

            def product(hi, lo, kts, chunks, group=None, per_chunk=None, before={}):
                for c in range(chunks):
                    pair = pairs.slot(me.body, me.chunk)
                    for r in out_read:
                        pe.wait_ge(r, pairs.free(me.body, me.step, me.chunk))
                    me.chunk += 1
                    for kt in range(kts):
                        if (c, kt) in before:
                            before[c, kt]()
                        if group is not None and c == 0 and kt % 2 == 0:
                            pe.wait_ge(t_read, tbanks.done(me.body, me.step, group + kt // 2))
                        k, j = divmod(me.slab, SLABS)
                        high, low = splits.slot(me.body, k), units.slot(me.body, k)
                        if j == 0:
                            pe.wait_ge(lo_made, units.done(me.body, me.step, k))
                        for tt in range(TT):
                            out = bank[2 * pair + tt][:, :]
                            rows = slice(tt * P, (tt + 1) * P)
                            cols = slice(j * NW, (j + 1) * NW)
                            pe.matmul(out, hi[:, kt, rows], w_hi[high][:, cols], start=kt == 0, stop=False)
                            pe.matmul(out, lo[:, kt, rows], w_hi[high][:, cols], start=False, stop=False)
                            mm = pe.matmul(out, hi[:, kt, rows], w_lo[low][:, cols], start=False, stop=kt == kts - 1)
                        if j == SLABS - 1:
                            mm.then_inc(w_used, 1)
                        me.slab += 1
                    if per_chunk is not None:
                        per_chunk(c)

            def turn(src, n):
                for i in range(n):
                    slot = tbanks.slot(me.body, me.group)
                    pe.wait_ge(t_read, tbanks.free(me.body, me.step, me.group))
                    me.group += 1
                    for j in range(2):
                        for tt in range(TT):
                            o = j * S + tt * P
                            op = pe.transpose(bank[4 + slot][:, o:o + P], src(2 * i + j, tt), ident)
                    op.then_inc(t_full, 1)

            def turn_four(src):
                b = bank[4 + tbanks.slot(me.body, me.group)]
                pe.wait_ge(t_read, tbanks.free(me.body, me.step, me.group))
                me.group += 1
                for j in range(4):
                    op = pe.transpose(b[:, j * P:(j + 1) * P], src(j), ident)
                op.then_inc(t_full, 1)

            def gather():
                pe.wait_ge(*me.next(s.sel_made))
                for i in range(KT // 4):
                    b = bank[4 + tbanks.slot(me.body, me.group)]
                    pe.wait_ge(t_read, tbanks.free(me.body, me.step, me.group))
                    me.group += 1
                    for j in range(4):
                        cols = slice((4 * i + j) * P, (4 * i + j + 1) * P)
                        for tt in range(TT):
                            op = pe.matmul(b[:, j * P:(j + 1) * P], x[:, tt, cols], sel[:, tt, :],
                                           start=tt == 0, stop=tt == TT - 1)
                    op.then_inc(t_full, 1)

            def rows_of(buf, start=0):
                return lambda blk, tt: buf[:, tt, start + blk * P:start + (blk + 1) * P]

            def small_product(w_h, w_l, n, b, group):
                for kt in range(KT):
                    if kt % 2 == 0:
                        pe.wait_ge(t_read, tbanks.done(me.body, me.step, group + kt // 2))
                    cols = slice(kt * n, (kt + 1) * n)
                    out = b[0:n, 0:S]
                    pe.matmul(out, w_h[:, cols], x_hi[:, kt, :], start=kt == 0, stop=False)
                    pe.matmul(out, w_h[:, cols], x_lo[:, kt, :], start=False, stop=False)
                    op = pe.matmul(out, w_l[:, cols], x_hi[:, kt, :], start=False, stop=kt == KT - 1)
                return op

            def small_gates(group):
                pe.wait_ge(*me.next(s.gw_low))
                small_product(gw_hi, gw_lo, 16, bank[6], group).then_inc(*me.up(s.small_full))

            def turn_rows(src, half_ready):
                def half(n):
                    half_ready(n)
                    turn(rows_of(src, n * 512), 2)

                half(0)
                return {(0, 1): lambda: half(1)}

            def normalised(half):
                pe.wait_ge(*me.next(s.rows_ready))

            def added(chunk):
                def wait(half):
                    for r in out_read:
                        pe.wait_ge(r, pairs.done(me.body, me.step, chunk + half))
                return wait

            def chunk_read(k):
                for r in out_read:
                    pe.wait_ge(r, pairs.done(me.body, me.step, k))

            pe.sem_inc(w_used, spare)
            pe.sem_inc(t_full, 2)
            pe.wait_ge(x_landed, 32)

            def weights(n):
                h, d = divmod(n, 2)
                b = bank[4 + n % 2]
                if n in (0, 1, 6, 7):
                    pe.wait_ge(t_read, tbanks.done(me.body, me.step, 6 + n if n < 2 else 4 + n))
                else:
                    pe.wait_ge(*me.at(s.w_exp, n - 1))
                sel = cst("sel", 4)[:, h * P:(h + 1) * P]
                mask = cst("dmask")[:, d * P:(d + 1) * P]
                pe.matmul(b[:, 0:S], sel, gmax[:, d, :], start=True, stop=False)
                o = d * P
                pe.matmul(b[:, o:o + P], ident, mask, start=False, stop=True)
                q0 = P * (1 - d)
                pe.matmul(b[:, S:S + P], sel, gmax[:, d, q0:q0 + P], start=True, stop=False)
                pe.matmul(b[:, S:S + P], ident, mask, start=False, stop=True).then_inc(*me.up(s.w_full))

            def turn_heads():
                pe.wait_ge(*me.at(s.w_exp, 6))
                pe.wait_ge(*me.at(s.rotated, 1))
                turn(rows_of(art), 4)

            def after_w_in(c):
                if c == 0:
                    pe.wait_ge(*me.next(s.small_copied))
                    for tt in range(TT):
                        op = pe.matmul(bank[7][:, tt * 16:(tt + 1) * 16], g16t[:, tt * P:(tt + 1) * P], ident[0:16, 0:16],
                                       start=True, stop=True)
                    op.then_inc(*me.up(s.small_by_token))
                if c == 1:
                    pe.wait_ge(*me.next(s.g16_made))
                    for i in range(4):
                        for tt in range(TT):
                            o = (i % 2) * S + tt * P
                            op = pe.transpose(bank[6 + i // 2][0:4, o:o + P], g16[:, tt, 4 * i:4 * i + 4], ident)
                    op.then_inc(*me.up(s.small_turned))
                if c == 3:
                    pe.wait_ge(*me.next(s.ag_made))
                    for i, src in enumerate((ga, gm)):
                        for d in range(2):
                            for tt in range(TT):
                                o = i * 16 + d * 8 + tt * 4
                                op = pe.matmul(bank[7][:, o:o + 4], src[0:4, d, tt * P:(tt + 1) * P], ident[0:4, 0:4],
                                               start=True, stop=True)
                    op.then_inc(*me.up(s.am_full))
                if c == 2:
                    chunk_read(1)
                    turn(rows_of(qk), 2)
                if c >= 3:
                    if c == 3:
                        pe.wait_ge(const_landed, 32)
                    weights(2 * (c - 3))
                    weights(2 * (c - 3) + 1)

            with pe.Fori(0, DEPTH) as layer:
                me.enter(0, layer)
                before = turn_rows(x, added(-2))
                before[0, 6] = lambda: small_gates(0)
                before[3, 2] = lambda: turn(rows_of(qk, 512), 2)
                before[6, 4] = turn_heads
                product(x_hi, x_lo, KT, 7, 0, after_w_in, before)
                def scores(h):
                    if h >= 2:
                        pe.wait_ge(*me.at(s.pt_made, 2 * h - 2))
                    elif h == 1:
                        pe.wait_ge(*me.at(s.w_exp, 2 * MH - 1))
                    for st in range(TT):
                        op = pe.matmul(bank[6 - 2 * (h % 2)][:, st * S:(st + 1) * S], conv[:, 4 + h, st * P:(st + 1) * P], conv[:, h, :],
                                       start=True, stop=True)
                    op.then_inc(*me.up(s.st_full))

                def mix(n):
                    h, d = divmod(n, 2)
                    pe.wait_ge(*me.at(s.pt_made, n + 1))
                    for tt in range(TT):
                        first = [(d, tt * P)]
                        if tt == 1 - d:
                            first.append((1 - d, S))
                        for i, (st, o) in enumerate(first):
                            op = pe.matmul(mixed(d, tt, h), pt[:, n % 2, o:o + P], v[:, st, h, :],
                                           start=i == 0, stop=i == len(first) - 1)
                    op.then_inc(*me.up(s.pv_done))

                pe.wait_ge(*me.next(s.silu_made))
                chunk_read(6)
                scores(0)
                scores(1)
                for n in range(2 * MH):
                    mix(n)
                    if n % 2 and n // 2 + 2 < MH:
                        scores(n // 2 + 2)

                def logits(h):
                    if h >= 2:
                        pe.wait_ge(*me.at(s.att_exp, h - 1))
                    else:
                        pe.wait_ge(*me.at(*((s.pt_made, 2 * MH), (s.num_read, 1))[h]))
                    b = bank[4 + h % 2]
                    for tt in range(TT):
                        pe.matmul(b[:, tt * S:(tt + 1) * S], aq_t[:, h // 2, tt * P:(tt + 1) * P], kz[:, h, :],
                                  start=True, stop=False)
                        op = pe.matmul(b[:, tt * S:(tt + 1) * S], ident, cst("lnc")[:, tt * S:(tt + 1) * S],
                                       start=False, stop=True)
                    op.then_inc(*me.up(s.as_full))

                def turn_p(h):
                    pe.wait_ge(*me.at(s.att_exp, h + 1))
                    if h >= 2:
                        pe.wait_ge(*me.at(s.pts_made, h - 1))
                    else:
                        pe.wait_ge(*me.at(s.num_read, 1))
                    for st in range(TT):
                        for tt in range(TT):
                            o = st * S + tt * P
                            op = pe.transpose(bank[6 + h % 2][:, o:o + P], pa[:, h % 2, tt, st * P:(st + 1) * P], ident)
                    op.then_inc(*me.up(s.p_turned))

                def attend(h):
                    pe.wait_ge(*me.at(s.pts_made, h + 1))
                    for tt in range(TT):
                        for st in range(TT):
                            o = (h % 4) * (AD + 1)
                            op = pe.matmul(bank[2 * (1 - h // 4) + tt][:, o:o + AD + 1], pts[:, h % 2, st, tt * P:(tt + 1) * P],
                                           av[:, st, h, :], start=st == 0, stop=st == TT - 1)
                    op.then_inc(*me.up(s.apv_done))

                logits(0)
                logits(1)
                for h in range(AH):
                    turn_p(h)
                    if h + 2 < AH:
                        logits(h + 2)
                    attend(h)
                product(x_hi, x_lo, KT, 2, 12, before=turn_rows(y, normalised))
                before = turn_rows(x, added(7))

                def after_up(c):
                    if c:
                        hidden_turn(c - 1)

                def hidden_turn(c, n=2):
                    chunk_read(hidden_chunk(c))
                    turn(rows_of(hid[c % 2]), n)

                hidden_chunk = lambda c: 9 + c
                product(x_hi, x_lo, KT, FF1 // NW, 16, after_up, before)
                product(h_hi, h_lo, FF1 // P, 2, 20, before={(0, 20): lambda: hidden_turn(FF1 // NW - 1)})

            me.enter(1, 0)
            for layer in range(DEPTH):
                g0, c0 = (0, 25)[layer], (0, 20)[layer]
                before = turn_rows(x, normalised)
                before[0, 6] = lambda: small_gates(g0)

                def after_w_in2(c):
                    if c == 1:
                        pe.wait_ge(*me.next(s.al_made))
                        for j in range(2):
                            op = pe.matmul(bank[7][:, j * S:(j + 1) * S], wa2[:, j * P:(j + 1) * P], al[:, :],
                                           start=True, stop=True)
                        op.then_inc(*me.up(s.decay_full))
                        chunk_read(c0)
                        turn(rows_of(qk2), 2)
                    if c == 3:
                        pe.wait_ge(*me.next(s.operands_made))
                        for tt in range(TT):
                            for j in range(2):
                                o = tt * S + j * P
                                op = pe.transpose(bank[6][:, o:o + P], kd[:, j, tt * P:(tt + 1) * P], ident)
                        op.then_inc(*me.up(s.kd_turned))
                        for tt in range(TT):
                            for h in range(GH):
                                rows = slice(tt * P, (tt + 1) * P)
                                op = pe.matmul(bank[4 + tt][:, h * P:(h + 1) * P], kiz[:, h, rows], qd[:, h // 2, rows],
                                               start=True, stop=True)
                        op.then_inc(*me.up(s.sc_full))
                    if c == 4:
                        pe.wait_ge(*me.next(s.kdt_made))
                        pe.wait_ge(*me.next(s.sc_made))
                        for n, b in enumerate((bank[6], bank[7], bank[4])):
                            tt, par = divmod(n, 2)
                            for j in range(2):
                                op = pe.matmul(b[:, j * 256:(j + 1) * 256], kdt[:, tt, j * P:(j + 1) * P],
                                               vz[:, par, tt, j * 256:(j + 1) * 256], start=True, stop=True)
                        op.then_inc(*me.up(s.updates_full))

                product(x_hi, x_lo, KT, 5, g0, after_w_in2, before)
                chunk_read(c0 + 4)
                pe.wait_ge(*me.next(s.vn_made))
                pe.wait_ge(*me.next(s.ws_causal))
                for tt in range(TT):
                    for h in range(GH):
                        op = pe.matmul(bank[tt][:, h * P:(h + 1) * P], ws_t[:, h, :], vn[:, tt, h * P:(h + 1) * P],
                                       start=True, stop=True)
                op.then_inc(*me.up(s.spatial_full))
                pe.wait_ge(*me.next(s.states_made))
                for tt in range(TT):
                    for h in range(GH):
                        rows = slice(tt * P, (tt + 1) * P)
                        parts = [(sc[:, tt, h, :], v2[:, tt, h * P:(h + 1) * P])]
                        for par in range(2):
                            n = 2 * tt + par
                            if n:
                                parts.append((qz[:, par, h // 2, rows], sz[:, n - 1, h, :]))
                        for i, (a, b) in enumerate(parts):
                            op = pe.matmul(bank[2 + tt][:, h * P:(h + 1) * P], a, b, start=i == 0, stop=i == len(parts) - 1)
                op.then_inc(*me.up(s.lin_full))
                product(x_hi, x_lo, KT, 2, g0 + 6, before=turn_rows(y, normalised))
                before = turn_rows(x, normalised)
                if layer == 0:
                    def after_pair(c):
                        j = c // 2
                        hidden_chunk = lambda i: 8 + 2 * i if i < 5 else 17
                        if c % 2 and j or c == 10:
                            chunk_read(hidden_chunk(j - 1))
                            turn(rows_of(hid[(j - 1) % 2]), 2)

                    product(x_hi, x_lo, KT, 11, 10, after_pair, before)
                    def last_hidden():
                        chunk_read(17)
                        turn(rows_of(hid[1]), 1)

                    product(h_hi, h_lo, FF2 // P, 2, 14, before={(0, 12): last_hidden})
                else:
                    before[0, 1]()
                    pe.wait_ge(s.rw_low.sem, 1)
                    small_product(rw_hi, rw_lo, NE, bank[6], 35).then_inc(*me.up(s.logits_full))
                    pe.wait_ge(*me.next(s.logits_copied))
                    for tt in range(TT):
                        op = pe.transpose(bank[7][:, tt * NE:(tt + 1) * NE], logits_t[:, tt * P:(tt + 1) * P],
                                          ident[0:NE, 0:NE])
                    op.then_inc(*me.up(s.logits_by_token))
                    pe.wait_ge(*me.next(s.mask_made))
                    pe.matmul(bank[7][:, 0:NE], upto[:, :], mask[:, 0, :], start=True, stop=True)
                    for o, stationary in ((NE, upto[:, :]), (2 * NE, ones[:, 0:P])):
                        pe.matmul(bank[7][:, o:o + NE], ones[:, 0:P], mask[:, 0, :], start=True, stop=False)
                        op = pe.matmul(bank[7][:, o:o + NE], stationary, mask[:, 1, :], start=False, stop=True)
                    op.then_inc(*me.up(s.counted))
                    gather()
                    pe.wait_ge(s.busiest_known.sem, 1)

            def experts(body):
                with pe.Fori(0, NE) as step:
                    me.enter(body, step)
                    slot = tbanks.slot(body, 0)
                    pe.wait_ge(t_read, tbanks.free(body, step, 0))
                    me.group = 1
                    for tt in range(TT):
                        op = pe.transpose(bank[4 + slot][:, tt * P:(tt + 1) * P], sel[:, tt, :], ident)
                    op.then_inc(t_full, 1)

                    def slabs(hi, lo, kts, half, before=None):
                        out = bank[2 * pairs.slot(body, me.chunk) + half][:, :]
                        pe.wait_ge(out_read[half], pairs.free(body, step, me.chunk))
                        for kt in range(kts):
                            if before is not None:
                                before(half, kt)
                            k, j = divmod(me.slab, SLABS)
                            high, low = splits.slot(body, k), units.slot(body, k)
                            if j == 0:
                                pe.wait_ge(lo_made, units.done(body, step, k))
                            rows = slice(kt % 4 * P, kt % 4 * P + P)
                            cols = slice(j * NW, (j + 1) * NW)
                            pe.matmul(out, hi[:, kt // 4, rows], w_hi[high][:, cols], start=kt == 0, stop=False)
                            pe.matmul(out, lo[:, kt // 4, rows], w_hi[high][:, cols], start=False, stop=False)
                            mm = pe.matmul(out, hi[:, kt // 4, rows], w_lo[low][:, cols], start=False, stop=kt == kts - 1)
                            if j == SLABS - 1:
                                mm.then_inc(w_used, 1)
                            me.slab += 1

                    def hidden_four(c):
                        pe.wait_ge(out_read[1], pairs.done(body, step, c))
                        turn_four(lambda j: hid[c % 2][:, 0, j * P:(j + 1) * P])

                    def before_input(half, kt):
                        if half == 0 and kt % 4 == 0:
                            pe.wait_ge(t_read, tbanks.done(body, step, kt // 4 - 2))

                    def before_down(half, kt):
                        if half == 0 and kt == 20:
                            hidden_four(FFE // NW - 1)
                        if half == 0 and kt % 4 == 0:
                            pe.wait_ge(t_read, tbanks.done(body, step, 1 + kt // 4))
                        if half == 1 and kt == 8:
                            scatter(0)
                        if half == 1 and kt == 16:
                            gather()

                    def scatter(half):
                        pe.wait_ge(out_read[half], pairs.done(body, step, FFE // NW))
                        for tt in range(TT):
                            pe.wait_ge(*me.at(s.acc_added, TT * (half - 1) + tt + 1))
                            pe.matmul(bank[6 + tt][:, :], sel_t[:, tt, :], y_e[:, half, :], start=True, stop=True)\
                                .then_inc(*me.up(s.scattered))

                    for c in range(FFE // NW):
                        slabs(xe_hi, xe_lo, KT, 0, before_input if c == 0 else None)
                        slabs(xe_hi, xe_lo, KT, 1)
                        me.chunk += 1
                        if c:
                            hidden_four(c - 1)
                    for half in range(2):
                        slabs(he_hi, he_lo, FFE // P, half, before_down)
                    me.chunk += 1
                    scatter(1)

            experts(2)
            with pe.If(pe.value_load(busiest[0:1, 0:1], min_val=0, max_val=S) > P):
                experts(3)

        for key, n in raised.items():
            assert key[0].raises[key[1]] == n or debug, (key, n)
        return raised, signals



def unit_stream(parts):
    slabs = []
    for w in parts:
        slabs.append(w.reshape(-1, P, NW))
    slabs = np.concatenate(slabs)
    return slabs.reshape(-1, SLABS, P, NW).transpose(0, 2, 1, 3).reshape(-1, P, UNIT)


def layout(inputs):
    a = {k: np.asarray(v) for k, v in inputs.items()}

    def chunks(w, starts):
        return [w[:, c:c + NW] for c in starts]

    def cols(v):
        return v.reshape(-1, P).T

    parts = []
    w = 512
    for l in range(DEPTH):
        w_in = a["w_in"][l]
        parts += chunks(w_in, (0, w, 2 * w, 4 * w + 16, 5 * w + 16, 6 * w + 16, 3 * w))
        parts += chunks(a["w_out"][l], range(0, D, NW)) + chunks(a["w_up"][l], range(0, FF1, NW))
        parts += chunks(a["w_down"][l], range(0, D, NW))
    for l in range(DEPTH):
        w_in = a["w_in_2"][l]
        parts += chunks(w_in, (1024, 1536, 512, 0, 2048)) + chunks(a["w_out_2"][l], range(0, D, NW))
        if l == 0:
            gate, up = a["ffn_w_gate_2"][0], a["ffn_w_up_2"][0]
            for c in range(0, 5 * NW, NW):
                parts += [gate[:, c:c + NW], up[:, c:c + NW]]
            parts += [np.concatenate([gate[:, 5 * NW:], up[:, 5 * NW:]], 1)]
            parts += chunks(a["ffn_w_down_2"][0], range(0, D, NW))
    for e in range(NE):
        for c in range(0, FFE, NW):
            parts += [a["exp_w_gate_2"][0, e][:, c:c + NW], a["exp_w_up_2"][0, e][:, c:c + NW]]
        parts += chunks(a["exp_w_down_2"][0, e], range(0, D, NW))
    parts += [a["exp_w_gate_2"][0, 0][:, 0:NW]]

    def small_w(m):
        n = m.shape[1]
        return m.reshape(KT, P, n).transpose(1, 0, 2).reshape(P, KT * n)

    def rows4(m, n):
        out = np.zeros((P, n), np.float32)
        out[:4] = m
        return out

    pc1 = np.stack([np.concatenate([
        cols(a["norm1_g"][l]), cols(a["norm2_g"][l]), cols(a["head_norm_g"][l]), np.ones((P, 4), np.float32),
        a["conv_w"][l].reshape(CW, 8, P).transpose(2, 1, 0).reshape(P, 8 * CW),
        rows4(np.concatenate([a["gate_i_b"][l].reshape(2, MH).T, a["gate_f_b"][l].reshape(2, MH).T], 1), 4),
    ], 1) for l in range(DEPTH)])
    pc2 = np.stack([np.concatenate([
        np.ones((P, 4), np.float32), cols(a["gla_norm_g_2"][l]), cols(a["gla_ba_2"][l]), a["gm_bs_2"][l].T,
    ], 1) for l in range(DEPTH)])
    tokens = a["x"].reshape(TT, P, D).transpose(1, 0, 2)
    return {
        "weights": unit_stream(parts),
        "x": tokens,
        "const": constants(),
        "pc1": pc1,
        "pc2": pc2,
        "gw": np.stack([small_w(a["w_in"][l][:, 2048:2064]) for l in range(DEPTH)]
                       + [small_w(a["w_in_2"][l][:, 2560:2576]) for l in range(DEPTH)]),
        "router": small_w(a["router_w_2"][0]),
        "ws_t": a["gm_ws_2"].transpose(0, 3, 1, 2),
        "wa2": a["gla_wa2_2"],
        "gm_ln_g": a["gm_ln_g_2"], "gm_ln_b": a["gm_ln_b_2"],
        "ln_mix_g": a["ln_mix_g_2"], "ln_mix_b": a["ln_mix_b_2"],
        "ln_ffn_g": a["ln_ffn_g_2"], "ln_ffn_b": a["ln_ffn_b_2"],
        "final_g": a["final_g"],
    }


def build(nc, arrays, debug=()):
    t = {n: nc.dram_tensor(f"in_{n}", a.shape, F32, kind="ExternalInput").ap() for n, a in arrays.items()}
    t["out"] = nc.dram_tensor("out_x", (P, TT, D), F32, kind="ExternalOutput").ap()
    return program(nc, t, debug)


def kernel(**inputs):
    import concourse.bacc as bacc
    from concourse.bass_utils import run_bass_kernel_spmd

    arrays = {n: np.ascontiguousarray(v) for n, v in layout(inputs).items()}
    nc = bacc.Bacc("TRN2", target_bir_lowering=False, num_devices=1)
    build(nc, arrays)
    r = run_bass_kernel_spmd(nc, [{f"in_{n}": v for n, v in arrays.items()}], core_ids=[0])
    return r.results[0]["out_x"].transpose(1, 0, 2).reshape(1, S, D)
```
